# Optimizing a Trainium2 kernel written in Bass

```python
import jax, jax.numpy as jnp
from jax import lax
import numpy as np

D_MODEL = 1024
BATCH = 1
SEQ = 512
DEPTH = 2

D_MIX = D_MODEL
CA = D_MIX // 2
A_GROUPS = 8
CONV_WIDTH = 31
CB = D_MIX // 2
GB = 4
DB = CB // GB
CHUNK = 128
N_HEADS = 16
HEAD_DIM = D_MIX // N_HEADS
Q_BLOCK = 128
D_FF = 2816
N_EVEN = (DEPTH + 1) // 2
N_ODD = DEPTH // 2
EPS = 1e-6

kernel_name = "hybrid_conv_gmlp_stickbreaking_macaron"

def rms_norm(x, g):
    xf = x.astype(jnp.float32)
    y = xf * lax.rsqrt(jnp.mean(xf * xf, axis=-1, keepdims=True) + EPS)
    return (y * g.astype(jnp.float32)).astype(x.dtype)

def layer_norm(x, g, b):
    xf = x.astype(jnp.float32)
    mu = jnp.mean(xf, axis=-1, keepdims=True)
    xc = xf - mu
    var = jnp.mean(xc * xc, axis=-1, keepdims=True)
    y = xc * lax.rsqrt(var + EPS)
    return (y * g.astype(jnp.float32) + b.astype(jnp.float32)).astype(x.dtype)

def swiglu(h, w_gate, w_up, w_down):
    return (jax.nn.silu(h @ w_gate) * (h @ w_up)) @ w_down

def causal_depthwise_conv(x, w, b):
    k, c = w.shape
    y = lax.conv_general_dilated(
        x, w[:, None, :], window_strides=(1,), padding=[(k - 1, 0)],
        dimension_numbers=("NWC", "WIO", "NWC"), feature_group_count=c)
    return y + b

def conv_gating_mixer(h, w_in, conv_w, conv_b, ln_a_g, ln_a_b, ln_v_g, ln_v_b,
                      sp_w, sp_b, w_out):
    bsz, s, _ = h.shape
    z = h @ w_in
    a_val, a_gate, u, v = jnp.split(z, [CA, 2 * CA, 2 * CA + CB], axis=-1)
    a = a_val * jax.nn.sigmoid(a_gate)
    a = causal_depthwise_conv(a, conv_w, conv_b)
    a = jax.nn.silu(layer_norm(a, ln_a_g, ln_a_b))
    v = layer_norm(v.reshape(bsz, s, GB, DB), ln_v_g, ln_v_b)
    v = v.reshape(bsz, s // CHUNK, CHUNK, GB, DB)
    causal = jnp.tril(jnp.ones((CHUNK, CHUNK), dtype=bool))
    w_s = jnp.where(causal[None], sp_w, 0)
    v = jnp.einsum("gts,bcsgd->bctgd", w_s, v) + sp_b.T[:, :, None]
    b_out = u * v.reshape(bsz, s, CB)
    return jnp.concatenate([a, b_out], axis=-1) @ w_out

def stick_breaking_attention(q, k, v):
    bsz, s, h, dh = q.shape
    nb = s // Q_BLOCK
    scale = dh ** -0.5

    def to_blocks(t):
        return t.reshape(bsz, nb, Q_BLOCK, h, dh).transpose(1, 0, 3, 2, 4)

    qb, kb, vb = to_blocks(q), to_blocks(k), to_blocks(v)
    pos = jnp.arange(Q_BLOCK)

    def per_query_block(args):
        qi, qblk = args
        qf = qblk.astype(jnp.float32)

        def step(carry, xs):
            kj, kblk, vblk = xs

            def accumulate(c):
                log_rem, acc = c
                z = jnp.einsum("bhtd,bhsd->bhts", qf, kblk.astype(jnp.float32)) * scale
                mask = (kj * Q_BLOCK + pos[None, :]) < (qi * Q_BLOCK + pos[:, None])
                log_keep = jnp.where(mask, -jax.nn.softplus(z), 0.0)
                suffix = lax.cumsum(log_keep, axis=3, reverse=True) - log_keep
                log_a = jax.nn.log_sigmoid(z) + suffix + log_rem[..., None]
                a = jnp.where(mask, jnp.exp(log_a), 0.0)
                acc = acc + jnp.einsum("bhts,bhsd->bhtd", a, vblk.astype(jnp.float32))
                return (log_rem + jnp.sum(log_keep, axis=-1), acc)

            return lax.cond(kj <= qi, accumulate, lambda c: c, carry), None

        init = (jnp.zeros((bsz, h, Q_BLOCK), jnp.float32),
                jnp.zeros((bsz, h, Q_BLOCK, dh), jnp.float32))
        (_, acc), _ = lax.scan(step, init, (jnp.arange(nb), kb, vb), reverse=True)
        return acc.astype(q.dtype)

    out = lax.map(per_query_block, (jnp.arange(nb), qb))
    return out.transpose(1, 0, 3, 2, 4).reshape(bsz, s, h * dh)

def stick_breaking_mixer(h, w_qkv, w_o):
    bsz, s, _ = h.shape
    q, k, v = jnp.split(h @ w_qkv, 3, axis=-1)
    q = q.reshape(bsz, s, N_HEADS, HEAD_DIM)
    k = k.reshape(bsz, s, N_HEADS, HEAD_DIM)
    v = v.reshape(bsz, s, N_HEADS, HEAD_DIM)
    return stick_breaking_attention(q, k, v) @ w_o

def setup_inputs(seed: int = 0) -> dict:
    key = jax.random.key(seed)
    ks = iter(jax.random.split(key, 32))
    f32 = jnp.float32

    def nrm(shape, fan_in):
        return jax.random.normal(next(ks), shape, f32) * (fan_in ** -0.5)

    def gain(shape):
        return 1.0 + 0.02 * jax.random.normal(next(ks), shape, f32)

    def bias(shape, s=0.02):
        return s * jax.random.normal(next(ks), shape, f32)

    return {
        "x": jax.random.normal(next(ks), (BATCH, SEQ, D_MODEL), f32),
        "g_ffn1": gain((DEPTH, D_MODEL)),
        "w_ffn1_gate": nrm((DEPTH, D_MODEL, D_FF), D_MODEL),
        "w_ffn1_up": nrm((DEPTH, D_MODEL, D_FF), D_MODEL),
        "w_ffn1_down": nrm((DEPTH, D_FF, D_MODEL), D_FF),
        "g_mix": gain((DEPTH, D_MODEL)),
        "w_in_ab": nrm((N_EVEN, D_MODEL, 2 * CA + 2 * CB), D_MODEL),
        "conv_w": nrm((N_EVEN, CONV_WIDTH, CA), CONV_WIDTH),
        "conv_b": bias((N_EVEN, CA)),
        "ln_a_g": gain((N_EVEN, CA)),
        "ln_a_b": bias((N_EVEN, CA)),
        "ln_v_g": gain((N_EVEN, GB, DB)),
        "ln_v_b": bias((N_EVEN, GB, DB)),
        "sp_w": nrm((N_EVEN, GB, CHUNK, CHUNK), CHUNK),
        "sp_b": 1.0 + bias((N_EVEN, GB, CHUNK), 0.1),
        "w_out_ab": nrm((N_EVEN, CA + CB, D_MODEL), CA + CB),
        "w_qkv": nrm((N_ODD, D_MODEL, 3 * D_MIX), D_MODEL),
        "w_o": nrm((N_ODD, D_MIX, D_MODEL), D_MIX),
        "g_ffn2": gain((DEPTH, D_MODEL)),
        "w_ffn2_gate": nrm((DEPTH, D_MODEL, D_FF), D_MODEL),
        "w_ffn2_up": nrm((DEPTH, D_MODEL, D_FF), D_MODEL),
        "w_ffn2_down": nrm((DEPTH, D_FF, D_MODEL), D_FF),
        "g_final": gain((D_MODEL,)),
    }

def reference(x, g_ffn1, w_ffn1_gate, w_ffn1_up, w_ffn1_down, g_mix, w_in_ab,
              conv_w, conv_b, ln_a_g, ln_a_b, ln_v_g, ln_v_b, sp_w, sp_b, w_out_ab,
              w_qkv, w_o, g_ffn2, w_ffn2_gate, w_ffn2_up, w_ffn2_down, g_final):
    for l in range(DEPTH):
        x = x + 0.5 * swiglu(rms_norm(x, g_ffn1[l]), w_ffn1_gate[l], w_ffn1_up[l], w_ffn1_down[l])
        h = rms_norm(x, g_mix[l])
        i = l // 2
        if l % 2 == 0:
            x = x + conv_gating_mixer(h, w_in_ab[i], conv_w[i], conv_b[i], ln_a_g[i], ln_a_b[i],
                                      ln_v_g[i], ln_v_b[i], sp_w[i], sp_b[i], w_out_ab[i])
        else:
            x = x + stick_breaking_mixer(h, w_qkv[i], w_o[i])
        x = x + 0.5 * swiglu(rms_norm(x, g_ffn2[l]), w_ffn2_gate[l], w_ffn2_up[l], w_ffn2_down[l])
    return rms_norm(x, g_final)


_drawn_inputs = setup_inputs


def setup_inputs(seed=0):
    import zlib

    import numpy as np

    out = dict(_drawn_inputs(seed))
    spreads = {}
    factors = {'g_ffn1': 4.817,
     'g_mix': 2.753,
     'conv_b': 3.974,
     'ln_a_g': 7.214,
     'ln_a_b': 7.502,
     'ln_v_g': 7.275,
     'ln_v_b': 7.749,
     'g_ffn2': 6.987,
     'g_final': 2.824}
    for name, (base, spread) in spreads.items():
        noise = np.random.default_rng([zlib.crc32(name.encode()), seed]).standard_normal(out[name].shape)
        drawn = base * np.exp(spread * noise) if base else spread * noise
        out[name] = __import__('jax').numpy.asarray(drawn.astype(out[name].dtype))
    for name, factor in factors.items():
        out[name] = (out[name] * factor).astype(out[name].dtype)
    return out
```

```python
from contextlib import ExitStack

import concourse.bass as bass
from concourse import mybir

F32 = mybir.dt.float32
F32R = mybir.dt.float32r
ALU = mybir.AluOpType
ACT = mybir.ActivationFunctionType
AX = mybir.AxisListType

P = 128
S = 512
D = 1024
DT = D // P
TT = S // P
FF = 2816
FT = FF // P
HK = FT // 2
CA = 512
CT = CA // P
TAPS = 31
PAD = TAPS - 1
GB = 4
HEADS = 16
DH = 64
EPS = 1e-6
SLOT = 16 * P

FFN_CHUNKS = FT + 2 * DT
CONV_CHUNKS = 12
ATT_CHUNKS = 16
C_FFN = [0, FFN_CHUNKS + CONV_CHUNKS, 2 * FFN_CHUNKS + CONV_CHUNKS,
         3 * FFN_CHUNKS + CONV_CHUNKS + ATT_CHUNKS]
C_CONV = FFN_CHUNKS
C_ATT = 3 * FFN_CHUNKS + CONV_CHUNKS
CHUNKS = 4 * FFN_CHUNKS + CONV_CHUNKS + ATT_CHUNKS
NORM_FFN = [0, 2, 3, 5]
NORM_CONV, NORM_ATT, NORM_FINAL = 1, 4, 6
ROW_LN_G, ROW_LN_B, ROW_CONV_B = 7 * DT, 7 * DT + CT, 7 * DT + 2 * CT
PARAM_ROWS = 7 * DT + 3 * CT
KEY_COLS = [S - P * b for b in range(TT)]
KEY_OFF = [0, 512, 1024, 896]
SCORES = 1280


def trunk_kernel(nc, x, g_ffn1, w_ffn1_gate, w_ffn1_up, w_ffn1_down, g_mix, w_in_ab, conv_w, conv_b,
                 ln_a_g, ln_a_b, ln_v_g, ln_v_b, sp_w, sp_b, w_out_ab, w_qkv, w_o, g_ffn2,
                 w_ffn2_gate, w_ffn2_up, w_ffn2_down, g_final, out):
    ctx = ExitStack()
    with ctx:
        def sb(name, shape, dt=F32, scope=ctx):
            return scope.enter_context(nc.sbuf_tensor(name, shape, dt))

        def sem(name):
            return ctx.enter_context(nc.semaphore(name))

        x_res = sb("x_res", [P, DT, S])
        xg_hi = sb("xg_hi", [P, DT, S], F32R)
        xg_lo = sb("xg_lo", [P, DT, S], F32R)
        stage = sb("stage", [P, 2, SLOT])
        w_hi = sb("w_hi", [P, 2, SLOT], F32R)
        w_lo = sb("w_lo", [P, 2, SLOT], F32R)
        sq = sb("sq", [P, S])
        ssq = sb("ssq", [P, S])
        rms = sb("rms", [P, S])
        rinv = sb("rinv", [P, S])
        tok_rms = sb("tok_rms", [P, TT])
        tok_rinv = sb("tok_rinv", [P, TT])
        ones = sb("ones", [P, P])
        neg_ones = sb("neg_ones", [P, P], F32R)
        neg_tri = sb("neg_tri", [P, P], F32R)
        ident = sb("ident", [P, P])
        params = sb("params", [P, PARAM_ROWS])
        eps_col = sb("eps_col", [P, 1])
        ps = ctx.enter_context(nc.psum_tensor("ps", [P, 8, 512], F32))

        with ExitStack() as begin:
            x_tok = sb("x_tok", [P, TT, D], scope=begin)
            param_rows = sb("param_rows", [PARAM_ROWS, P], scope=begin)
        with ExitStack() as ffn_scope:
            hid_hi = sb("hid_hi", [P, FT, S], F32R, ffn_scope)
            hid_lo = sb("hid_lo", [P, FT, S], F32R, ffn_scope)
            gate = sb("gate", [P, 2, S], scope=ffn_scope)
            up = sb("up", [P, 2, S], scope=ffn_scope)
        with ExitStack() as conv_scope:
            a_pad = sb("a_pad", [P, CT, PAD + S], scope=conv_scope)
            y = sb("y", [P, CT, S], scope=conv_scope)
            u = sb("u", [P, GB, S], scope=conv_scope)
            v_cen = sb("v_cen", [P, TT, GB, P], scope=conv_scope)
            v_n_hi = sb("v_n_hi", [P, TT, S], F32R, conv_scope)
            v_n_lo = sb("v_n_lo", [P, TT, S], F32R, conv_scope)
            v_mean = sb("v_mean", [P, TT, GB], scope=conv_scope)
            v_stat = sb("v_stat", [P, TT, GB], scope=conv_scope)
            v_rstd = sb("v_rstd", [P, TT, GB], scope=conv_scope)
            rinv2 = sb("rinv2", [P, TT], scope=conv_scope)
            ab_hi = sb("ab_hi", [P, 2 * CT, S], F32R, conv_scope)
            ab_lo = sb("ab_lo", [P, 2 * CT, S], F32R, conv_scope)
            g_buf = sb("g_buf", [P, 2, S], scope=conv_scope)
            sp_rows = sb("sp_rows", [P, GB, P], scope=conv_scope)
            sp_hi = sb("sp_hi", [P, GB, P], F32R, conv_scope)
            sp_lo = sb("sp_lo", [P, GB, P], F32R, conv_scope)
            sp_bias = sb("sp_bias", [P, GB, P], scope=conv_scope)
            lnv_g = sb("lnv_g", [P, S], scope=conv_scope)
            lnv_b = sb("lnv_b", [P, S], scope=conv_scope)
            conv_rows = sb("conv_rows", [TAPS * CT, P], scope=conv_scope)
            taps = sb("taps", [P, TAPS * CT], scope=conv_scope)
        with ExitStack() as att_scope:
            v_hi = sb("v_hi", [P, TT, D], F32R, att_scope)
            v_lo = sb("v_lo", [P, TT, D], F32R, att_scope)
            qk_f = sb("qk_f", [P, S], scope=att_scope)
            qk_hi = sb("qk_hi", [P, 2, 2, S], F32R, att_scope)
            qk_lo = sb("qk_lo", [P, 2, 2, S], F32R, att_scope)
            keep = sb("keep", [P, SCORES], scope=att_scope)
            keep_hi = sb("keep_hi", [P, SCORES], F32R, att_scope)
            keep_lo = sb("keep_lo", [P, SCORES], F32R, att_scope)
            prob = sb("prob", [P, SCORES], scope=att_scope)
            prob_hi = sb("prob_hi", [P, SCORES], F32R, att_scope)
            prob_lo = sb("prob_lo", [P, SCORES], F32R, att_scope)
            o_att = sb("o_att", [P, DT, S], scope=att_scope)
        with ExitStack() as end:
            out_tok = sb("out_tok", [P, TT, D], scope=end)

        x_loaded = [sem(f"x_loaded{t}") for t in range(TT)]
        params_loaded = sem("params_loaded")
        mixer_params = sem("mixer_params")
        consts_made = sem("consts_made")
        turned = sem("turned")
        turned_out = sem("turned_out")
        w_loaded = [sem("w_loaded0"), sem("w_loaded1")]
        w_hi_made = sem("w_hi_made")
        w_lo_made = sem("w_lo_made")
        w_used = sem("w_used")
        x_ready = sem("x_ready")
        xg_hi_made = sem("xg_hi_made")
        xg_lo_made = sem("xg_lo_made")
        x_added = sem("x_added")
        ssq_cleared = sem("ssq_cleared")
        sq_made = sem("sq_made")
        ssq_added = sem("ssq_added")
        ssq_summed = sem("ssq_summed")
        rms_made = sem("rms_made")
        rinv_made = sem("rinv_made")
        tok_summed = sem("tok_summed")
        tok_rms_made = sem("tok_rms_made")
        tok_rinv_made = sem("tok_rinv_made")
        gate_scaled = sem("gate_scaled")
        up_scaled = sem("up_scaled")
        silu_made = sem("silu_made")
        gated = sem("gated")
        hid_hi_made = sem("hid_hi_made")
        hid_lo_made = sem("hid_lo_made")
        pool_step = sem("pool_step")
        dve_step = sem("dve_step")
        act_step = sem("act_step")
        a_gate_scaled = sem("a_gate_scaled")
        a_val_scaled = sem("a_val_scaled")
        a_sigmoid = sem("a_sigmoid")
        v_centred = sem("v_centred")
        v_squared = sem("v_squared")
        v_stat_made = sem("v_stat_made")
        v_std_made = sem("v_std_made")
        v_rstd_made = sem("v_rstd_made")
        v_normed = sem("v_normed")
        v_n_hi_made = sem("v_n_hi_made")
        v_n_lo_made = sem("v_n_lo_made")
        sp_ready = sem("sp_ready")
        u_scaled = sem("u_scaled")
        mixed = sem("mixed")
        b_made = sem("b_made")
        b_hi_made = sem("b_hi_made")
        b_lo_made = sem("b_lo_made")
        conv_made = sem("conv_made")
        ysum_made = sem("ysum_made")
        y_mean_sum = sem("y_mean_sum")
        y_centred = sem("y_centred")
        y_squared = sem("y_squared")
        ysq_sum_made = sem("ysq_sum_made")
        y_var_sum = sem("y_var_sum")
        y_std_made = sem("y_std_made")
        y_normed = sem("y_normed")
        a_silu = sem("a_silu")
        a_hi_made = sem("a_hi_made")
        a_lo_made = sem("a_lo_made")
        v_half_summed = sem("v_half_summed")
        v_hi_made = sem("v_hi_made")
        v_lo_made = sem("v_lo_made")
        proj_summed = sem("proj_summed")
        proj_scaled = sem("proj_scaled")
        proj_hi_made = sem("proj_hi_made")
        proj_lo_made = sem("proj_lo_made")
        scores_summed = sem("scores_summed")
        log1p_made = sem("log1p_made")
        keep_made = sem("keep_made")
        keep_masked = sem("keep_masked")
        keep_hi_made = sem("keep_hi_made")
        keep_lo_made = sem("keep_lo_made")
        suffix_summed = sem("suffix_summed")
        prob_made = sem("prob_made")
        prob_masked = sem("prob_masked")
        prob_hi_made = sem("prob_hi_made")
        prob_lo_made = sem("prob_lo_made")
        att_summed = sem("att_summed")
        o_copied = sem("o_copied")
        o_hi_made = sem("o_hi_made")
        o_lo_made = sem("o_lo_made")
        y_fin_made = sem("y_fin_made")
        fin_turned = sem("fin_turned")
        fin_scaled = sem("fin_scaled")
        out_stored = sem("out_stored")

        ffn_weights = [(w_ffn1_gate[0], w_ffn1_up[0], w_ffn1_down[0]),
                       (w_ffn2_gate[0], w_ffn2_up[0], w_ffn2_down[0]),
                       (w_ffn1_gate[1], w_ffn1_up[1], w_ffn1_down[1]),
                       (w_ffn2_gate[1], w_ffn2_up[1], w_ffn2_down[1])]
        norm_rows = [g_ffn1[0:1], g_mix[0:1], g_ffn2[0:1], g_ffn1[1:2], g_mix[1:2], g_ffn2[1:2],
                     g_final.rearrange("(a d) -> a d", a=1)]
        x_dram = x.rearrange("b (t p) d -> p (b t) d", p=P)
        out_dram = out.rearrange("b (t p) d -> p (b t) d", p=P)

        def rows_of(w, k0, k1, cols):
            return w.rearrange("(k p) f -> p k f", p=P)[:, k0:k1, cols]

        def three(pe, to, a_hi, a_lo, b_hi, b_lo, start, stop=False):
            pe.matmul(to, a_hi, b_hi, start=start, stop=False, skip_group_check=True)
            pe.matmul(to, a_hi, b_lo, start=False, stop=False, skip_group_check=True)
            return pe.matmul(to, a_lo, b_hi, start=False, stop=stop, skip_group_check=True)

        block = ctx.enter_context(nc.Block())

        @block.sync
        def _(sp):
            def free_slot(c):
                sp.wait_ge(w_hi_made, c - 1)
                sp.wait_ge(w_lo_made, c - 1)

            def load(slot, first, second):
                for n, src in enumerate((first, second)):
                    k, cols = src.shape[1], src.shape[2]
                    at = n * first.shape[1] * cols
                    sp.dma_start(stage[:, slot, at:at + k * cols].rearrange("p (k f) -> p k f", k=k),
                                 src).then_inc(w_loaded[slot], 16)

            def load_ffn(n):
                w_gate, w_up, w_down = ffn_weights[n]
                c0 = C_FFN[n]

                def pair(f, slot):
                    load(slot, rows_of(w_gate, 0, DT, bass.ds(f * P, P)), rows_of(w_up, 0, DT, bass.ds(f * P, P)))

                for f in range(2):
                    if c0 + f >= 2:
                        free_slot(c0 + f)
                    pair(f, f)
                with sp.Fori(1, FT // 2) as i:
                    for s in range(2):
                        free_slot(2 * i + (c0 + s))
                        pair(2 * i + s, s)
                with sp.Fori(0, DT) as j:
                    for s in range(2):
                        free_slot(2 * j + (c0 + FT + s))
                        k = s * HK
                        load(s, rows_of(w_down, k, k + 6, bass.ds(j * P, P)),
                             rows_of(w_down, k + 6, k + HK, bass.ds(j * P, P)))

            def load_cols(c, w, k0, k1, col0, cols):
                free_slot(c)
                mid = (k0 + k1) // 2
                load(c % 2, rows_of(w, k0, mid, slice(col0, col0 + cols)),
                     rows_of(w, mid, k1, slice(col0, col0 + cols)))

            def load_pair(c, w, col_a, col_b):
                free_slot(c)
                load(c % 2, rows_of(w, 0, DT, slice(col_a, col_a + P)), rows_of(w, 0, DT, slice(col_b, col_b + P)))

            for t in range(TT):
                sp.dma_start(x_tok[:, t, :], x_dram[:, t, :]).then_inc(x_loaded[t], 16)
            load_ffn(0)

            sp.wait_ge(w_used, C_CONV)
            sp.dma_start(conv_rows[:, :], conv_w[0].rearrange("k (c p) -> (k c) p", p=P)).then_inc(mixer_params, 16)
            sp.dma_start(sp_rows[:, :, :], sp_w[0].rearrange("g t s -> t g s")).then_inc(mixer_params, 16)
            sp.dma_start(sp_bias[:, :, :], sp_b[0].partition_broadcast(P)).then_inc(mixer_params, 16)
            sp.dma_start(lnv_g[:, :], ln_v_g[0].rearrange("g d -> (g d)").partition_broadcast(P)).then_inc(mixer_params, 16)
            sp.dma_start(lnv_b[:, :], ln_v_b[0].rearrange("g d -> (g d)").partition_broadcast(P)).then_inc(mixer_params, 16)
            w_in, w_out = w_in_ab[0], w_out_ab[0]
            for i in range(CT):
                load_pair(C_CONV + i, w_in, i * P, CA + i * P)
            for kh in range(2):
                load_cols(C_CONV + 4 + kh, w_in, 4 * kh, 4 * kh + 4, 3 * CA, CA)
            for i in range(2):
                load_pair(C_CONV + 6 + i, w_in, 2 * CA + 2 * i * P, 2 * CA + (2 * i + 1) * P)
            for n in range(4):
                k0 = CT if n < 2 else 0
                load_cols(C_CONV + 8 + n, w_out, k0, k0 + 4, (n % 2) * S, S)
            load_ffn(1)
            load_ffn(2)
            for n in range(4):
                load_cols(C_ATT + n, w_qkv[0], 4 * (n % 2), 4 * (n % 2) + 4, 2 * D + (n // 2) * 512, 512)
            for j in range(DT):
                load_pair(C_ATT + 4 + j, w_qkv[0], j * P, D + j * P)
            for n in range(4):
                load_cols(C_ATT + 12 + n, w_o[0], 0, DT, n * 256, 256)
            load_ffn(3)

            for t in range(TT):
                sp.wait_ge(fin_scaled, 2 * (t + 1))
                sp.dma_start(out_dram[:, t, :], out_tok[:, t, :]).then_inc(out_stored, 16)
            sp.wait_ge(out_stored, 16 * TT)

        @block.tensor
        def _(pe):
            def sum_squares():
                return pe.matmul(ps[:, 6, :], ones[:, :], ssq[:, :], start=True, stop=True)

            def sum_squares_tok():
                for t in range(TT):
                    mm = pe.matmul(ps[:, 7, t:t + 1], ssq[:, t * P:(t + 1) * P], ones[:, 0:1], start=True, stop=True)
                return mm

            def tile(slot, n):
                return w_hi[:, slot, n * P:(n + 1) * P], w_lo[:, slot, n * P:(n + 1) * P]

            def pair_chunk(slot, banks, norm=None, tok=False, wait_x=None):
                for k in range(DT):
                    if wait_x is not None:
                        pe.wait_ge(xg_lo_made, wait_x * DT + k + 1)
                    for n in range(2):
                        mm = three(pe, ps[:, banks[n], :], *tile(slot, n * DT + k),
                                   xg_hi[:, k, :], xg_lo[:, k, :], start=(k == 0), stop=(k == DT - 1))
                    if norm is not None and k == 5:
                        pe.wait_ge(ssq_added, (norm + 1) * DT)
                        sum_squares().then_inc(ssq_summed, 1)
                        if tok:
                            sum_squares_tok().then_inc(tok_summed, 1)
                mm.then_inc(w_used, 1)

            def ffn(n):
                c0, f0, norm = C_FFN[n], n * FT, NORM_FFN[n]
                for s in range(2):
                    pe.wait_ge(w_lo_made, c0 + s + 1)
                    pair_chunk(s, (2 * s, 2 * s + 1), norm if s == 0 else None, False, norm if s == 0 else None)
                with pe.Fori(1, FT // 2) as i:
                    for s in range(2):
                        pe.wait_ge(w_lo_made, 2 * i + (c0 + s + 1))
                        pe.wait_ge(up_scaled, 2 * i + (f0 + s - 1))
                        pair_chunk(s, (2 * s, 2 * s + 1))
                with pe.Fori(0, DT // 2) as i:
                    for q in range(2):
                        pe.wait_ge(x_ready, 2 * i + ((norm + 1) * DT + q - 1))
                        for s in range(2):
                            pe.wait_ge(w_lo_made, 4 * i + (c0 + FT + 2 * q + s + 1))
                            for k in range(HK):
                                if s == 1 and k == HK - 1:
                                    pe.wait_ge(hid_lo_made, f0 + FT)
                                elif s == 0 and k == 0:
                                    pe.wait_ge(hid_lo_made, f0 + FT - 1)
                                h = s * HK + k
                                mm = three(pe, ps[:, 4 + q, :], *tile(s, k), hid_hi[:, h, :], hid_lo[:, h, :],
                                           start=(h == 0), stop=(h == FT - 1))
                            mm.then_inc(w_used, 1)

            def v_chunk(slot, k0, bank0, stop, wait_x=None):
                for k in range(4):
                    if wait_x is not None:
                        pe.wait_ge(xg_lo_made, wait_x * DT + k0 + k + 1)
                    w_h, w_l = w_hi[:, slot, k * 512:(k + 1) * 512], w_lo[:, slot, k * 512:(k + 1) * 512]
                    for t in range(TT):
                        mm = three(pe, ps[:, bank0 + t, :], xg_hi[:, k0 + k, t * P:(t + 1) * P],
                                   xg_lo[:, k0 + k, t * P:(t + 1) * P], w_h, w_l,
                                   start=(k0 + k == 0), stop=(k0 + k == DT - 1))
                return mm

            pe.wait_ge(consts_made, 1)
            for j in range(DT):
                for t in range(TT):
                    if j == 0:
                        pe.wait_ge(x_loaded[t], 16)
                    mm = pe.transpose(ps[:, j, t * P:(t + 1) * P], x_tok[:, t, j * P:(j + 1) * P], ident[:, :])
                mm.then_inc(turned, 1)
            pe.wait_ge(params_loaded, 16 * 10)
            pe.wait_ge(x_ready, 1)
            pe.transpose(ps[:, 0, 0:PARAM_ROWS], param_rows[:, :], ident[0:PARAM_ROWS, 0:PARAM_ROWS]).then_inc(turned, 1)
            pe.wait_ge(turned_out, 1)
            ffn(0)

            c0 = C_CONV
            for i in range(CT):
                pe.wait_ge(w_lo_made, c0 + i + 1)
                if i >= 2:
                    pe.wait_ge(a_val_scaled, i - 1)
                s = i % 2
                first = i == 0
                pair_chunk(s, (2 * s, 2 * s + 1), NORM_CONV if first else None, first, NORM_CONV if first else None)
            pe.wait_ge(rms_made, NORM_CONV + 1)
            pe.wait_ge(tok_rms_made, 1)
            for kh in range(2):
                pe.wait_ge(w_lo_made, c0 + 5 + kh)
                v_chunk(kh, 4 * kh, 4, kh == 1).then_inc(w_used, 1)
            pe.wait_ge(a_val_scaled, CT)
            for i in range(2):
                pe.wait_ge(w_lo_made, c0 + 7 + i)
                pair_chunk(i, (2 * i, 2 * i + 1))
            pe.wait_ge(mixer_params, 16 * 5)
            pe.wait_ge(v_centred, TT)
            pe.transpose(ps[:, 4, 0:TAPS * CT], conv_rows[:, :], ident[0:TAPS * CT, 0:TAPS * CT]).then_inc(turned, 1)
            for g in range(GB):
                mm = pe.transpose(ps[:, 5, g * P:(g + 1) * P], sp_rows[:, g, :], ident[:, :])
            mm.then_inc(turned, 1)
            pe.wait_ge(sp_ready, 1)
            pe.wait_ge(turned_out, 3)
            for g in range(GB):
                for t in range(TT):
                    pe.wait_ge(v_n_lo_made, t + 1)
                    mm = three(pe, ps[:, 4 + g, t * P:(t + 1) * P], v_n_hi[:, t, g * P:(g + 1) * P],
                               v_n_lo[:, t, g * P:(g + 1) * P], sp_hi[:, g, :], sp_lo[:, g, :], start=True, stop=True)
                mm.then_inc(mixed, 1)
            for n in range(4):
                pe.wait_ge(w_lo_made, c0 + 9 + n)
                for m in range(4):
                    j = 4 * n + m
                    if j < 4:
                        pe.wait_ge(u_scaled, j + 1)
                    else:
                        pe.wait_ge(x_added, min(j - 3, DT))
                        if j >= DT + 4:
                            pe.wait_ge(x_ready, NORM_FFN[1] * DT + j - 3 - DT)
                    for k in range(4):
                        src = k + (CT if n < 2 else 0)
                        if n < 2:
                            pe.wait_ge(b_lo_made, k + 1)
                        else:
                            pe.wait_ge(a_lo_made, k + 1)
                        mm = three(pe, ps[:, j % 4 + (4 if n >= 2 else 0), :], *tile(n % 2, 4 * k + m), ab_hi[:, src, :], ab_lo[:, src, :],
                                   start=(k == 0), stop=(k == 3))
                mm.then_inc(w_used, 1)
                if n == 0:
                    pe.wait_ge(ysum_made, 1)
                    pe.matmul(ps[:, 4, :], ones[:, :], sq[:, :], start=True, stop=True).then_inc(y_mean_sum, 1)
                if n == 1:
                    pe.wait_ge(ysq_sum_made, 1)
                    pe.matmul(ps[:, 5, :], ones[:, :], sq[:, :], start=True, stop=True).then_inc(y_var_sum, 1)
            ffn(1)
            ffn(2)

            c0 = C_ATT
            for n in range(4):
                half, kh = n // 2, n % 2
                pe.wait_ge(w_lo_made, c0 + n + 1)
                if n == 2:
                    pe.wait_ge(rms_made, NORM_ATT + 1)
                    pe.wait_ge(tok_rms_made, 2)
                mm = v_chunk(n % 2, 4 * kh, 4 * half, kh == 1, NORM_ATT if half == 0 else None)
                mm.then_inc(w_used, 1)
                if n == 0:
                    pe.wait_ge(ssq_added, (NORM_ATT + 1) * DT)
                    sum_squares().then_inc(ssq_summed, 1)
                    sum_squares_tok().then_inc(tok_summed, 1)

            def project(n):
                slot = (n // 2) % 2
                pe.wait_ge(w_lo_made, c0 + 5 + n // 2)
                if n == 0:
                    pe.wait_ge(v_lo_made, 2 * TT)
                else:
                    pe.wait_ge(proj_scaled, n)
                for k in range(DT):
                    mm = three(pe, ps[:, 6, :], *tile(slot, (n % 2) * DT + k), xg_hi[:, k, :], xg_lo[:, k, :],
                               start=(k == 0), stop=(k == DT - 1))
                mm.then_inc(w_used if n % 2 else proj_summed, 1)

            def zcols(h, b, skip=0):
                at = 3 * (h % 2) * 512 + KEY_OFF[b] + skip * P
                return ps[:, :, :].rearrange("p a c -> p (a c)")[:, at:at + KEY_COLS[b] - skip * P]

            def scores(h):
                j, r0 = h // 2, DH * (h % 2)
                pe.wait_ge(proj_lo_made, 2 * j + 2)
                if h >= 2:
                    pe.wait_ge(prob_made, h - 1)
                for b in range(TT):
                    r = slice(r0, r0 + DH)
                    mm = three(pe, zcols(h, b), qk_hi[r, j % 2, 1, b * P:(b + 1) * P],
                               qk_lo[r, j % 2, 1, b * P:(b + 1) * P], qk_hi[r, j % 2, 0, b * P:S],
                               qk_lo[r, j % 2, 0, b * P:S], start=(b < 3))
                mm.then_inc(scores_summed, 1)

            def suffix(h):
                pe.wait_ge(keep_lo_made, h + 1)
                for b in range(TT):
                    for part in (keep_hi, keep_lo):
                        off = KEY_OFF[b]
                        mm = pe.matmul(zcols(h, b), neg_tri[:, :], part[:, off:off + KEY_COLS[b]],
                                       start=False, stop=False, skip_group_check=True)
                        for later in range(b + 1, TT):
                            off = KEY_OFF[later]
                            mm = pe.matmul(zcols(h, b, later - b), neg_ones[:, :],
                                           part[:, off:off + KEY_COLS[later]],
                                           start=False, stop=False, skip_group_check=True)
                mm.then_inc(suffix_summed, 1)

            def attend(h):
                j = h // 2
                pe.wait_ge(prob_lo_made, h + 1)
                if h >= 1:
                    pe.wait_ge(o_copied, h)
                for b in range(TT):
                    off = KEY_OFF[b]
                    cols = slice(off, off + KEY_COLS[b])
                    mm = three(pe, ps[:, 7, b * P:S], v_hi[:, b, j * P:(j + 1) * P], v_lo[:, b, j * P:(j + 1) * P],
                               prob_hi[:, cols], prob_lo[:, cols], start=(b == 0), stop=(b == TT - 1))
                mm.then_inc(att_summed, 1)

            for n in range(3):
                project(n)
            for h in range(HEADS + 2):
                if h < HEADS:
                    scores(h)
                if 1 <= h <= HEADS:
                    suffix(h - 1)
                if h >= 2:
                    attend(h - 2)
                if h + 3 < HEADS:
                    project(h + 3)
            for n in range(4):
                pe.wait_ge(w_lo_made, c0 + 13 + n)
                for m in range(2):
                    j = 2 * n + m
                    if j >= 4:
                        pe.wait_ge(x_ready, NORM_FFN[3] * DT + j - 3)
                    for k in range(DT):
                        pe.wait_ge(o_lo_made, k + 1)
                        w_h = w_hi[:, n % 2, k * 256 + m * P:k * 256 + (m + 1) * P]
                        w_l = w_lo[:, n % 2, k * 256 + m * P:k * 256 + (m + 1) * P]
                        mm = three(pe, ps[:, 4 + j % 4, :].rearrange("p (t c) -> p t c", t=TT), w_h, w_l,
                                   v_hi[:, :, k * P:(k + 1) * P], v_lo[:, :, k * P:(k + 1) * P],
                                   start=(k == 0), stop=(k == DT - 1))
                mm.then_inc(w_used, 1)
            ffn(3)

            pe.wait_ge(ssq_added, (NORM_FINAL + 1) * DT)
            sum_squares_tok().then_inc(tok_summed, 1)
            order = [0, 1, 2, 3, 4, 5, 6, 0]
            for t in range(TT):
                for half in range(2):
                    n = 2 * t + half
                    for m in range(4):
                        pe.wait_ge(y_fin_made, 4 * half + m + 1)
                        if n == 7 and m == 0:
                            pe.wait_ge(fin_scaled, 1)
                        mm = pe.transpose(ps[:, order[n], m * P:(m + 1) * P],
                                          x_res[:, 4 * half + m, t * P:(t + 1) * P], ident[:, :])
                    mm.then_inc(fin_turned, 1)

        @block.scalar
        def _(act):
            steps = [0]

            def step(ins):
                steps[0] += 1
                ins.then_inc(act_step, 1)
                act.wait_ge(act_step, steps[0])

            def split_hi(c, slot, loads, cols=SLOT):
                act.wait_ge(w_loaded[slot], loads)
                act.wait_ge(w_used, c - 1)
                act.activation(w_hi[:, slot, 0:cols], stage[:, slot, 0:cols], ACT.Copy).then_inc(w_hi_made, 1)

            def split_static(c, cols=SLOT):
                if c < CHUNKS:
                    act.wait_ge(w_loaded[c % 2], 32 * (c // 2 + 1))
                    if c >= 2:
                        act.wait_ge(w_used, c - 1)
                    act.activation(w_hi[:, c % 2, 0:cols], stage[:, c % 2, 0:cols], ACT.Copy).then_inc(w_hi_made, 1)

            def x_tile(n, j, ready):
                act.wait_ge(x_ready, ready)
                act.activation(xg_hi[:, bass.ds(j, 1), :].rearrange("p a s -> p (a s)"),
                               x_res[:, bass.ds(j, 1), :].rearrange("p a s -> p (a s)"), ACT.Copy,
                               scale=params[:, bass.ds(j + n * DT, 1)]).then_inc(xg_hi_made, 1)

            def token_rms(n):
                act.wait_ge(ssq_summed, n + 1)
                act.activation(rms[:, :], ps[:, 6, :], ACT.Sqrt, bias=eps_col[:, 0:1], scale=1.0 / D).then_inc(rms_made, 1)

            def token_rms_tok(n):
                act.wait_ge(tok_summed, n)
                act.activation(tok_rms[:, :], ps[:, 7, 0:TT], ACT.Sqrt, bias=eps_col[:, 0:1],
                               scale=1.0 / D).then_inc(tok_rms_made, 1)

            def hidden(f, count, s):
                act.wait_ge(gate_scaled, count)
                act.activation(gate[:, s, :], gate[:, s, :], ACT.Silu).then_inc(silu_made, 1)
                act.wait_ge(gated, count)
                act.activation(hid_hi[:, bass.ds(f, 1), :].rearrange("p a s -> p (a s)"), up[:, s, :],
                               ACT.Copy).then_inc(hid_hi_made, 1)

            def ffn(n):
                c0, f0, norm = C_FFN[n], n * FT, NORM_FFN[n]
                half0 = c0 // 2
                split_static(c0 + 1)
                token_rms(norm)
                hidden(0, f0 + 1, 0)
                split_static(c0 + 2)
                hidden(1, f0 + 2, 1)
                with act.Fori(1, FT // 2 - 1) as i:
                    for s in range(2):
                        o = 1 - s
                        split_hi(2 * i + (c0 + s + 1), o, 32 * i + 32 * (half0 + s + 1))
                        hidden(2 * i + s, 2 * i + (f0 + s + 1), s)
                split_static(c0 + FT - 1)
                hidden(FT - 2, f0 + FT - 1, 0)
                split_static(c0 + FT, HK * P)
                hidden(FT - 1, f0 + FT, 1)
                last = n == 3
                with act.Fori(0, DT - 1) as j:
                    split_hi(2 * j + (c0 + FT + 1), 1, 32 * j + 32 * (half0 + HK + 1), HK * P)
                    split_hi(2 * j + (c0 + FT + 2), 0, 32 * j + 32 * (half0 + HK + 2), HK * P)
                    if last:
                        final_tile(j, j + (NORM_FINAL * DT + 1))
                    else:
                        x_tile(norm + 1, j, j + ((norm + 1) * DT + 1))
                split_static(c0 + FT + 2 * DT - 1, HK * P)
                split_static(c0 + FT + 2 * DT)
                if last:
                    final_tile(DT - 1, (NORM_FINAL + 1) * DT)
                else:
                    x_tile(norm + 1, DT - 1, (norm + 2) * DT)

            def final_tile(j, ready):
                act.wait_ge(ssq_added, ready)
                act.activation(x_res[:, bass.ds(j, 1), :].rearrange("p a s -> p (a s)"),
                               x_res[:, bass.ds(j, 1), :].rearrange("p a s -> p (a s)"), ACT.Copy,
                               scale=params[:, bass.ds(j + NORM_FINAL * DT, 1)]).then_inc(y_fin_made, 1)

            for n in range(7):
                act.dma_start(param_rows[n * DT:(n + 1) * DT, :],
                              norm_rows[n].rearrange("a (j p) -> (a j) p", p=P)).then_inc(params_loaded, 16)
            for row, vec in ((ROW_LN_G, ln_a_g), (ROW_LN_B, ln_a_b), (ROW_CONV_B, conv_b)):
                act.dma_start(param_rows[row:row + CT, :], vec.rearrange("a (j p) -> (a j) p", p=P)).then_inc(params_loaded, 16)
            act.wait_ge(consts_made, 2)
            act.wait_ge(turned_out, 1)
            for j in range(DT):
                x_tile(0, j, j + 1)
            split_static(0)
            ffn(0)

            c0 = C_CONV
            for i in range(CT):
                split_static(c0 + i + 1)
                if i == 0:
                    token_rms(NORM_CONV)
                    token_rms_tok(1)
                act.wait_ge(a_gate_scaled, i + 1)
                act.activation(g_buf[:, 0, :], g_buf[:, 0, :], ACT.Sigmoid).then_inc(a_sigmoid, 1)
            split_static(c0 + 5)
            split_static(c0 + 6)
            for t in range(TT):
                act.wait_ge(v_centred, t + 1)
                act.activation(u[:, t, :], v_cen[:, t].rearrange("p g c -> p (g c)"), ACT.Square).then_inc(v_squared, 1)
            act.wait_ge(v_stat_made, 1)
            act.activation(v_stat[:, :, :], v_stat[:, :, :], ACT.Sqrt, bias=eps_col[:, 0:1], scale=1.0 / P).then_inc(v_std_made, 1)
            split_static(c0 + 7)
            for t in range(TT):
                act.wait_ge(v_normed, t + 1)
                act.activation(v_n_hi[:, t, :], v_cen[:, t].rearrange("p g c -> p (g c)"), ACT.Copy).then_inc(v_n_hi_made, 1)
            split_static(c0 + 8)
            for g in range(GB):
                act.wait_ge(b_made, g + 1)
                act.activation(ab_hi[:, CT + g, :], u[:, g, :], ACT.Copy).then_inc(b_hi_made, 1)
            split_static(c0 + 9)
            for i in range(CT):
                act.wait_ge(y_centred, i + 1)
                act.activation(v_cen[:, i].rearrange("p g c -> p (g c)"), y[:, i, :], ACT.Square).then_inc(y_squared, 1)
            split_static(c0 + 10)
            act.wait_ge(y_var_sum, 1)
            act.activation(rms[:, :], ps[:, 5, :], ACT.Sqrt, bias=eps_col[:, 0:1], scale=1.0 / CA).then_inc(y_std_made, 1)
            for i in range(CT):
                act.wait_ge(y_normed, i + 1)
                act.activation(y[:, i, :], y[:, i, :], ACT.Silu, scale=params[:, ROW_LN_G + i:ROW_LN_G + i + 1],
                               bias=params[:, ROW_LN_B + i:ROW_LN_B + i + 1]).then_inc(a_silu, 1)
                act.wait_ge(a_silu, i + 1)
                act.activation(ab_hi[:, i, :], y[:, i, :], ACT.Copy).then_inc(a_hi_made, 1)
            split_static(c0 + 11)
            for j in range(4):
                x_tile(2, j, 2 * DT + j + 1)
            split_static(c0 + 12)
            for j in range(4, DT):
                x_tile(2, j, 2 * DT + j + 1)
            ffn(1)
            ffn(2)

            c0 = C_ATT
            for n in range(4):
                split_static(c0 + n + 1)
                if n == 0:
                    token_rms(NORM_ATT)
                    token_rms_tok(2)
                if n % 2:
                    half = n // 2
                    act.wait_ge(tok_rinv_made, 2)
                    act.wait_ge(w_used, c0 + n + 1)
                    for t in range(TT):
                        act.activation(v_hi[:, t, half * 512:(half + 1) * 512], ps[:, 4 * half + t, :], ACT.Copy,
                                       scale=tok_rinv[:, t:t + 1]).then_inc(v_hi_made, 1)

            def split_proj(n):
                act.wait_ge(proj_scaled, n + 1)
                act.activation(qk_hi[:, (n // 2) % 2, n % 2, :], qk_f[:, :], ACT.Copy).then_inc(proj_hi_made, 1)

            def zall(h):
                at = 3 * (h % 2) * 512
                return ps[:, :, :].rearrange("p a c -> p (a c)")[:, at:at + SCORES]

            def split_out(j):
                act.wait_ge(o_copied, 2 * j + 2)
                act.activation(v_hi[:, :, j * P:(j + 1) * P], o_att[:, j, :].rearrange("p (t c) -> p t c", t=TT),
                               ACT.Copy).then_inc(o_hi_made, 1)

            split_proj(0)
            split_proj(1)
            split_static(c0 + 5)
            for h in range(HEADS + 2):
                if h + 2 < HEADS:
                    split_proj(h + 2)
                if h < HEADS:
                    act.wait_ge(scores_summed, h + 1)
                    if h >= 1:
                        act.wait_ge(keep_lo_made, h)
                    step(act.activation(keep[:, :], zall(h), ACT.Abs))
                    step(act.activation(keep[:, :], keep[:, :], ACT.Exp, scale=-1.0))
                    act.activation(keep[:, :], keep[:, :], ACT.Ln, bias=1.0).then_inc(log1p_made, 1)
                if 1 <= h <= HEADS:
                    act.wait_ge(suffix_summed, h)
                    if h >= 2:
                        act.wait_ge(prob_lo_made, h - 1)
                    act.activation(prob[:, :], zall(h - 1), ACT.Exp).then_inc(prob_made, 1)
                if h >= 2:
                    act.wait_ge(att_summed, h - 1)
                    r = slice(DH * (h % 2), DH * (h % 2) + DH)
                    act.activation(o_att[r, (h - 2) // 2, :], ps[r, 7, :], ACT.Copy).then_inc(o_copied, 1)
                if h % 2 == 0 and h <= 12:
                    split_static(c0 + 6 + h // 2)
                if h >= 3 and h % 2:
                    split_out((h - 3) // 2)
            for n in range(4):
                split_static(c0 + 13 + n)
                for j in range(2 * n, 2 * n + 2):
                    x_tile(5, j, 5 * DT + j + 1)
            ffn(3)
            token_rms_tok(3)
            for n in range(1, 8, 2):
                act.wait_ge(tok_rinv_made, 3)
                act.wait_ge(fin_turned, n + 1)
                t, half = n // 2, n % 2
                act.wait_ge(fin_scaled, n)
                act.activation(out_tok[:, t, half * 512:(half + 1) * 512], ps[:, [0, 1, 2, 3, 4, 5, 6, 0][n], :], ACT.Copy,
                               scale=tok_rinv[:, t:t + 1]).then_inc(fin_scaled, 1)

        @block.vector
        def _(dve):
            steps = [0]

            def step(ins):
                steps[0] += 1
                ins.then_inc(dve_step, 1)
                dve.wait_ge(dve_step, steps[0])
                return ins

            def split_lo(c, slot, cols=SLOT):
                dve.wait_ge(w_hi_made, c + 1)
                dve.tensor_tensor(w_lo[:, slot, 0:cols], stage[:, slot, 0:cols],
                                  w_hi[:, slot, 0:cols].bitcast(F32), ALU.subtract).then_inc(w_lo_made, 1)

            def split_static(c, cols=SLOT):
                if c < CHUNKS:
                    split_lo(c, c % 2, cols)

            def x_low(n, j, made):
                dve.wait_ge(xg_hi_made, made)
                dve.scalar_tensor_tensor(xg_lo[:, bass.ds(j, 1), :].rearrange("p a s -> p (a s)"),
                                         x_res[:, bass.ds(j, 1), :].rearrange("p a s -> p (a s)"),
                                         params[:, bass.ds(j + n * DT, 1)],
                                         xg_hi[:, bass.ds(j, 1), :].rearrange("p a s -> p (a s)").bitcast(F32),
                                         ALU.mult, ALU.subtract).then_inc(xg_lo_made, 1)

            def add_to_x(j, bank, factor, done):
                xj = x_res[:, bass.ds(j, 1), :].rearrange("p a s -> p (a s)")
                dve.scalar_tensor_tensor(xj, ps[:, bank, :], factor, xj, ALU.mult, ALU.add).then_inc(done, 1)

            def invert_rms(n):
                dve.wait_ge(rms_made, n + 1)
                dve.reciprocal(rinv[:, :], rms[:, :]).then_inc(rinv_made, 1)
                dve.wait_ge(rinv_made, n + 1)

            def invert_rms_tok(n):
                dve.wait_ge(tok_rms_made, n)
                dve.reciprocal(tok_rinv[:, :], tok_rms[:, :]).then_inc(tok_rinv_made, 1)
                dve.wait_ge(tok_rinv_made, n)

            def hidden(c_used, count, prev, s):
                dve.wait_ge(w_used, c_used)
                if prev is not None:
                    dve.wait_ge(hid_lo_made, prev)
                dve.tensor_tensor(gate[:, s, :], ps[:, 2 * s, :], rinv[:, :], ALU.mult).then_inc(gate_scaled, 1)
                dve.tensor_tensor(up[:, s, :], ps[:, 2 * s + 1, :], rinv[:, :], ALU.mult).then_inc(up_scaled, 1)
                dve.wait_ge(silu_made, count)
                dve.wait_ge(up_scaled, count)
                dve.tensor_tensor(up[:, s, :], gate[:, s, :], up[:, s, :], ALU.mult).then_inc(gated, 1)

            def ffn(n):
                c0, f0, norm = C_FFN[n], n * FT, NORM_FFN[n]
                split_static(c0 + 1)
                invert_rms(norm)
                hidden(c0 + 1, f0 + 1, None, 0)
                split_static(c0 + 2)
                hidden(c0 + 2, f0 + 2, None, 1)
                with dve.Fori(1, FT // 2 - 1) as i:
                    for s in range(2):
                        split_lo(2 * i + (c0 + s + 1), 1 - s)
                        hidden(2 * i + (c0 + s + 1), 2 * i + (f0 + s + 1), 2 * i + (f0 + s - 1), s)
                split_static(c0 + FT - 1)
                hidden(c0 + FT - 1, f0 + FT - 1, f0 + FT - 3, 0)
                split_static(c0 + FT, HK * P)
                hidden(c0 + FT, f0 + FT, f0 + FT - 2, 1)
                last = n == 3
                a = (norm + 1) * DT

                def down(j, q, next_cols):
                    split_lo(2 * j + (c0 + FT + 1), 1, HK * P)
                    if next_cols is not None:
                        split_lo(2 * j + (c0 + FT + 2), 0, next_cols)
                    dve.wait_ge(w_used, 2 * j + (c0 + FT + 2))
                    add_to_x(j, 4 + q, 0.5, x_ready)
                    if not last:
                        x_low(norm + 1, j, j + (a + 1))

                with dve.Fori(0, DT // 2 - 1) as i:
                    for q in range(2):
                        down(2 * i + q, q, HK * P)
                down(DT - 2, 0, HK * P)
                down(DT - 1, 1, SLOT if not last else None)

            for j in range(DT):
                dve.wait_ge(turned, j + 1)
                dve.tensor_copy(x_res[:, j, :], ps[:, j, :]).then_inc(x_ready, 1)
            dve.wait_ge(turned, DT + 1)
            dve.tensor_copy(params[:, :], ps[:, 0, 0:PARAM_ROWS]).then_inc(turned_out, 1)
            dve.wait_ge(turned_out, 1)
            for j in range(DT):
                x_low(0, j, j + 1)
            split_static(0)
            ffn(0)

            c0 = C_CONV
            todo = [(i, k) for i in range(CT) for k in range(TAPS)]

            def tap(i, k):
                seen = a_pad[:, i, k:k + S]
                w = taps[:, k * CT + i:k * CT + i + 1]
                if k == 0:
                    step(dve.tensor_scalar(y[:, i, :], seen, w, params[:, ROW_CONV_B + i:ROW_CONV_B + i + 1],
                                           ALU.mult, ALU.add))
                elif k < TAPS - 1:
                    step(dve.scalar_tensor_tensor(y[:, i, :], seen, w, y[:, i, :], ALU.mult, ALU.add))
                else:
                    dve.scalar_tensor_tensor(y[:, i, :], seen, w, y[:, i, :], ALU.mult, ALU.add).then_inc(conv_made, 1)

            def convolve(n):
                for _ in range(min(n, len(todo))):
                    tap(*todo.pop(0))

            for i in range(CT):
                split_static(c0 + i + 1)
                if i == 0:
                    step(dve.memset(a_pad[:, :, 0:PAD], 0.0))
                    invert_rms(NORM_CONV)
                    invert_rms_tok(1)
                    step(dve.tensor_tensor(rinv2[:, :], tok_rinv[:, :], tok_rinv[:, :], ALU.mult))
                dve.wait_ge(w_used, c0 + i + 1)
                dve.tensor_tensor(g_buf[:, 0, :], ps[:, 2 * (i % 2) + 1, :], rinv[:, :], ALU.mult).then_inc(a_gate_scaled, 1)
                dve.tensor_tensor(g_buf[:, 1, :], ps[:, 2 * (i % 2), :], rinv[:, :], ALU.mult).then_inc(a_val_scaled, 1)
                dve.wait_ge(a_val_scaled, i + 1)
                dve.wait_ge(a_sigmoid, i + 1)
                step(dve.tensor_tensor(a_pad[:, i, PAD:PAD + S], g_buf[:, 0, :], g_buf[:, 1, :], ALU.mult))
            split_static(c0 + 5)
            split_static(c0 + 6)
            dve.wait_ge(w_used, c0 + 6)
            for t in range(TT):
                raw = ps[:, 4 + t, :].rearrange("p (g c) -> p g c", g=GB)
                step(dve.tensor_reduce(v_mean[:, t, :], raw, AX.X, ALU.add))
                step(dve.tensor_scalar(v_mean[:, t, :], v_mean[:, t, :], 1.0 / P, None, ALU.mult))
                dve.tensor_tensor(v_cen[:, t], raw, v_mean[:, t, :].unsqueeze(2).to_broadcast([P, GB, P]),
                                  ALU.subtract).then_inc(v_centred, 1)
            for t in range(TT):
                dve.wait_ge(v_squared, t + 1)
                step(dve.tensor_reduce(v_stat[:, t, :], u[:, t, :].rearrange("p (g c) -> p g c", g=GB), AX.X, ALU.add))
            dve.tensor_tensor(v_stat[:, :, :], v_stat[:, :, :], rinv2[:, :].unsqueeze(2).to_broadcast([P, TT, GB]),
                              ALU.mult).then_inc(v_stat_made, 1)
            dve.wait_ge(v_std_made, 1)
            step(dve.reciprocal(v_rstd[:, :, :], v_stat[:, :, :]))
            dve.tensor_tensor(v_rstd[:, :, :], v_rstd[:, :, :], tok_rinv[:, :].unsqueeze(2).to_broadcast([P, TT, GB]),
                              ALU.mult).then_inc(v_rstd_made, 1)
            split_static(c0 + 7)
            dve.wait_ge(turned, DT + 2)
            dve.tensor_copy(taps[:, :], ps[:, 4, 0:TAPS * CT]).then_inc(turned_out, 1)
            dve.wait_ge(turned, DT + 3)
            dve.tensor_copy(sp_rows[:, :, :], ps[:, 5, :].rearrange("p (g t) -> p g t", g=GB)).then_inc(turned_out, 1)
            dve.wait_ge(turned_out, 3)
            for t in range(TT):
                dve.wait_ge(v_n_hi_made, t + 1)
                dve.tensor_tensor(v_n_lo[:, t, :], v_cen[:, t].rearrange("p g c -> p (g c)"),
                                  v_n_hi[:, t, :].bitcast(F32), ALU.subtract).then_inc(v_n_lo_made, 1)
            for g in range(GB):
                if g % 2 == 0:
                    dve.wait_ge(w_used, c0 + 7 + g // 2)
                dve.tensor_tensor(u[:, g, :], ps[:, g, :], rinv[:, :], ALU.mult).then_inc(u_scaled, 1)
            dve.wait_ge(u_scaled, GB)
            split_static(c0 + 8)
            for g in range(GB):
                dve.wait_ge(mixed, g + 1)
                step(dve.tensor_tensor(v_cen[:, g].rearrange("p g c -> p (g c)").rearrange("p (t c) -> p t c", t=TT),
                                       ps[:, 4 + g, :].rearrange("p (t c) -> p t c", t=TT),
                                       sp_bias[:, g, :].unsqueeze(1).to_broadcast([P, TT, P]), ALU.add))
                dve.tensor_tensor(u[:, g, :], u[:, g, :], v_cen[:, g].rearrange("p g c -> p (g c)"),
                                  ALU.mult).then_inc(b_made, 1)
            convolve(124)
            split_static(c0 + 9)

            def add_b(lo, hi):
                for j in range(lo, hi):
                    if j % 4 == 0:
                        dve.wait_ge(w_used, c0 + 9 + j // 4)
                    xj = x_res[:, j, :]
                    dve.tensor_tensor(xj, ps[:, j % 4, :], xj, ALU.add).then_inc(x_added, 1)

            add_b(0, 4)
            dve.wait_ge(y_mean_sum, 1)
            step(dve.tensor_scalar(g_buf[:, 0, :], ps[:, 4, :], 1.0 / CA, None, ALU.mult))
            for i in range(CT):
                dve.tensor_tensor(y[:, i, :], y[:, i, :], g_buf[:, 0, :], ALU.subtract).then_inc(y_centred, 1)
            split_static(c0 + 10)
            add_b(4, 8)
            dve.wait_ge(y_std_made, 1)
            step(dve.reciprocal(g_buf[:, 1, :], rms[:, :]))
            for i in range(CT):
                dve.wait_ge(y_squared, CT)
                dve.tensor_tensor(y[:, i, :], y[:, i, :], g_buf[:, 1, :], ALU.mult).then_inc(y_normed, 1)
            for i in range(CT):
                dve.wait_ge(a_hi_made, i + 1)
                dve.tensor_tensor(ab_lo[:, i, :], y[:, i, :], ab_hi[:, i, :].bitcast(F32), ALU.subtract).then_inc(a_lo_made, 1)
            split_static(c0 + 11)
            dve.wait_ge(x_added, DT)
            for j in range(DT):
                if j == 4:
                    split_static(c0 + 12)
                dve.wait_ge(w_used, c0 + 11 + j // 4)
                add_to_x(j, 4 + j % 4, 1.0, x_ready)
                x_low(2, j, 2 * DT + j + 1)
            ffn(1)
            ffn(2)

            c0 = C_ATT
            for n in range(4):
                split_static(c0 + n + 1)
                if n == 0:
                    invert_rms(NORM_ATT)
                    invert_rms_tok(2)
                if n % 2:
                    half = n // 2
                    for t in range(TT):
                        dve.wait_ge(v_hi_made, 4 * half + t + 1)
                        cols = slice(half * 512, (half + 1) * 512)
                        dve.scalar_tensor_tensor(v_lo[:, t, cols], ps[:, 4 * half + t, :], tok_rinv[:, t:t + 1],
                                                 v_hi[:, t, cols].bitcast(F32), ALU.mult,
                                                 ALU.subtract).then_inc(v_lo_made, 1)

            def split_proj(n):
                if n % 2:
                    dve.wait_ge(w_used, c0 + 5 + n // 2)
                else:
                    dve.wait_ge(proj_summed, n // 2 + 1)
                dve.scalar_tensor_tensor(qk_f[:, :], ps[:, 6, :], 1.0 if n % 2 else DH ** -0.5, rinv[:, :],
                                         ALU.mult, ALU.mult).then_inc(proj_scaled, 1)
                dve.wait_ge(proj_scaled, n + 1)
                dve.wait_ge(proj_hi_made, n + 1)
                dve.tensor_tensor(qk_lo[:, (n // 2) % 2, n % 2, :], qk_f[:, :],
                                  qk_hi[:, (n // 2) % 2, n % 2, :].bitcast(F32), ALU.subtract).then_inc(proj_lo_made, 1)
                dve.wait_ge(proj_lo_made, n + 1)

            def zall(h):
                at = 3 * (h % 2) * 512
                return ps[:, :, :].rearrange("p a c -> p (a c)")[:, at:at + SCORES]

            def split_out(j):
                dve.wait_ge(o_hi_made, j + 1)
                cols = slice(j * P, (j + 1) * P)
                dve.tensor_tensor(v_lo[:, :, cols], o_att[:, j, :].rearrange("p (t c) -> p t c", t=TT),
                                  v_hi[:, :, cols].bitcast(F32), ALU.subtract).then_inc(o_lo_made, 1)

            split_proj(0)
            split_proj(1)
            split_static(c0 + 5)
            for h in range(HEADS + 2):
                if h + 2 < HEADS:
                    split_proj(h + 2)
                if h < HEADS:
                    dve.wait_ge(log1p_made, h + 1)
                    dve.scalar_tensor_tensor(keep[:, :], zall(h), 0.0, keep[:, :], ALU.max, ALU.add).then_inc(keep_made, 1)
                    dve.wait_ge(keep_masked, h + 1)
                    if h >= 1:
                        dve.wait_ge(suffix_summed, h)
                    dve.tensor_copy(keep_hi[:, :], keep[:, :]).then_inc(keep_hi_made, 1)
                    dve.wait_ge(keep_hi_made, h + 1)
                    dve.tensor_tensor(keep_lo[:, :], keep[:, :], keep_hi[:, :].bitcast(F32),
                                      ALU.subtract).then_inc(keep_lo_made, 1)
                if 1 <= h <= HEADS:
                    dve.wait_ge(prob_masked, h)
                    if h >= 2:
                        dve.wait_ge(att_summed, h - 1)
                    dve.tensor_copy(prob_hi[:, :], prob[:, :]).then_inc(prob_hi_made, 1)
                    dve.wait_ge(prob_hi_made, h)
                    dve.tensor_tensor(prob_lo[:, :], prob[:, :], prob_hi[:, :].bitcast(F32),
                                      ALU.subtract).then_inc(prob_lo_made, 1)
                if h % 2 == 0 and h <= 12:
                    split_static(c0 + 6 + h // 2)
                if h >= 3 and h % 2:
                    split_out((h - 3) // 2)
            for n in range(4):
                split_static(c0 + 13 + n)
                for j in range(2 * n, 2 * n + 2):
                    dve.wait_ge(w_used, c0 + 13 + n)
                    add_to_x(j, 4 + j % 4, 1.0, x_ready)
                    x_low(5, j, 5 * DT + j + 1)
            ffn(3)
            invert_rms_tok(3)
            for n in range(0, 8, 2):
                dve.wait_ge(fin_turned, n + 1)
                t, half = n // 2, n % 2
                if n:
                    dve.wait_ge(fin_scaled, n)
                dve.tensor_scalar(out_tok[:, t, half * 512:(half + 1) * 512], ps[:, [0, 1, 2, 3, 4, 5, 6, 0][n], :],
                                  tok_rinv[:, t:t + 1], None, ALU.mult).then_inc(fin_scaled, 1)

        @block.gpsimd
        def _(pool):
            steps = [0]

            def step(ins):
                steps[0] += 1
                ins.then_inc(pool_step, 1)
                pool.wait_ge(pool_step, steps[0])

            def clear_ssq(n):
                if n:
                    if n - 1 in (NORM_CONV, NORM_ATT):
                        pool.wait_ge(tok_summed, 1 if n - 1 == NORM_CONV else 2)
                    pool.wait_ge(ssq_summed, n)
                pool.memset(ssq[:, :], 0.0).then_inc(ssq_cleared, 1)
                pool.wait_ge(ssq_cleared, n + 1)

            def square_tile(j, count):
                pool.wait_ge(x_ready, count)
                xj = x_res[:, bass.ds(j, 1), :].rearrange("p a s -> p (a s)")
                pool.tensor_tensor(sq[:, :], xj, xj, ALU.mult).then_inc(sq_made, 1)
                pool.wait_ge(sq_made, count)
                pool.tensor_tensor(ssq[:, :], ssq[:, :], sq[:, :], ALU.add).then_inc(ssq_added, 1)
                pool.wait_ge(ssq_added, count)

            def ffn(n):
                f0, norm = n * FT, NORM_FFN[n]
                with pool.Fori(0, FT // 2) as i:
                    for s in range(2):
                        pool.wait_ge(hid_hi_made, 2 * i + (f0 + s + 1))
                        pool.tensor_tensor(hid_lo[:, bass.ds(2 * i + s, 1), :].rearrange("p a s -> p (a s)"),
                                           up[:, s, :], hid_hi[:, bass.ds(2 * i + s, 1), :].rearrange(
                                               "p a s -> p (a s)").bitcast(F32), ALU.subtract).then_inc(hid_lo_made, 1)
                clear_ssq(norm + 1)
                with pool.Fori(0, DT) as j:
                    square_tile(j, j + ((norm + 1) * DT + 1))

            def mask_diagonals(of, compare, count_sem):
                for b in range(TT):
                    at = KEY_OFF[b]
                    ins = pool.affine_select(out=of[:, at:at + P], in_=of[:, at:at + P], compare_op=compare, fill=0.0,
                                             base=0, pattern=[[1, P]], channel_multiplier=-1)
                ins.then_inc(count_sem, 1)

            step(pool.memset(ident[:, :], 0.0))
            pool.affine_select(out=ident[:, :], in_=ident[:, :], compare_op=ALU.not_equal, fill=1.0, base=0,
                               pattern=[[-1, P]], channel_multiplier=1).then_inc(consts_made, 1)
            pool.memset(ones[:, :], 1.0)
            pool.memset(eps_col[:, :], EPS)
            step(pool.memset(neg_ones[:, :].bitcast(F32), -1.0))
            pool.affine_select(out=neg_tri[:, :], in_=neg_ones[:, :].bitcast(F32), compare_op=ALU.is_ge, fill=0.0, base=0,
                               pattern=[[-1, P]], channel_multiplier=1).then_inc(consts_made, 1)
            clear_ssq(0)
            for j in range(DT):
                square_tile(j, j + 1)
            ffn(0)

            for t in range(TT):
                pool.wait_ge(v_rstd_made, 1)
                if t == 0:
                    pool.wait_ge(mixer_params, 16 * 5)
                v4 = v_cen[:, t]
                step(pool.tensor_tensor(v4, v4, v_rstd[:, t, :].unsqueeze(2).to_broadcast([P, GB, P]), ALU.mult))
                vt = v4.rearrange("p g c -> p (g c)")
                step(pool.tensor_tensor(vt, vt, lnv_g[:, :], ALU.mult))
                pool.tensor_tensor(vt, vt, lnv_b[:, :], ALU.add).then_inc(v_normed, 1)
            pool.wait_ge(turned_out, 3)
            for g in range(GB):
                ins = pool.affine_select(out=sp_rows[:, g, :], in_=sp_rows[:, g, :], compare_op=ALU.is_ge, fill=0.0, base=0,
                                         pattern=[[1, P]], channel_multiplier=-1)
            step(ins)
            step(pool.tensor_copy(sp_hi[:, :, :], sp_rows[:, :, :]))
            pool.tensor_tensor(sp_lo[:, :, :], sp_rows[:, :, :], sp_hi[:, :, :].bitcast(F32), ALU.subtract).then_inc(sp_ready, 1)
            for g in range(GB):
                pool.wait_ge(b_hi_made, g + 1)
                pool.tensor_tensor(ab_lo[:, CT + g, :], u[:, g, :], ab_hi[:, CT + g, :].bitcast(F32),
                                   ALU.subtract).then_inc(b_lo_made, 1)
            pool.wait_ge(conv_made, 2)
            step(pool.tensor_tensor(sq[:, :], y[:, 0, :], y[:, 1, :], ALU.add))
            pool.wait_ge(conv_made, 3)
            step(pool.tensor_tensor(sq[:, :], sq[:, :], y[:, 2, :], ALU.add))
            pool.wait_ge(conv_made, 4)
            pool.tensor_tensor(sq[:, :], sq[:, :], y[:, 3, :], ALU.add).then_inc(ysum_made, 1)
            ysq = [v_cen[:, i].rearrange("p g c -> p (g c)") for i in range(CT)]
            pool.wait_ge(y_squared, 2)
            step(pool.tensor_tensor(sq[:, :], ysq[0], ysq[1], ALU.add))
            pool.wait_ge(y_squared, 3)
            step(pool.tensor_tensor(sq[:, :], sq[:, :], ysq[2], ALU.add))
            pool.wait_ge(y_squared, 4)
            pool.tensor_tensor(sq[:, :], sq[:, :], ysq[3], ALU.add).then_inc(ysq_sum_made, 1)
            clear_ssq(2)
            for j in range(DT):
                square_tile(j, 2 * DT + j + 1)
            ffn(1)
            ffn(2)

            for h in range(HEADS + 1):
                if h < HEADS:
                    pool.wait_ge(keep_made, h + 1)
                    mask_diagonals(keep, ALU.is_gt, keep_masked)
                if h >= 1:
                    pool.wait_ge(prob_made, h)
                    mask_diagonals(prob, ALU.is_gt, prob_masked)
            clear_ssq(5)
            for j in range(DT):
                square_tile(j, 5 * DT + j + 1)
            ffn(3)


_INS = ["x", "g_ffn1", "w_ffn1_gate", "w_ffn1_up", "w_ffn1_down", "g_mix", "w_in_ab", "conv_w", "conv_b", "ln_a_g",
        "ln_a_b", "ln_v_g", "ln_v_b", "sp_w", "sp_b", "w_out_ab", "w_qkv", "w_o", "g_ffn2", "w_ffn2_gate",
        "w_ffn2_up", "w_ffn2_down", "g_final"]
_OUT = ((1, S, D), "float32")


def kernel(**inputs):
    import numpy as _np
    import concourse.bacc as _bacc
    from concourse import mybir as _mybir
    from concourse.bass_utils import run_bass_kernel_spmd as _run

    nc = _bacc.Bacc("TRN2", target_bir_lowering=False, num_devices=1)
    arrays, args = {}, []
    for name in _INS:
        a = _np.ascontiguousarray(inputs[name])
        arrays[f"in_{name}_dram"] = a
        args.append(nc.dram_tensor(f"in_{name}_dram", a.shape, _mybir.dt.from_np(a.dtype), kind="ExternalInput").ap())
    shape, dtype = _OUT
    args.append(nc.dram_tensor("out_0_dram", shape, _mybir.dt.from_np(_np.dtype(dtype)), kind="ExternalOutput").ap())
    trunk_kernel(nc, *args)
    r = _run(nc, [arrays], core_ids=[0])
    return r.results[0]["out_0_dram"]
```

```python
from contextlib import ExitStack

import concourse.bass as bass
from concourse import mybir

F32 = mybir.dt.float32
F32R = mybir.dt.float32r
ALU = mybir.AluOpType
ACT = mybir.ActivationFunctionType
AX = mybir.AxisListType

P = 128
S = 512
D = 1024
DT = D // P
TT = S // P
FF = 2816
FT = FF // P
HK = FT // 2
CA = 512
CT = CA // P
TAPS = 31
PAD = TAPS - 1
GB = 4
HEADS = 16
DH = 64
EPS = 1e-6
SLOT = 16 * P

FFN_CHUNKS = FT + 2 * DT
CONV_CHUNKS = 12
ATT_CHUNKS = 16
C_FFN = [0, FFN_CHUNKS + CONV_CHUNKS, 2 * FFN_CHUNKS + CONV_CHUNKS,
         3 * FFN_CHUNKS + CONV_CHUNKS + ATT_CHUNKS]
C_CONV = FFN_CHUNKS
C_ATT = 3 * FFN_CHUNKS + CONV_CHUNKS
CHUNKS = 4 * FFN_CHUNKS + CONV_CHUNKS + ATT_CHUNKS
NORM_FFN = [0, 2, 3, 5]
NORM_CONV, NORM_ATT, NORM_FINAL = 1, 4, 6
GAIN_ROW = [0, 2 * DT, 4 * DT, DT, 3 * DT, 5 * DT, 6 * DT]
ROW_LN_G, ROW_LN_B, ROW_CONV_B = 7 * DT, 7 * DT + CT, 7 * DT + 2 * CT
PARAM_ROWS = 7 * DT + 3 * CT
PE_TILE = CT - 1
EARLY = 16
TAPS_AT = [10, 10, 8, 26, 27, 2, 4, 1, 1]
KEY_COLS = [S - P * b for b in range(TT)]
KEY_OFF = [0, 512, 1024, 896]
SCORES = 1280
EXP_LN_SET = 6


def trunk_kernel(nc, x, g_ffn1, w_ffn1_gate, w_ffn1_up, w_ffn1_down, g_mix, w_in_ab, conv_w, conv_b,
                 ln_a_g, ln_a_b, ln_v_g, ln_v_b, sp_w, sp_b, w_out_ab, w_qkv, w_o, g_ffn2,
                 w_ffn2_gate, w_ffn2_up, w_ffn2_down, g_final, out):
    ctx = ExitStack()
    with ctx:
        def sb(name, shape, dt=F32, scope=ctx):
            return scope.enter_context(nc.sbuf_tensor(name, shape, dt))

        def sem(name):
            return ctx.enter_context(nc.semaphore(name))

        x_res = sb("x_res", [P, DT, S])
        xg_hi = sb("xg_hi", [P, DT, S], F32R)
        xg_lo = sb("xg_lo", [P, DT, S], F32R)
        stage = sb("stage", [P, 2, SLOT])
        w_hi = sb("w_hi", [P, 2, SLOT], F32R)
        w_lo = sb("w_lo", [P, 2, SLOT], F32R)
        sq = sb("sq", [P, S])
        ssq = sb("ssq", [P, S])
        rms = sb("rms", [P, S])
        rinv = sb("rinv", [P, S])
        tok_rms = sb("tok_rms", [P, TT])
        tok_rinv = sb("tok_rinv", [P, TT])
        ones = sb("ones", [P, P])
        neg_ones = sb("neg_ones", [P, P], F32R)
        neg_tri = sb("neg_tri", [P, P], F32R)
        ident = sb("ident", [P, P])
        params = sb("params", [P, PARAM_ROWS])
        taps = sb("taps", [P, TAPS * CT])
        eps_col = sb("eps_col", [P, 1])
        ps = ctx.enter_context(nc.psum_tensor("ps", [P, 8, 512], F32))

        with ExitStack() as begin:
            x_tok = sb("x_tok", [P, TT, D], scope=begin)
            param_rows = sb("param_rows", [PARAM_ROWS, P], scope=begin)
            conv_rows = sb("conv_rows", [TAPS * CT, P], scope=begin)
        with ExitStack() as ffn_scope:
            hid_hi = sb("hid_hi", [P, FT, S], F32R, ffn_scope)
            hid_lo = sb("hid_lo", [P, FT, S], F32R, ffn_scope)
            gate = sb("gate", [P, 2, S], scope=ffn_scope)
            up = sb("up", [P, 2, S], scope=ffn_scope)
        with ExitStack() as conv_scope:
            a_pad = sb("a_pad", [P, CT, PAD + S], scope=conv_scope)
            y = sb("y", [P, CT, S], scope=conv_scope)
            v_mean = sb("v_mean", [P, TT, GB], scope=conv_scope)
            v_stat = sb("v_stat", [P, TT, GB], scope=conv_scope)
            v_rstd = sb("v_rstd", [P, TT, GB], scope=conv_scope)
            rinv2 = sb("rinv2", [P, TT], scope=conv_scope)
            g_buf = sb("g_buf", [P, 2, S], scope=conv_scope)
            sp_rows = sb("sp_rows", [P, GB, P], scope=conv_scope)
            sp_hi = sb("sp_hi", [P, GB, P], F32R, conv_scope)
            sp_lo = sb("sp_lo", [P, GB, P], F32R, conv_scope)
            sp_bias = sb("sp_bias", [P, GB, P], scope=conv_scope)
            lnv_g = sb("lnv_g", [P, S], scope=conv_scope)
            lnv_b = sb("lnv_b", [P, S], scope=conv_scope)
            taps_hi = sb("taps_hi", [P, TAPS], F32R, conv_scope)
            taps_lo = sb("taps_lo", [P, TAPS], F32R, conv_scope)
            with ExitStack() as early_scope:
                diags_early = [sb(f"diags_early_{part}", [P, EARLY, P], F32R, early_scope) for part in ("hi", "lo")]
            u = sb("u", [P, GB, S], scope=conv_scope)
            v_cen = sb("v_cen", [P, TT, GB, P], scope=conv_scope)
            v_n_hi = sb("v_n_hi", [P, TT, S], F32R, conv_scope)
            v_n_lo = sb("v_n_lo", [P, TT, S], F32R, conv_scope)
            with ExitStack() as late_scope:
                a_pad_hi = sb("a_pad_hi", [P, PAD + S], F32R, late_scope)
                a_pad_lo = sb("a_pad_lo", [P, PAD + S], F32R, late_scope)
                diags_late = [sb(f"diags_late_{part}", [P, TAPS - EARLY, P], F32R, late_scope) for part in ("hi", "lo")]
            ab_hi = sb("ab_hi", [P, 2 * CT, S], F32R, conv_scope)
            ab_lo = sb("ab_lo", [P, 2 * CT, S], F32R, conv_scope)
        with ExitStack() as att_scope:
            v_hi = sb("v_hi", [P, TT, D], F32R, att_scope)
            v_lo = sb("v_lo", [P, TT, D], F32R, att_scope)
            qk_f = sb("qk_f", [P, S], scope=att_scope)
            qk_hi = sb("qk_hi", [P, 2, 2, S], F32R, att_scope)
            qk_lo = sb("qk_lo", [P, 2, 2, S], F32R, att_scope)
            keep = sb("keep", [P, SCORES], scope=att_scope)
            keep_hi = sb("keep_hi", [P, SCORES], F32R, att_scope)
            keep_lo = sb("keep_lo", [P, SCORES], F32R, att_scope)
            prob = sb("prob", [P, SCORES], scope=att_scope)
            prob_hi = sb("prob_hi", [P, SCORES], F32R, att_scope)
            prob_lo = sb("prob_lo", [P, SCORES], F32R, att_scope)
            o_att = sb("o_att", [P, DT, S], scope=att_scope)
        with ExitStack() as end:
            out_tok = sb("out_tok", [P, TT, D], scope=end)

        x_loaded = [sem(f"x_loaded{t}") for t in range(TT)]
        params_loaded = sem("params_loaded")
        mixer_params = sem("mixer_params")
        consts_made = sem("consts_made")
        turned = sem("turned")
        turned_out = sem("turned_out")
        w_loaded = [sem("w_loaded0"), sem("w_loaded1")]
        w_hi_made = sem("w_hi_made")
        w_lo_made = sem("w_lo_made")
        w_used = sem("w_used")
        x_ready = sem("x_ready")
        xg_hi_made = sem("xg_hi_made")
        xg_lo_made = sem("xg_lo_made")
        x_added = sem("x_added")
        ssq_cleared = sem("ssq_cleared")
        sq_made = sem("sq_made")
        ssq_added = sem("ssq_added")
        ssq_summed = sem("ssq_summed")
        rms_made = sem("rms_made")
        rinv_made = sem("rinv_made")
        tok_summed = sem("tok_summed")
        tok_rms_made = sem("tok_rms_made")
        tok_rinv_made = sem("tok_rinv_made")
        gate_scaled = sem("gate_scaled")
        up_scaled = sem("up_scaled")
        silu_made = sem("silu_made")
        gated = sem("gated")
        hid_hi_made = sem("hid_hi_made")
        hid_lo_made = sem("hid_lo_made")
        pool_step = sem("pool_step")
        dve_step = sem("dve_step")
        act_step = sem("act_step")
        a_gate_scaled = sem("a_gate_scaled")
        a_val_scaled = sem("a_val_scaled")
        a_sigmoid = sem("a_sigmoid")
        taps_hi_made = sem("taps_hi_made")
        taps_lo_made = sem("taps_lo_made")
        diags_made = sem("diags_made")
        a_made = sem("a_made")
        a_pad_hi_made = sem("a_pad_hi_made")
        a_pad_lo_made = sem("a_pad_lo_made")
        taps_summed = sem("taps_summed")
        taps_copied = sem("taps_copied")
        late_added = sem("late_added")
        v_scaled = sem("v_scaled")
        v_centred = sem("v_centred")
        v_squared = sem("v_squared")
        v_stat_made = sem("v_stat_made")
        v_std_made = sem("v_std_made")
        v_rstd_made = sem("v_rstd_made")
        v_normed = sem("v_normed")
        v_n_hi_made = sem("v_n_hi_made")
        v_n_lo_made = sem("v_n_lo_made")
        sp_ready = sem("sp_ready")
        u_scaled = sem("u_scaled")
        mixed = sem("mixed")
        b_made = sem("b_made")
        b_hi_made = sem("b_hi_made")
        b_lo_made = sem("b_lo_made")
        conv_made = sem("conv_made")
        ysum_made = sem("ysum_made")
        y_mean_sum = sem("y_mean_sum")
        y_centred = sem("y_centred")
        y_squared = sem("y_squared")
        ysq_sum_made = sem("ysq_sum_made")
        y_var_sum = sem("y_var_sum")
        y_std_made = sem("y_std_made")
        y_normed = sem("y_normed")
        a_silu = sem("a_silu")
        a_hi_made = sem("a_hi_made")
        a_lo_made = sem("a_lo_made")
        mix_summed = sem("mix_summed")
        v_half_summed = sem("v_half_summed")
        v_hi_made = sem("v_hi_made")
        v_lo_made = sem("v_lo_made")
        proj_summed = sem("proj_summed")
        proj_scaled = sem("proj_scaled")
        proj_hi_made = sem("proj_hi_made")
        proj_lo_made = sem("proj_lo_made")
        scores_summed = sem("scores_summed")
        log1p_made = sem("log1p_made")
        keep_made = sem("keep_made")
        keep_masked = sem("keep_masked")
        keep_hi_made = sem("keep_hi_made")
        keep_lo_made = sem("keep_lo_made")
        suffix_summed = sem("suffix_summed")
        prob_made = sem("prob_made")
        prob_masked = sem("prob_masked")
        prob_hi_made = sem("prob_hi_made")
        prob_lo_made = sem("prob_lo_made")
        att_summed = sem("att_summed")
        o_part_summed = sem("o_part_summed")
        o_half_summed = sem("o_half_summed")
        o_copied = sem("o_copied")
        o_hi_made = sem("o_hi_made")
        o_lo_made = sem("o_lo_made")
        y_fin_made = sem("y_fin_made")
        fin_turned = sem("fin_turned")
        fin_scaled = sem("fin_scaled")
        out_stored = sem("out_stored")

        ffn_weights = [(w_ffn1_gate[0], w_ffn1_up[0], w_ffn1_down[0]),
                       (w_ffn2_gate[0], w_ffn2_up[0], w_ffn2_down[0]),
                       (w_ffn1_gate[1], w_ffn1_up[1], w_ffn1_down[1]),
                       (w_ffn2_gate[1], w_ffn2_up[1], w_ffn2_down[1])]
        param_vectors = [g_ffn1, g_mix, g_ffn2, g_final.rearrange("(a d) -> a d", a=1), ln_a_g, ln_a_b, conv_b]
        x_dram = x.rearrange("b (t p) d -> p (b t) d", p=P)
        out_dram = out.rearrange("b (t p) d -> p (b t) d", p=P)

        def rows_of(w, k0, k1, cols):
            return w.rearrange("(k p) f -> p k f", p=P)[:, k0:k1, cols]

        def three(pe, to, a_hi, a_lo, b_hi, b_lo, start, stop=False):
            pe.matmul(to, a_hi, b_hi, start=start, stop=False, skip_group_check=True)
            pe.matmul(to, a_hi, b_lo, start=False, stop=False, skip_group_check=True)
            return pe.matmul(to, a_lo, b_hi, start=False, stop=stop, skip_group_check=True)

        block = ctx.enter_context(nc.Block())

        @block.sync
        def _(sp):
            def free_slot(c):
                sp.wait_ge(w_hi_made, c - 1)
                sp.wait_ge(w_lo_made, c - 1)

            def load(slot, first, second):
                for n, src in enumerate((first, second)):
                    k, cols = src.shape[1], src.shape[2]
                    at = n * first.shape[1] * cols
                    sp.dma_start(stage[:, slot, at:at + k * cols].rearrange("p (k f) -> p k f", k=k),
                                 src).then_inc(w_loaded[slot], 16)

            def load_ffn(n):
                w_gate, w_up, w_down = ffn_weights[n]
                c0 = C_FFN[n]

                def pair(f, slot):
                    load(slot, rows_of(w_gate, 0, DT, bass.ds(f * P, P)), rows_of(w_up, 0, DT, bass.ds(f * P, P)))

                for f in range(2):
                    if c0 + f >= 2:
                        free_slot(c0 + f)
                    pair(f, f)
                with sp.Fori(1, FT // 2) as i:
                    for s in range(2):
                        free_slot(2 * i + (c0 + s))
                        pair(2 * i + s, s)
                with sp.Fori(0, DT) as j:
                    for s in range(2):
                        free_slot(2 * j + (c0 + FT + s))
                        k = s * HK
                        load(s, rows_of(w_down, k, k + 6, bass.ds(j * P, P)),
                             rows_of(w_down, k + 6, k + HK, bass.ds(j * P, P)))

            def load_cols(c, w, k0, k1, col0, cols):
                free_slot(c)
                mid = (k0 + k1) // 2
                load(c % 2, rows_of(w, k0, mid, slice(col0, col0 + cols)),
                     rows_of(w, mid, k1, slice(col0, col0 + cols)))

            def load_pair(c, w, col_a, col_b):
                free_slot(c)
                load(c % 2, rows_of(w, 0, DT, slice(col_a, col_a + P)), rows_of(w, 0, DT, slice(col_b, col_b + P)))

            for t in range(TT):
                sp.dma_start(x_tok[:, t, :], x_dram[:, t, :]).then_inc(x_loaded[t], 16)
            load_ffn(0)

            w_in, w_out = w_in_ab[0], w_out_ab[0]
            for i in range(CT):
                load_pair(C_CONV + i, w_in, i * P, CA + i * P)
            sp.wait_ge(w_used, C_CONV)
            sp.dma_start(sp_rows[:, :, :], sp_w[0].rearrange("g t s -> t g s")).then_inc(mixer_params, 16)
            sp.dma_start(sp_bias[:, :, :], sp_b[0].partition_broadcast(P)).then_inc(mixer_params, 16)
            sp.dma_start(lnv_g[:, :], ln_v_g[0].rearrange("g d -> (g d)").partition_broadcast(P)).then_inc(mixer_params, 16)
            sp.dma_start(lnv_b[:, :], ln_v_b[0].rearrange("g d -> (g d)").partition_broadcast(P)).then_inc(mixer_params, 16)
            for kh in range(2):
                load_cols(C_CONV + 4 + kh, w_in, 4 * kh, 4 * kh + 4, 3 * CA, CA)
            for i in range(2):
                load_pair(C_CONV + 6 + i, w_in, 2 * CA + 2 * i * P, 2 * CA + (2 * i + 1) * P)
            for n in range(4):
                k0 = CT if n < 2 else 0
                load_cols(C_CONV + 8 + n, w_out, k0, k0 + 4, (n % 2) * S, S)
            load_ffn(1)
            load_ffn(2)
            for n in range(4):
                load_cols(C_ATT + n, w_qkv[0], 4 * (n % 2), 4 * (n % 2) + 4, 2 * D + (n // 2) * 512, 512)
            for j in range(DT):
                load_pair(C_ATT + 4 + j, w_qkv[0], j * P, D + j * P)
            for n in range(4):
                k0 = 4 * (n // 2)
                load_cols(C_ATT + 12 + n, w_o[0], k0, k0 + 4, (n % 2) * 512, 512)
            load_ffn(3)

            for t in range(TT):
                sp.wait_ge(fin_scaled, 2 * (t + 1))
                sp.dma_start(out_dram[:, t, :], out_tok[:, t, :]).then_inc(out_stored, 16)
            sp.wait_ge(out_stored, 16 * TT)

        @block.tensor
        def _(pe):
            def sum_squares():
                return pe.matmul(ps[:, 6, :], ones[:, :], ssq[:, :], start=True, stop=True)

            def sum_squares_tok():
                for t in range(TT):
                    mm = pe.matmul(ps[:, 7, t:t + 1], ssq[:, t * P:(t + 1) * P], ones[:, 0:1], start=True, stop=True)
                return mm

            def tile(slot, n):
                return w_hi[:, slot, n * P:(n + 1) * P], w_lo[:, slot, n * P:(n + 1) * P]

            def pair_chunk(slot, banks, norm=None, tok=False, wait_x=None):
                for k in range(DT):
                    if wait_x is not None:
                        pe.wait_ge(xg_lo_made, wait_x * DT + k + 1)
                    for n in range(2):
                        mm = three(pe, ps[:, banks[n], :], *tile(slot, n * DT + k),
                                   xg_hi[:, k, :], xg_lo[:, k, :], start=(k == 0), stop=(k == DT - 1))
                    if norm is not None and k == 5:
                        pe.wait_ge(ssq_added, (norm + 1) * DT)
                        sum_squares().then_inc(ssq_summed, 1)
                        if tok:
                            sum_squares_tok().then_inc(tok_summed, 1)
                mm.then_inc(w_used, 1)

            def ffn(n):
                c0, f0, norm = C_FFN[n], n * FT, NORM_FFN[n]
                for s in range(2):
                    pe.wait_ge(w_lo_made, c0 + s + 1)
                    pair_chunk(s, (2 * s, 2 * s + 1), norm if s == 0 else None, False, norm if s == 0 else None)
                with pe.Fori(1, FT // 2) as i:
                    for s in range(2):
                        pe.wait_ge(w_lo_made, 2 * i + (c0 + s + 1))
                        pe.wait_ge(up_scaled, 2 * i + (f0 + s - 1))
                        pair_chunk(s, (2 * s, 2 * s + 1))
                with pe.Fori(0, DT // 2) as i:
                    for q in range(2):
                        pe.wait_ge(x_ready, 2 * i + ((norm + 1) * DT + q - 1))
                        for s in range(2):
                            pe.wait_ge(w_lo_made, 4 * i + (c0 + FT + 2 * q + s + 1))
                            for k in range(HK):
                                if s == 1 and k == HK - 1:
                                    pe.wait_ge(hid_lo_made, f0 + FT)
                                elif s == 0 and k == 0:
                                    pe.wait_ge(hid_lo_made, f0 + FT - 1)
                                h = s * HK + k
                                mm = three(pe, ps[:, 4 + q, :], *tile(s, k), hid_hi[:, h, :], hid_lo[:, h, :],
                                           start=(h == 0), stop=(h == FT - 1))
                            mm.then_inc(w_used, 1)

            def v_chunk(slot, k0, bank0, stop, wait_x=None):
                for k in range(4):
                    if wait_x is not None:
                        pe.wait_ge(xg_lo_made, wait_x * DT + k0 + k + 1)
                    w_h, w_l = w_hi[:, slot, k * 512:(k + 1) * 512], w_lo[:, slot, k * 512:(k + 1) * 512]
                    for t in range(TT):
                        mm = three(pe, ps[:, bank0 + t, :], xg_hi[:, k0 + k, t * P:(t + 1) * P],
                                   xg_lo[:, k0 + k, t * P:(t + 1) * P], w_h, w_l,
                                   start=(k0 + k == 0), stop=(k0 + k == DT - 1))
                return mm

            pe.wait_ge(consts_made, 1)
            pe.wait_ge(params_loaded, 16 * 8)
            pe.transpose(ps[:, 7, 0:PARAM_ROWS], param_rows[:, :], ident[0:PARAM_ROWS, 0:PARAM_ROWS])
            pe.transpose(ps[:, 7, P:P + TAPS * CT], conv_rows[:, :], ident[0:TAPS * CT, 0:TAPS * CT]).then_inc(turned, 1)
            for j in range(DT):
                if j == DT - 1:
                    pe.wait_ge(turned_out, 1)
                for t in range(TT):
                    if j == 0:
                        pe.wait_ge(x_loaded[t], 16)
                    mm = pe.transpose(ps[:, j, t * P:(t + 1) * P], x_tok[:, t, j * P:(j + 1) * P], ident[:, :])
                mm.then_inc(turned, 1)
            pe.wait_ge(x_ready, DT)
            ffn(0)

            c0 = C_CONV
            for i in range(CT):
                pe.wait_ge(w_lo_made, c0 + i + 1)
                if i >= 2:
                    pe.wait_ge(a_val_scaled, i - 1)
                s = i % 2
                first = i == 0
                pair_chunk(s, (2 * s, 2 * s + 1), NORM_CONV if first else None, first, NORM_CONV if first else None)
            pe.wait_ge(mixer_params, 16 * 4)
            pe.wait_ge(a_val_scaled, 3)
            for g in range(GB):
                mm = pe.transpose(ps[:, 0, g * P:(g + 1) * P], sp_rows[:, g, :], ident[:, :])
            mm.then_inc(turned, 1)
            pe.wait_ge(rms_made, NORM_CONV + 1)
            pe.wait_ge(tok_rms_made, 1)
            pe.wait_ge(w_lo_made, c0 + 5)
            v_chunk(0, 0, 4, False).then_inc(w_used, 1)

            def convolve_diagonal(bank, diags, first):
                taps = diags[0].shape[1]
                for n in range(taps):
                    k = first + n
                    mm = three(pe, ps[:, bank, :], diags[0][:, n, :], diags[1][:, n, :], a_pad_hi[:, k:k + S],
                               a_pad_lo[:, k:k + S], start=(n == 0), stop=(n == taps - 1))
                mm.then_inc(taps_summed, 1)

            pe.wait_ge(diags_made, 2)
            pe.wait_ge(a_pad_lo_made, 1)
            convolve_diagonal(1, diags_early, 0)
            pe.wait_ge(w_lo_made, c0 + 6)
            v_chunk(1, 4, 4, True).then_inc(w_used, 1)
            pe.wait_ge(a_val_scaled, CT)
            pe.wait_ge(taps_copied, 1)
            pe.wait_ge(turned_out, 2)
            for i in range(2):
                pe.wait_ge(w_lo_made, c0 + 7 + i)
                pair_chunk(i, (2 * i, 2 * i + 1))
            pe.wait_ge(v_centred, TT)
            pe.wait_ge(diags_made, 4)
            convolve_diagonal(7, diags_late, EARLY)
            pe.wait_ge(sp_ready, 1)
            for g in range(GB):
                if g == 3:
                    pe.wait_ge(late_added, 1)
                for t in range(TT):
                    pe.wait_ge(v_n_lo_made, t + 1)
                    mm = three(pe, ps[:, 4 + g, t * P:(t + 1) * P], v_n_hi[:, t, g * P:(g + 1) * P],
                               v_n_lo[:, t, g * P:(g + 1) * P], sp_hi[:, g, :], sp_lo[:, g, :], start=True, stop=True)
                mm.then_inc(mixed, 1)
            for n in range(4):
                pe.wait_ge(w_lo_made, c0 + 9 + n)
                for m in range(4):
                    j = 4 * (n % 2) + m
                    if n == 0:
                        pe.wait_ge(u_scaled, m + 1)
                    elif n == 1 and m == 2:
                        pe.wait_ge(y_centred, CT)
                    elif n == 1 and m == 3:
                        pe.wait_ge(y_std_made, 1)
                    for k in range(4):
                        src = k + (CT if n < 2 else 0)
                        if n < 2:
                            pe.wait_ge(b_lo_made, k + 1)
                        else:
                            pe.wait_ge(a_lo_made, k + 1)
                        mm = three(pe, ps[:, j, :], *tile(n % 2, 4 * k + m), ab_hi[:, src, :], ab_lo[:, src, :],
                                   start=(n < 2 and k == 0), stop=(n >= 2 and k == 3))
                    if n >= 2 and m < 3:
                        mm.then_inc(mix_summed, 1)
                    if n == 0 and m == 1:
                        pe.wait_ge(ysum_made, 1)
                        pe.matmul(ps[:, 6, :], ones[:, :], sq[:, :], start=True, stop=True).then_inc(y_mean_sum, 1)
                mm.then_inc(w_used, 1)
                if n == 0:
                    pe.wait_ge(ysq_sum_made, 1)
                    pe.matmul(ps[:, 7, :], ones[:, :], sq[:, :], start=True, stop=True).then_inc(y_var_sum, 1)
            ffn(1)
            ffn(2)

            c0 = C_ATT
            for n in range(4):
                half, kh = n // 2, n % 2
                pe.wait_ge(w_lo_made, c0 + n + 1)
                if n == 2:
                    pe.wait_ge(rms_made, NORM_ATT + 1)
                    pe.wait_ge(tok_rms_made, 2)
                mm = v_chunk(n % 2, 4 * kh, 4 * half, kh == 1, NORM_ATT if half == 0 else None)
                mm.then_inc(w_used, 1)
                if n == 0:
                    pe.wait_ge(ssq_added, (NORM_ATT + 1) * DT)
                    sum_squares().then_inc(ssq_summed, 1)
                    sum_squares_tok().then_inc(tok_summed, 1)

            def project(n):
                slot = (n // 2) % 2
                pe.wait_ge(w_lo_made, c0 + 5 + n // 2)
                if n == 0:
                    pe.wait_ge(v_lo_made, 2 * TT)
                else:
                    pe.wait_ge(proj_scaled, n)
                for k in range(DT):
                    mm = three(pe, ps[:, 6, :], *tile(slot, (n % 2) * DT + k), xg_hi[:, k, :], xg_lo[:, k, :],
                               start=(k == 0), stop=(k == DT - 1))
                mm.then_inc(w_used if n % 2 else proj_summed, 1)

            def zcols(h, b, skip=0):
                at = 3 * (h % 2) * 512 + KEY_OFF[b] + skip * P
                return ps[:, :, :].rearrange("p a c -> p (a c)")[:, at:at + KEY_COLS[b] - skip * P]

            def scores(h):
                j, r0 = h // 2, DH * (h % 2)
                pe.wait_ge(proj_lo_made, 2 * j + 2)
                if h >= 2:
                    pe.wait_ge(prob_made, h - 1)
                for b in range(TT):
                    r = slice(r0, r0 + DH)
                    mm = three(pe, zcols(h, b), qk_hi[r, j % 2, 1, b * P:(b + 1) * P],
                               qk_lo[r, j % 2, 1, b * P:(b + 1) * P], qk_hi[r, j % 2, 0, b * P:S],
                               qk_lo[r, j % 2, 0, b * P:S], start=(b < 3))
                mm.then_inc(scores_summed, 1)

            def suffix(h):
                pe.wait_ge(keep_lo_made, h + 1)
                for b in range(TT):
                    for part in (keep_hi, keep_lo):
                        off = KEY_OFF[b]
                        mm = pe.matmul(zcols(h, b), neg_tri[:, :], part[:, off:off + KEY_COLS[b]],
                                       start=False, stop=False, skip_group_check=True)
                        for later in range(b + 1, TT):
                            off = KEY_OFF[later]
                            mm = pe.matmul(zcols(h, b, later - b), neg_ones[:, :],
                                           part[:, off:off + KEY_COLS[later]],
                                           start=False, stop=False, skip_group_check=True)
                mm.then_inc(suffix_summed, 1)

            def attend(h):
                j = h // 2
                pe.wait_ge(prob_lo_made, h + 1)
                if h >= 1:
                    pe.wait_ge(o_copied, h)
                for b in range(TT):
                    off = KEY_OFF[b]
                    cols = slice(off, off + KEY_COLS[b])
                    mm = three(pe, ps[:, 7, b * P:S], v_hi[:, b, j * P:(j + 1) * P], v_lo[:, b, j * P:(j + 1) * P],
                               prob_hi[:, cols], prob_lo[:, cols], start=(b == 0), stop=(b == TT - 1))
                mm.then_inc(att_summed, 1)

            def out_tile(q, bank):
                n, k0 = q // 4, 4 * (q // 8)
                pe.wait_ge(w_lo_made, c0 + 13 + n)
                for k in range(4):
                    pe.wait_ge(o_lo_made, k0 + k + 1)
                    cols = slice((k0 + k) * P, (k0 + k + 1) * P)
                    mm = three(pe, ps[:, bank, :].rearrange("p (t c) -> p t c", t=TT), *tile(n % 2, 4 * k + q % 4),
                               v_hi[:, :, cols], v_lo[:, :, cols], start=(k == 0), stop=(k == 3))
                if q % 4 == 3:
                    mm.then_inc(w_used, 1)
                else:
                    mm.then_inc(o_part_summed if q < DT else o_half_summed, 1)

            def out_part(q):
                if q:
                    pe.wait_ge(x_added, q)
                else:
                    pe.wait_ge(proj_scaled, HEADS)
                out_tile(q, 6)

            for n in range(3):
                project(n)
            for h in range(HEADS + 2):
                if h < HEADS:
                    scores(h)
                if h >= 13 and h < 17:
                    out_part(2 * (h - 13))
                if 1 <= h <= HEADS:
                    suffix(h - 1)
                if h >= 2:
                    attend(h - 2)
                if h + 3 < HEADS:
                    project(h + 3)
                if h >= 13 and h < 17:
                    out_part(2 * (h - 13) + 1)
            for j in range(DT):
                if j >= 4:
                    pe.wait_ge(x_ready, NORM_FFN[3] * DT + j - 3)
                elif j == 2:
                    pe.wait_ge(x_added, DT)
                out_tile(DT + j, 4 + j % 4)
            ffn(3)

            pe.wait_ge(ssq_added, (NORM_FINAL + 1) * DT)
            sum_squares_tok().then_inc(tok_summed, 1)
            order = [0, 1, 2, 3, 4, 5, 6, 0]
            for t in range(TT):
                for half in range(2):
                    n = 2 * t + half
                    for m in range(4):
                        pe.wait_ge(y_fin_made, 4 * half + m + 1)
                        if n == 7 and m == 0:
                            pe.wait_ge(fin_scaled, 1)
                        mm = pe.transpose(ps[:, order[n], m * P:(m + 1) * P],
                                          x_res[:, 4 * half + m, t * P:(t + 1) * P], ident[:, :])
                    mm.then_inc(fin_turned, 1)

        @block.scalar
        def _(act):
            steps = [0]

            def step(ins):
                steps[0] += 1
                ins.then_inc(act_step, 1)
                act.wait_ge(act_step, steps[0])

            def split_hi(c, slot, loads, cols=SLOT):
                act.wait_ge(w_loaded[slot], loads)
                act.wait_ge(w_used, c - 1)
                act.activation(w_hi[:, slot, 0:cols], stage[:, slot, 0:cols], ACT.Copy).then_inc(w_hi_made, 1)

            def split_static(c, cols=SLOT):
                if c < CHUNKS:
                    act.wait_ge(w_loaded[c % 2], 32 * (c // 2 + 1))
                    if c >= 2:
                        act.wait_ge(w_used, c - 1)
                    act.activation(w_hi[:, c % 2, 0:cols], stage[:, c % 2, 0:cols], ACT.Copy).then_inc(w_hi_made, 1)

            def x_tile(n, j, ready):
                act.wait_ge(x_ready, ready)
                act.activation(xg_hi[:, bass.ds(j, 1), :].rearrange("p a s -> p (a s)"),
                               x_res[:, bass.ds(j, 1), :].rearrange("p a s -> p (a s)"), ACT.Copy,
                               scale=params[:, bass.ds(j + GAIN_ROW[n], 1)]).then_inc(xg_hi_made, 1)

            def token_rms(n):
                act.wait_ge(ssq_summed, n + 1)
                act.activation(rms[:, :], ps[:, 6, :], ACT.Sqrt, bias=eps_col[:, 0:1], scale=1.0 / D).then_inc(rms_made, 1)

            def token_rms_tok(n):
                act.wait_ge(tok_summed, n)
                act.activation(tok_rms[:, :], ps[:, 7, 0:TT], ACT.Sqrt, bias=eps_col[:, 0:1],
                               scale=1.0 / D).then_inc(tok_rms_made, 1)

            def hidden(f, count, s):
                act.wait_ge(gate_scaled, count)
                act.activation(gate[:, s, :], gate[:, s, :], ACT.Silu).then_inc(silu_made, 1)
                act.wait_ge(gated, count)
                act.activation(hid_hi[:, bass.ds(f, 1), :].rearrange("p a s -> p (a s)"), up[:, s, :],
                               ACT.Copy).then_inc(hid_hi_made, 1)

            def ffn(n):
                c0, f0, norm = C_FFN[n], n * FT, NORM_FFN[n]
                half0 = c0 // 2
                split_static(c0 + 1)
                token_rms(norm)
                hidden(0, f0 + 1, 0)
                split_static(c0 + 2)
                hidden(1, f0 + 2, 1)
                with act.Fori(1, FT // 2 - 1) as i:
                    for s in range(2):
                        o = 1 - s
                        split_hi(2 * i + (c0 + s + 1), o, 32 * i + 32 * (half0 + s + 1))
                        hidden(2 * i + s, 2 * i + (f0 + s + 1), s)
                split_static(c0 + FT - 1)
                hidden(FT - 2, f0 + FT - 1, 0)
                split_static(c0 + FT, HK * P)
                hidden(FT - 1, f0 + FT, 1)
                last = n == 3
                with act.Fori(0, DT - 1) as j:
                    split_hi(2 * j + (c0 + FT + 1), 1, 32 * j + 32 * (half0 + HK + 1), HK * P)
                    split_hi(2 * j + (c0 + FT + 2), 0, 32 * j + 32 * (half0 + HK + 2), HK * P)
                    if last:
                        final_tile(j, j + (NORM_FINAL * DT + 1))
                    else:
                        x_tile(norm + 1, j, j + ((norm + 1) * DT + 1))
                split_static(c0 + FT + 2 * DT - 1, HK * P)
                split_static(c0 + FT + 2 * DT)
                if last:
                    final_tile(DT - 1, (NORM_FINAL + 1) * DT)
                else:
                    x_tile(norm + 1, DT - 1, (norm + 2) * DT)

            def final_tile(j, ready):
                act.wait_ge(ssq_added, ready)
                act.activation(x_res[:, bass.ds(j, 1), :].rearrange("p a s -> p (a s)"),
                               x_res[:, bass.ds(j, 1), :].rearrange("p a s -> p (a s)"), ACT.Copy,
                               scale=params[:, bass.ds(j + GAIN_ROW[NORM_FINAL], 1)]).then_inc(y_fin_made, 1)

            row = 0
            for vec in param_vectors:
                rows = vec.shape[0] * vec.shape[1] // P
                act.dma_start(param_rows[row:row + rows, :], vec.rearrange("a (j p) -> (a j) p", p=P)).then_inc(params_loaded, 16)
                row += rows
            act.dma_start(conv_rows[:, :], conv_w[0].rearrange("k (c p) -> (k c) p", p=P)).then_inc(params_loaded, 16)
            act.wait_ge(consts_made, 2)
            act.wait_ge(turned_out, 1)
            for j in range(DT):
                x_tile(0, j, j + 1)
            split_static(0)
            ffn(0)

            c0 = C_CONV
            for i in range(CT):
                split_static(c0 + i + 1)
                if i == 0:
                    token_rms(NORM_CONV)
                    token_rms_tok(1)
                act.wait_ge(a_gate_scaled, i + 1)
                act.activation(g_buf[:, 0, :], g_buf[:, 0, :], ACT.Sigmoid).then_inc(a_sigmoid, 1)
                if i == 1:
                    act.activation(taps_hi[:, :], taps[:, PE_TILE:TAPS * CT:CT], ACT.Copy).then_inc(taps_hi_made, 1)
            act.wait_ge(a_made, 1)
            act.activation(a_pad_hi[:, :], a_pad[:, PE_TILE, :], ACT.Copy).then_inc(a_pad_hi_made, 1)
            split_static(c0 + 5)
            split_static(c0 + 6)
            act.wait_ge(taps_summed, 1)
            act.activation(y[:, PE_TILE, :], ps[:, 1, :], ACT.Identity,
                           bias=params[:, ROW_CONV_B + PE_TILE:ROW_CONV_B + PE_TILE + 1]).then_inc(taps_copied, 1)
            split_static(c0 + 7)
            for t in range(TT):
                act.wait_ge(v_centred, t + 1)
                act.activation(u[:, t, :], v_cen[:, t].rearrange("p g c -> p (g c)"), ACT.Square).then_inc(v_squared, 1)
            act.wait_ge(v_stat_made, 1)
            act.activation(v_stat[:, :, :], v_stat[:, :, :], ACT.Sqrt, bias=eps_col[:, 0:1], scale=1.0 / P).then_inc(v_std_made, 1)
            act.wait_ge(v_rstd_made, 1)
            for t in range(TT):
                for g in range(GB):
                    ins = act.activation(v_cen[:, t, g, :], v_cen[:, t, g, :], ACT.Copy, scale=v_rstd[:, t, g:g + 1])
                ins.then_inc(v_scaled, 1)
            split_static(c0 + 8)
            for t in range(TT):
                act.wait_ge(v_normed, t + 1)
                act.activation(v_n_hi[:, t, :], v_cen[:, t].rearrange("p g c -> p (g c)"), ACT.Copy).then_inc(v_n_hi_made, 1)
            split_static(c0 + 9)
            for g in range(GB):
                act.wait_ge(b_made, g + 1)
                act.activation(ab_hi[:, CT + g, :], u[:, g, :], ACT.Copy).then_inc(b_hi_made, 1)
            for i in range(CT):
                act.wait_ge(y_centred, i + 1)
                act.activation(v_cen[:, i].rearrange("p g c -> p (g c)"), y[:, i, :], ACT.Square).then_inc(y_squared, 1)
            split_static(c0 + 10)
            act.wait_ge(y_var_sum, 1)
            act.activation(rms[:, :], ps[:, 7, :], ACT.Sqrt, bias=eps_col[:, 0:1], scale=1.0 / CA).then_inc(y_std_made, 1)
            for i in range(CT):
                act.wait_ge(y_normed, i + 1)
                act.activation(y[:, i, :], y[:, i, :], ACT.Silu, scale=params[:, ROW_LN_G + i:ROW_LN_G + i + 1],
                               bias=params[:, ROW_LN_B + i:ROW_LN_B + i + 1]).then_inc(a_silu, 1)
                act.wait_ge(a_silu, i + 1)
                act.activation(ab_hi[:, i, :], y[:, i, :], ACT.Copy).then_inc(a_hi_made, 1)
            split_static(c0 + 11)
            for j in range(4):
                x_tile(2, j, 2 * DT + j + 1)
            split_static(c0 + 12)
            for j in range(4, DT):
                x_tile(2, j, 2 * DT + j + 1)
            ffn(1)
            ffn(2)

            c0 = C_ATT
            for n in range(4):
                split_static(c0 + n + 1)
                if n == 0:
                    token_rms(NORM_ATT)
                    token_rms_tok(2)
                if n % 2:
                    half = n // 2
                    act.wait_ge(tok_rinv_made, 2)
                    act.wait_ge(w_used, c0 + n + 1)
                    for t in range(TT):
                        act.activation(v_hi[:, t, half * 512:(half + 1) * 512], ps[:, 4 * half + t, :], ACT.Copy,
                                       scale=tok_rinv[:, t:t + 1]).then_inc(v_hi_made, 1)

            def split_proj(n):
                act.wait_ge(proj_scaled, n + 1)
                act.activation(qk_hi[:, (n // 2) % 2, n % 2, :], qk_f[:, :], ACT.Copy).then_inc(proj_hi_made, 1)

            def zall(h):
                at = 3 * (h % 2) * 512
                return ps[:, :, :].rearrange("p a c -> p (a c)")[:, at:at + SCORES]

            def split_out(j):
                act.wait_ge(o_copied, 2 * j + 2)
                act.activation(v_hi[:, :, j * P:(j + 1) * P], o_att[:, j, :].rearrange("p (t c) -> p t c", t=TT),
                               ACT.Copy).then_inc(o_hi_made, 1)

            act.add_instruction(mybir.InstLoadActFuncSet(
                name=nc.get_next_instruction_name(), engine=mybir.EngineType.Activation, act_func_set_id=EXP_LN_SET))
            split_proj(0)
            split_proj(1)
            split_static(c0 + 5)
            split_static(c0 + 6)
            for h in range(HEADS + 2):
                if h < HEADS:
                    act.wait_ge(scores_summed, h + 1)
                    if h >= 1:
                        act.wait_ge(keep_lo_made, h)
                    step(act.activation(keep[:, :], zall(h), ACT.Abs))
                    step(act.activation(keep[:, :], keep[:, :], ACT.Exp, scale=-1.0))
                    act.activation(keep[:, :], keep[:, :], ACT.Ln, bias=1.0).then_inc(log1p_made, 1)
                if 1 <= h <= HEADS:
                    act.wait_ge(suffix_summed, h)
                    if h >= 2:
                        act.wait_ge(prob_lo_made, h - 1)
                    act.activation(prob[:, :], zall(h - 1), ACT.Exp).then_inc(prob_made, 1)
                if h + 2 < HEADS:
                    split_proj(h + 2)
                if h >= 2:
                    act.wait_ge(att_summed, h - 1)
                    r = slice(DH * (h % 2), DH * (h % 2) + DH)
                    act.activation(o_att[r, (h - 2) // 2, :], ps[r, 7, :], ACT.Copy).then_inc(o_copied, 1)
                if h >= 3 and h % 2:
                    split_out((h - 3) // 2)
                if h % 2 and h <= 13:
                    split_static(c0 + 6 + (h + 1) // 2)
                elif h == 15:
                    split_static(c0 + 14)
            for j in range(DT):
                if j % 4 == 0:
                    split_static(c0 + 15 + j // 4)
                x_tile(5, j, 5 * DT + j + 1)
            ffn(3)
            token_rms_tok(3)
            for n in range(1, 8, 2):
                act.wait_ge(tok_rinv_made, 3)
                act.wait_ge(fin_turned, n + 1)
                t, half = n // 2, n % 2
                act.wait_ge(fin_scaled, n)
                act.activation(out_tok[:, t, half * 512:(half + 1) * 512], ps[:, [0, 1, 2, 3, 4, 5, 6, 0][n], :], ACT.Copy,
                               scale=tok_rinv[:, t:t + 1]).then_inc(fin_scaled, 1)

        @block.vector
        def _(dve):
            steps = [0]

            def step(ins):
                steps[0] += 1
                ins.then_inc(dve_step, 1)
                dve.wait_ge(dve_step, steps[0])
                return ins

            def split_lo(c, slot, cols=SLOT):
                dve.wait_ge(w_hi_made, c + 1)
                dve.tensor_tensor(w_lo[:, slot, 0:cols], stage[:, slot, 0:cols],
                                  w_hi[:, slot, 0:cols].bitcast(F32), ALU.subtract).then_inc(w_lo_made, 1)

            def split_static(c, cols=SLOT):
                if c < CHUNKS:
                    split_lo(c, c % 2, cols)

            def x_low(n, j, made):
                dve.wait_ge(xg_hi_made, made)
                dve.scalar_tensor_tensor(xg_lo[:, bass.ds(j, 1), :].rearrange("p a s -> p (a s)"),
                                         x_res[:, bass.ds(j, 1), :].rearrange("p a s -> p (a s)"),
                                         params[:, bass.ds(j + GAIN_ROW[n], 1)],
                                         xg_hi[:, bass.ds(j, 1), :].rearrange("p a s -> p (a s)").bitcast(F32),
                                         ALU.mult, ALU.subtract).then_inc(xg_lo_made, 1)

            def add_to_x(j, bank, factor, done):
                xj = x_res[:, bass.ds(j, 1), :].rearrange("p a s -> p (a s)")
                dve.scalar_tensor_tensor(xj, ps[:, bank, :], factor, xj, ALU.mult, ALU.add).then_inc(done, 1)

            def invert_rms(n):
                dve.wait_ge(rms_made, n + 1)
                dve.reciprocal(rinv[:, :], rms[:, :]).then_inc(rinv_made, 1)
                dve.wait_ge(rinv_made, n + 1)

            def invert_rms_tok(n):
                dve.wait_ge(tok_rms_made, n)
                dve.reciprocal(tok_rinv[:, :], tok_rms[:, :]).then_inc(tok_rinv_made, 1)
                dve.wait_ge(tok_rinv_made, n)

            def hidden(c_used, count, prev, s):
                dve.wait_ge(w_used, c_used)
                if prev is not None:
                    dve.wait_ge(hid_lo_made, prev)
                dve.tensor_tensor(gate[:, s, :], ps[:, 2 * s, :], rinv[:, :], ALU.mult).then_inc(gate_scaled, 1)
                dve.tensor_tensor(up[:, s, :], ps[:, 2 * s + 1, :], rinv[:, :], ALU.mult).then_inc(up_scaled, 1)
                dve.wait_ge(silu_made, count)
                dve.wait_ge(up_scaled, count)
                dve.tensor_tensor(up[:, s, :], gate[:, s, :], up[:, s, :], ALU.mult).then_inc(gated, 1)

            def ffn(n):
                c0, f0, norm = C_FFN[n], n * FT, NORM_FFN[n]
                split_static(c0 + 1)
                invert_rms(norm)
                hidden(c0 + 1, f0 + 1, None, 0)
                split_static(c0 + 2)
                hidden(c0 + 2, f0 + 2, None, 1)
                with dve.Fori(1, FT // 2 - 1) as i:
                    for s in range(2):
                        split_lo(2 * i + (c0 + s + 1), 1 - s)
                        hidden(2 * i + (c0 + s + 1), 2 * i + (f0 + s + 1), 2 * i + (f0 + s - 1), s)
                split_static(c0 + FT - 1)
                hidden(c0 + FT - 1, f0 + FT - 1, f0 + FT - 3, 0)
                split_static(c0 + FT, HK * P)
                hidden(c0 + FT, f0 + FT, f0 + FT - 2, 1)
                last = n == 3
                a = (norm + 1) * DT

                def down(j, q, next_cols):
                    split_lo(2 * j + (c0 + FT + 1), 1, HK * P)
                    if next_cols is not None:
                        split_lo(2 * j + (c0 + FT + 2), 0, next_cols)
                    dve.wait_ge(w_used, 2 * j + (c0 + FT + 2))
                    add_to_x(j, 4 + q, 0.5, x_ready)
                    if not last:
                        x_low(norm + 1, j, j + (a + 1))

                with dve.Fori(0, DT // 2 - 1) as i:
                    for q in range(2):
                        down(2 * i + q, q, HK * P)
                down(DT - 2, 0, HK * P)
                down(DT - 1, 1, SLOT if not last else None)

            dve.wait_ge(turned, 1)
            dve.tensor_copy(params[:, :], ps[:, 7, 0:PARAM_ROWS])
            dve.tensor_copy(taps[:, :], ps[:, 7, P:P + TAPS * CT]).then_inc(turned_out, 1)
            dve.wait_ge(turned_out, 1)
            for j in range(DT):
                dve.wait_ge(turned, j + 2)
                dve.tensor_copy(x_res[:, j, :], ps[:, j, :]).then_inc(x_ready, 1)
                if j:
                    x_low(0, j - 1, j)
            x_low(0, DT - 1, DT)
            split_static(0)
            ffn(0)

            c0 = C_CONV
            taken = [0] * (CT - 1)
            last = [0] * CT

            def convolve(n, *tiles):
                for _ in range(n):
                    i = min((i for i in tiles if taken[i] < TAPS), key=lambda i: taken[i])
                    k = taken[i]
                    seen, yi = a_pad[:, i, k:k + S], y[:, i, :]
                    w = taps[:, k * CT + i:k * CT + i + 1]
                    if k:
                        dve.wait_ge(dve_step, last[i])
                        ins = dve.scalar_tensor_tensor(yi, seen, w, yi, ALU.mult, ALU.add)
                    else:
                        ins = dve.tensor_scalar(yi, seen, w, params[:, ROW_CONV_B + i:ROW_CONV_B + i + 1],
                                                ALU.mult, ALU.add)
                    taken[i] += 1
                    if taken[i] == TAPS:
                        ins.then_inc(conv_made, 1)
                    else:
                        steps[0] += 1
                        last[i] = steps[0]
                        ins.then_inc(dve_step, 1)

            def gate_pair(i):
                dve.wait_ge(w_used, c0 + i + 1)
                dve.tensor_tensor(g_buf[:, 0, :], ps[:, 2 * (i % 2) + 1, :], rinv[:, :], ALU.mult).then_inc(a_gate_scaled, 1)
                dve.tensor_tensor(g_buf[:, 1, :], ps[:, 2 * (i % 2), :], rinv[:, :], ALU.mult).then_inc(a_val_scaled, 1)
                dve.wait_ge(a_val_scaled, i + 1)
                dve.wait_ge(a_sigmoid, i + 1)
                ins = dve.tensor_tensor(a_pad[:, i, PAD:PAD + S], g_buf[:, 0, :], g_buf[:, 1, :], ALU.mult)
                if i == PE_TILE:
                    ins.then_inc(a_made, 1)
                else:
                    step(ins)

            def scale_u(g):
                dve.tensor_tensor(u[:, g, :], ps[:, g, :], rinv[:, :], ALU.mult).then_inc(u_scaled, 1)

            split_static(c0 + 1)
            step(dve.memset(a_pad[:, :, 0:PAD], 0.0))
            invert_rms(NORM_CONV)
            invert_rms_tok(1)
            step(dve.tensor_tensor(rinv2[:, :], tok_rinv[:, :], tok_rinv[:, :], ALU.mult))
            gate_pair(0)
            split_static(c0 + 2)
            convolve(TAPS_AT[0], 0)
            gate_pair(1)
            split_static(c0 + 3)
            dve.wait_ge(taps_hi_made, 1)
            dve.tensor_tensor(taps_lo[:, :], taps[:, PE_TILE:TAPS * CT:CT], taps_hi[:, :].bitcast(F32),
                              ALU.subtract).then_inc(taps_lo_made, 1)
            convolve(TAPS_AT[1], 0, 1)
            gate_pair(2)
            split_static(c0 + 4)
            convolve(TAPS_AT[2], 0, 1, 2)
            gate_pair(3)
            dve.wait_ge(turned, DT + 2)
            dve.tensor_copy(sp_rows[:, :, :], ps[:, 0, :].rearrange("p (g t) -> p g t", g=GB)).then_inc(turned_out, 1)
            dve.wait_ge(a_pad_hi_made, 1)
            dve.tensor_tensor(a_pad_lo[:, :], a_pad[:, PE_TILE, :], a_pad_hi[:, :].bitcast(F32),
                              ALU.subtract).then_inc(a_pad_lo_made, 1)
            split_static(c0 + 5)
            convolve(TAPS_AT[3], 0, 1, 2)
            split_static(c0 + 6)
            convolve(TAPS_AT[4], 0, 1, 2)
            dve.wait_ge(w_used, c0 + 6)
            for t in range(TT):
                raw = ps[:, 4 + t, :].rearrange("p (g c) -> p g c", g=GB)
                step(dve.tensor_reduce(v_mean[:, t, :], raw, AX.X, ALU.add))
                dve.scalar_tensor_tensor(v_cen[:, t], v_mean[:, t, :].unsqueeze(2).to_broadcast([P, GB, P]), -1.0 / P,
                                         raw, ALU.mult, ALU.add).then_inc(v_centred, 1)
            split_static(c0 + 7)
            for t in range(TT):
                dve.wait_ge(v_squared, t + 1)
                ins = dve.tensor_reduce(v_stat[:, t, :], u[:, t, :].rearrange("p (g c) -> p g c", g=GB), AX.X, ALU.add)
            step(ins)
            dve.tensor_tensor(v_stat[:, :, :], v_stat[:, :, :], rinv2[:, :].unsqueeze(2).to_broadcast([P, TT, GB]),
                              ALU.mult).then_inc(v_stat_made, 1)
            convolve(TAPS_AT[5], 0, 1, 2)
            dve.wait_ge(v_std_made, 1)
            step(dve.reciprocal(v_rstd[:, :, :], v_stat[:, :, :]))
            dve.tensor_tensor(v_rstd[:, :, :], v_rstd[:, :, :], tok_rinv[:, :].unsqueeze(2).to_broadcast([P, TT, GB]),
                              ALU.mult).then_inc(v_rstd_made, 1)
            dve.wait_ge(w_used, c0 + 7)
            scale_u(0)
            scale_u(1)
            convolve(TAPS_AT[6], 0, 1, 2)
            split_static(c0 + 8)
            for t in range(TT):
                convolve(TAPS_AT[7], 0, 1, 2)
                dve.wait_ge(v_n_hi_made, t + 1)
                dve.tensor_tensor(v_n_lo[:, t, :], v_cen[:, t].rearrange("p g c -> p (g c)"),
                                  v_n_hi[:, t, :].bitcast(F32), ALU.subtract).then_inc(v_n_lo_made, 1)
            dve.wait_ge(w_used, c0 + 8)
            scale_u(2)
            scale_u(3)
            convolve(TAPS * PE_TILE - sum(taken), 0, 1, 2)
            split_static(c0 + 9)
            dve.wait_ge(taps_summed, 2)
            dve.wait_ge(taps_copied, 1)
            dve.tensor_tensor(y[:, PE_TILE, :], ps[:, 7, :], y[:, PE_TILE, :], ALU.add).then_inc(late_added, 1)
            dve.wait_ge(u_scaled, GB)
            for g in range(GB):
                dve.wait_ge(mixed, g + 1)
                step(dve.tensor_tensor(v_cen[:, g].rearrange("p g c -> p (g c)").rearrange("p (t c) -> p t c", t=TT),
                                       ps[:, 4 + g, :].rearrange("p (t c) -> p t c", t=TT),
                                       sp_bias[:, g, :].unsqueeze(1).to_broadcast([P, TT, P]), ALU.add))
                dve.tensor_tensor(u[:, g, :], u[:, g, :], v_cen[:, g].rearrange("p g c -> p (g c)"),
                                  ALU.mult).then_inc(b_made, 1)
            dve.wait_ge(y_mean_sum, 1)
            for i in range(CT):
                dve.scalar_tensor_tensor(y[:, i, :], ps[:, 6, :], -1.0 / CA, y[:, i, :], ALU.mult,
                                         ALU.add).then_inc(y_centred, 1)
            split_static(c0 + 10)
            dve.wait_ge(y_std_made, 1)
            step(dve.reciprocal(g_buf[:, 1, :], rms[:, :]))
            for i in range(CT):
                dve.wait_ge(y_squared, CT)
                dve.tensor_tensor(y[:, i, :], y[:, i, :], g_buf[:, 1, :], ALU.mult).then_inc(y_normed, 1)
            for i in range(CT):
                dve.wait_ge(a_hi_made, i + 1)
                dve.tensor_tensor(ab_lo[:, i, :], y[:, i, :], ab_hi[:, i, :].bitcast(F32), ALU.subtract).then_inc(a_lo_made, 1)
            split_static(c0 + 11)
            for j in range(DT):
                if j == 4:
                    split_static(c0 + 12)
                if j % 4 == 3:
                    dve.wait_ge(w_used, c0 + 11 + j // 4)
                else:
                    dve.wait_ge(mix_summed, j + 1 - j // 4)
                add_to_x(j, j, 1.0, x_ready)
                x_low(2, j, 2 * DT + j + 1)
            ffn(1)
            ffn(2)

            c0 = C_ATT
            for n in range(4):
                split_static(c0 + n + 1)
                if n == 0:
                    invert_rms(NORM_ATT)
                    invert_rms_tok(2)
                if n % 2:
                    half = n // 2
                    for t in range(TT):
                        dve.wait_ge(v_hi_made, 4 * half + t + 1)
                        cols = slice(half * 512, (half + 1) * 512)
                        dve.scalar_tensor_tensor(v_lo[:, t, cols], ps[:, 4 * half + t, :], tok_rinv[:, t:t + 1],
                                                 v_hi[:, t, cols].bitcast(F32), ALU.mult,
                                                 ALU.subtract).then_inc(v_lo_made, 1)

            def scale_proj(n):
                if n % 2:
                    dve.wait_ge(w_used, c0 + 5 + n // 2)
                else:
                    dve.wait_ge(proj_summed, n // 2 + 1)
                dve.scalar_tensor_tensor(qk_f[:, :], ps[:, 6, :], 1.0 if n % 2 else DH ** -0.5, rinv[:, :],
                                         ALU.mult, ALU.mult).then_inc(proj_scaled, 1)

            def proj_low(n):
                dve.wait_ge(proj_scaled, n + 1)
                dve.wait_ge(proj_hi_made, n + 1)
                dve.tensor_tensor(qk_lo[:, (n // 2) % 2, n % 2, :], qk_f[:, :],
                                  qk_hi[:, (n // 2) % 2, n % 2, :].bitcast(F32), ALU.subtract).then_inc(proj_lo_made, 1)
                dve.wait_ge(proj_lo_made, n + 1)

            def zall(h):
                at = 3 * (h % 2) * 512
                return ps[:, :, :].rearrange("p a c -> p (a c)")[:, at:at + SCORES]

            def split_out(j):
                dve.wait_ge(o_hi_made, j + 1)
                cols = slice(j * P, (j + 1) * P)
                dve.tensor_tensor(v_lo[:, :, cols], o_att[:, j, :].rearrange("p (t c) -> p t c", t=TT),
                                  v_hi[:, :, cols].bitcast(F32), ALU.subtract).then_inc(o_lo_made, 1)

            def add_part(q):
                if q % 4 == 3:
                    dve.wait_ge(w_used, c0 + 13 + q // 4)
                else:
                    dve.wait_ge(o_part_summed, q + 1 - q // 4)
                add_to_x(q, 6, 1.0, x_added)

            for n in range(2):
                scale_proj(n)
                proj_low(n)
            split_static(c0 + 5)
            for h in range(HEADS + 2):
                if h + 2 < HEADS:
                    scale_proj(h + 2)
                if h >= 14:
                    add_part(2 * (h - 14) + 1)
                if h % 2 == 0 and h <= 14:
                    split_static(c0 + 6 + h // 2)
                elif h == 16:
                    split_static(c0 + 14)
                if h < HEADS:
                    dve.wait_ge(log1p_made, h + 1)
                    dve.scalar_tensor_tensor(keep[:, :], zall(h), 0.0, keep[:, :], ALU.max, ALU.add).then_inc(keep_made, 1)
                    if h + 2 < HEADS:
                        proj_low(h + 2)
                if 13 <= h < 17:
                    add_part(2 * (h - 13))
                if h < HEADS:
                    dve.wait_ge(keep_masked, h + 1)
                    if h >= 1:
                        dve.wait_ge(suffix_summed, h)
                    dve.tensor_copy(keep_hi[:, :], keep[:, :]).then_inc(keep_hi_made, 1)
                    dve.wait_ge(keep_hi_made, h + 1)
                    dve.tensor_tensor(keep_lo[:, :], keep[:, :], keep_hi[:, :].bitcast(F32),
                                      ALU.subtract).then_inc(keep_lo_made, 1)
                if 1 <= h <= HEADS:
                    dve.wait_ge(prob_masked, h)
                    if h >= 2:
                        dve.wait_ge(att_summed, h - 1)
                    dve.tensor_copy(prob_hi[:, :], prob[:, :]).then_inc(prob_hi_made, 1)
                    dve.wait_ge(prob_hi_made, h)
                    dve.tensor_tensor(prob_lo[:, :], prob[:, :], prob_hi[:, :].bitcast(F32),
                                      ALU.subtract).then_inc(prob_lo_made, 1)
                if h >= 3 and h % 2:
                    split_out((h - 3) // 2)
            for j in range(DT):
                if j % 4 == 0:
                    split_static(c0 + 15 + j // 4)
                if j == 0:
                    dve.wait_ge(x_added, DT)
                if j % 4 == 3:
                    dve.wait_ge(w_used, c0 + 15 + j // 4)
                else:
                    dve.wait_ge(o_half_summed, j + 1 - j // 4)
                add_to_x(j, 4 + j % 4, 1.0, x_ready)
                x_low(5, j, 5 * DT + j + 1)
            ffn(3)
            invert_rms_tok(3)
            for n in range(0, 8, 2):
                dve.wait_ge(fin_turned, n + 1)
                t, half = n // 2, n % 2
                if n:
                    dve.wait_ge(fin_scaled, n)
                dve.tensor_scalar(out_tok[:, t, half * 512:(half + 1) * 512], ps[:, [0, 1, 2, 3, 4, 5, 6, 0][n], :],
                                  tok_rinv[:, t:t + 1], None, ALU.mult).then_inc(fin_scaled, 1)

        @block.gpsimd
        def _(pool):
            steps = [0]

            def step(ins):
                steps[0] += 1
                ins.then_inc(pool_step, 1)
                pool.wait_ge(pool_step, steps[0])

            def clear_ssq(n):
                if n:
                    if n - 1 in (NORM_CONV, NORM_ATT):
                        pool.wait_ge(tok_summed, 1 if n - 1 == NORM_CONV else 2)
                    pool.wait_ge(ssq_summed, n)
                pool.memset(ssq[:, :], 0.0).then_inc(ssq_cleared, 1)
                pool.wait_ge(ssq_cleared, n + 1)

            def square_tile(j, count):
                pool.wait_ge(x_ready, count)
                xj = x_res[:, bass.ds(j, 1), :].rearrange("p a s -> p (a s)")
                pool.tensor_tensor(sq[:, :], xj, xj, ALU.mult).then_inc(sq_made, 1)
                pool.wait_ge(sq_made, count)
                pool.tensor_tensor(ssq[:, :], ssq[:, :], sq[:, :], ALU.add).then_inc(ssq_added, 1)
                pool.wait_ge(ssq_added, count)

            def ffn(n):
                f0, norm = n * FT, NORM_FFN[n]
                with pool.Fori(0, FT // 2) as i:
                    for s in range(2):
                        pool.wait_ge(hid_hi_made, 2 * i + (f0 + s + 1))
                        pool.tensor_tensor(hid_lo[:, bass.ds(2 * i + s, 1), :].rearrange("p a s -> p (a s)"),
                                           up[:, s, :], hid_hi[:, bass.ds(2 * i + s, 1), :].rearrange(
                                               "p a s -> p (a s)").bitcast(F32), ALU.subtract).then_inc(hid_lo_made, 1)
                clear_ssq(norm + 1)
                with pool.Fori(0, DT) as j:
                    square_tile(j, j + ((norm + 1) * DT + 1))

            def mask_diagonals(of, compare, count_sem):
                for b in range(TT):
                    at = KEY_OFF[b]
                    ins = pool.affine_select(out=of[:, at:at + P], in_=of[:, at:at + P], compare_op=compare, fill=0.0,
                                             base=0, pattern=[[1, P]], channel_multiplier=-1)
                ins.then_inc(count_sem, 1)

            step(pool.memset(ident[:, :], 0.0))
            pool.affine_select(out=ident[:, :], in_=ident[:, :], compare_op=ALU.not_equal, fill=1.0, base=0,
                               pattern=[[-1, P]], channel_multiplier=1).then_inc(consts_made, 1)
            pool.memset(ones[:, :], 1.0)
            pool.memset(eps_col[:, :], EPS)
            step(pool.memset(neg_ones[:, :].bitcast(F32), -1.0))
            pool.affine_select(out=neg_tri[:, :], in_=neg_ones[:, :].bitcast(F32), compare_op=ALU.is_ge, fill=0.0, base=0,
                               pattern=[[-1, P]], channel_multiplier=1).then_inc(consts_made, 1)
            clear_ssq(0)
            for j in range(DT):
                square_tile(j, j + 1)
            ffn(0)

            pool.wait_ge(taps_lo_made, 1)
            for diags, k0 in ((diags_early, 0), (diags_late, EARLY)):
                for diag, part in zip(diags, (taps_hi, taps_lo)):
                    n = diag.shape[1]
                    pool.affine_select(out=diag[:, :, :], in_=part[:, k0:k0 + n].unsqueeze(2).to_broadcast([P, n, P]),
                                       compare_op=ALU.is_equal, fill=0.0, base=0, pattern=[[0, n], [-1, P]],
                                       channel_multiplier=1).then_inc(diags_made, 1)
            pool.wait_ge(turned_out, 2)
            for g in range(GB):
                ins = pool.affine_select(out=sp_rows[:, g, :], in_=sp_rows[:, g, :], compare_op=ALU.is_ge, fill=0.0, base=0,
                                         pattern=[[1, P]], channel_multiplier=-1)
            step(ins)
            step(pool.tensor_copy(sp_hi[:, :, :], sp_rows[:, :, :]))
            pool.tensor_tensor(sp_lo[:, :, :], sp_rows[:, :, :], sp_hi[:, :, :].bitcast(F32), ALU.subtract).then_inc(sp_ready, 1)
            for t in range(TT):
                pool.wait_ge(v_scaled, t + 1)
                if t == 0:
                    pool.wait_ge(mixer_params, 16 * 4)
                vt = v_cen[:, t].rearrange("p g c -> p (g c)")
                step(pool.tensor_tensor(vt, vt, lnv_g[:, :], ALU.mult))
                pool.tensor_tensor(vt, vt, lnv_b[:, :], ALU.add).then_inc(v_normed, 1)
            pool.wait_ge(conv_made, 2)
            step(pool.tensor_tensor(sq[:, :], y[:, 0, :], y[:, 1, :], ALU.add))
            pool.wait_ge(conv_made, 3)
            step(pool.tensor_tensor(sq[:, :], sq[:, :], y[:, 2, :], ALU.add))
            for g in range(GB):
                pool.wait_ge(b_hi_made, g + 1)
                pool.tensor_tensor(ab_lo[:, CT + g, :], u[:, g, :], ab_hi[:, CT + g, :].bitcast(F32),
                                   ALU.subtract).then_inc(b_lo_made, 1)
            pool.wait_ge(late_added, 1)
            pool.tensor_tensor(sq[:, :], sq[:, :], y[:, PE_TILE, :], ALU.add).then_inc(ysum_made, 1)
            ysq = [v_cen[:, i].rearrange("p g c -> p (g c)") for i in range(CT)]
            pool.wait_ge(y_squared, 2)
            step(pool.tensor_tensor(sq[:, :], ysq[0], ysq[1], ALU.add))
            pool.wait_ge(y_squared, 3)
            step(pool.tensor_tensor(sq[:, :], sq[:, :], ysq[2], ALU.add))
            pool.wait_ge(y_squared, 4)
            pool.tensor_tensor(sq[:, :], sq[:, :], ysq[3], ALU.add).then_inc(ysq_sum_made, 1)
            clear_ssq(2)
            for j in range(DT):
                square_tile(j, 2 * DT + j + 1)
            ffn(1)
            ffn(2)

            for h in range(HEADS + 1):
                if h < HEADS:
                    pool.wait_ge(keep_made, h + 1)
                    mask_diagonals(keep, ALU.is_gt, keep_masked)
                if h >= 1:
                    pool.wait_ge(prob_made, h)
                    mask_diagonals(prob, ALU.is_gt, prob_masked)
            clear_ssq(5)
            for j in range(DT):
                square_tile(j, 5 * DT + j + 1)
            ffn(3)


_INS = ["x", "g_ffn1", "w_ffn1_gate", "w_ffn1_up", "w_ffn1_down", "g_mix", "w_in_ab", "conv_w", "conv_b", "ln_a_g",
        "ln_a_b", "ln_v_g", "ln_v_b", "sp_w", "sp_b", "w_out_ab", "w_qkv", "w_o", "g_ffn2", "w_ffn2_gate",
        "w_ffn2_up", "w_ffn2_down", "g_final"]
_OUT = ((1, S, D), "float32")


def kernel(**inputs):
    import numpy as _np
    import concourse.bacc as _bacc
    from concourse import mybir as _mybir
    from concourse.bass_utils import run_bass_kernel_spmd as _run

    nc = _bacc.Bacc("TRN2", target_bir_lowering=False, num_devices=1)
    arrays, args = {}, []
    for name in _INS:
        a = _np.ascontiguousarray(inputs[name])
        arrays[f"in_{name}_dram"] = a
        args.append(nc.dram_tensor(f"in_{name}_dram", a.shape, _mybir.dt.from_np(a.dtype), kind="ExternalInput").ap())
    shape, dtype = _OUT
    args.append(nc.dram_tensor("out_0_dram", shape, _mybir.dt.from_np(_np.dtype(dtype)), kind="ExternalOutput").ap())
    trunk_kernel(nc, *args)
    r = _run(nc, [arrays], core_ids=[0])
    return r.results[0]["out_0_dram"]
```

```python
from contextlib import ExitStack

import concourse.bass as bass
from concourse import mybir

F32 = mybir.dt.float32
F32R = mybir.dt.float32r
ALU = mybir.AluOpType
ACT = mybir.ActivationFunctionType
AX = mybir.AxisListType

P = 128
S = 512
D = 1024
DT = D // P
TT = S // P
FF = 2816
FT = FF // P
HK = FT // 2
CA = 512
CT = CA // P
TAPS = 31
PAD = TAPS - 1
GB = 4
HEADS = 16
DH = 64
EPS = 1e-6
SLOT = 16 * P

FFN_CHUNKS = FT + 2 * DT
CONV_CHUNKS = 12
ATT_CHUNKS = 16
C_FFN = [0, FFN_CHUNKS + CONV_CHUNKS, 2 * FFN_CHUNKS + CONV_CHUNKS,
         3 * FFN_CHUNKS + CONV_CHUNKS + ATT_CHUNKS]
C_CONV = FFN_CHUNKS
C_ATT = 3 * FFN_CHUNKS + CONV_CHUNKS
CHUNKS = 4 * FFN_CHUNKS + CONV_CHUNKS + ATT_CHUNKS
NORM_FFN = [0, 2, 3, 5]
NORM_CONV, NORM_ATT, NORM_FINAL = 1, 4, 6
GAIN_ROW = [0, 2 * DT, 4 * DT, DT, 3 * DT, 5 * DT, 6 * DT]
ROW_LN_G, ROW_LN_B, ROW_CONV_B = 7 * DT, 7 * DT + CT, 7 * DT + 2 * CT
PARAM_ROWS = 7 * DT + 3 * CT
PE_TILE = CT - 1
EARLY = 16
TAPS_AT = [10, 10, 8, 26, 4, 3, 6, 1, 3, 1]
KEY_COLS = [S - P * b for b in range(TT)]
KEY_OFF = [0, 512, 1024, 896]
SCORES = 1280
FIN = [(0, 0, 0), (0, 1, 1), (0, 2, 2), (0, 3, 3), (1, 0, 6), (1, 1, 4), (1, 2, 5), (1, 3, 0)]
EXP_LN_SET = 6


def trunk_kernel(nc, x, g_ffn1, w_ffn1_gate, w_ffn1_up, w_ffn1_down, g_mix, w_in_ab, conv_w, conv_b,
                 ln_a_g, ln_a_b, ln_v_g, ln_v_b, sp_w, sp_b, w_out_ab, w_qkv, w_o, g_ffn2,
                 w_ffn2_gate, w_ffn2_up, w_ffn2_down, g_final, out):
    ctx = ExitStack()
    with ctx:
        def sb(name, shape, dt=F32, scope=ctx):
            return scope.enter_context(nc.sbuf_tensor(name, shape, dt))

        def sem(name):
            return ctx.enter_context(nc.semaphore(name))

        x_res = sb("x_res", [P, DT, S])
        xg_hi = sb("xg_hi", [P, DT, S], F32R)
        xg_lo = sb("xg_lo", [P, DT, S], F32R)
        stage = sb("stage", [P, 2, SLOT])
        w_hi = sb("w_hi", [P, 2, SLOT], F32R)
        w_lo = sb("w_lo", [P, 2, SLOT], F32R)
        sq = sb("sq", [P, S])
        ssq = sb("ssq", [P, S])
        rms = sb("rms", [P, S])
        rinv = sb("rinv", [P, S])
        tok_rms = sb("tok_rms", [P, TT])
        tok_rinv = sb("tok_rinv", [P, TT])
        ones = sb("ones", [P, P])
        neg_ones = sb("neg_ones", [P, P], F32R)
        neg_tri = sb("neg_tri", [P, P], F32R)
        ident = sb("ident", [P, P])
        params = sb("params", [P, PARAM_ROWS])
        taps = sb("taps", [P, TAPS * CT])
        eps_col = sb("eps_col", [P, 1])
        eps_root = sb("eps_root", [P, 1])
        ps = ctx.enter_context(nc.psum_tensor("ps", [P, 8, 512], F32))

        with ExitStack() as begin:
            x_tok = sb("x_tok", [P, TT, D], scope=begin)
            param_rows = sb("param_rows", [PARAM_ROWS, P], scope=begin)
            conv_rows = sb("conv_rows", [TAPS * CT, P], scope=begin)
        with ExitStack() as ffn_scope:
            hid_hi = sb("hid_hi", [P, FT, S], F32R, ffn_scope)
            hid_lo = sb("hid_lo", [P, FT, S], F32R, ffn_scope)
            gate = sb("gate", [P, 2, S], scope=ffn_scope)
            up = sb("up", [P, 2, S], scope=ffn_scope)
        with ExitStack() as conv_scope:
            a_pad = sb("a_pad", [P, CT, PAD + S], scope=conv_scope)
            y = sb("y", [P, CT, S], scope=conv_scope)
            v_mean = sb("v_mean", [P, TT, GB], scope=conv_scope)
            v_stat = sb("v_stat", [P, TT, GB], scope=conv_scope)
            v_rstd = sb("v_rstd", [P, TT, GB], scope=conv_scope)
            rinv2 = sb("rinv2", [P, TT], scope=conv_scope)
            g_buf = sb("g_buf", [P, 2, S], scope=conv_scope)
            sp_rows = sb("sp_rows", [P, GB, P], scope=conv_scope)
            sp_hi = sb("sp_hi", [P, GB, P], F32R, conv_scope)
            sp_lo = sb("sp_lo", [P, GB, P], F32R, conv_scope)
            sp_bias = sb("sp_bias", [P, GB, P], scope=conv_scope)
            lnv_g = sb("lnv_g", [P, S], scope=conv_scope)
            lnv_b = sb("lnv_b", [P, S], scope=conv_scope)
            taps_hi = sb("taps_hi", [P, TAPS], F32R, conv_scope)
            taps_lo = sb("taps_lo", [P, TAPS], F32R, conv_scope)
            with ExitStack() as early_scope:
                diags_early = [sb(f"diags_early_{part}", [P, EARLY, P], F32R, early_scope) for part in ("hi", "lo")]
            u = sb("u", [P, GB, S], scope=conv_scope)
            v_cen = sb("v_cen", [P, TT, GB, P], scope=conv_scope)
            v_n_hi = sb("v_n_hi", [P, TT, S], F32R, conv_scope)
            v_n_lo = sb("v_n_lo", [P, TT, S], F32R, conv_scope)
            with ExitStack() as late_scope:
                a_pad_hi = sb("a_pad_hi", [P, PAD + S], F32R, late_scope)
                a_pad_lo = sb("a_pad_lo", [P, PAD + S], F32R, late_scope)
                diags_late = [sb(f"diags_late_{part}", [P, TAPS - EARLY, P], F32R, late_scope) for part in ("hi", "lo")]
            ab_hi = sb("ab_hi", [P, 2 * CT, S], F32R, conv_scope)
            ab_lo = sb("ab_lo", [P, 2 * CT, S], F32R, conv_scope)
        with ExitStack() as att_scope:
            v_hi = sb("v_hi", [P, TT, D], F32R, att_scope)
            v_lo = sb("v_lo", [P, TT, D], F32R, att_scope)
            qk_f = sb("qk_f", [P, S], scope=att_scope)
            qk_hi = sb("qk_hi", [P, 2, 2, S], F32R, att_scope)
            qk_lo = sb("qk_lo", [P, 2, 2, S], F32R, att_scope)
            keep = sb("keep", [P, SCORES], scope=att_scope)
            keep_hi = sb("keep_hi", [P, SCORES], F32R, att_scope)
            keep_lo = sb("keep_lo", [P, SCORES], F32R, att_scope)
            prob = sb("prob", [P, SCORES], scope=att_scope)
            prob_hi = sb("prob_hi", [P, SCORES], F32R, att_scope)
            prob_lo = sb("prob_lo", [P, SCORES], F32R, att_scope)
            o_att = sb("o_att", [P, DT, S], scope=att_scope)
        with ExitStack() as end:
            out_tok = sb("out_tok", [P, TT, D], scope=end)

        x_loaded = [sem(f"x_loaded{t}") for t in range(TT)]
        gains_loaded = sem("gains_loaded")
        biases_loaded = sem("biases_loaded")
        mixer_params = sem("mixer_params")
        consts_made = sem("consts_made")
        turned = sem("turned")
        turned_out = sem("turned_out")
        w_loaded = [sem("w_loaded0"), sem("w_loaded1")]
        w_hi_made = sem("w_hi_made")
        w_lo_made = sem("w_lo_made")
        w_used = sem("w_used")
        x_ready = sem("x_ready")
        xg_hi_made = sem("xg_hi_made")
        xg_lo_made = sem("xg_lo_made")
        x_added = sem("x_added")
        ssq_cleared = sem("ssq_cleared")
        sq_made = sem("sq_made")
        ssq_added = sem("ssq_added")
        ssq_summed = sem("ssq_summed")
        rms_made = sem("rms_made")
        rinv_made = sem("rinv_made")
        tok_summed = sem("tok_summed")
        tok_rms_made = sem("tok_rms_made")
        tok_rinv_made = sem("tok_rinv_made")
        gate_scaled = sem("gate_scaled")
        up_scaled = sem("up_scaled")
        silu_made = sem("silu_made")
        gated = sem("gated")
        hid_hi_made = sem("hid_hi_made")
        hid_lo_made = sem("hid_lo_made")
        pool_step = sem("pool_step")
        dve_step = sem("dve_step")
        act_step = sem("act_step")
        a_gate_scaled = sem("a_gate_scaled")
        a_val_scaled = sem("a_val_scaled")
        a_sigmoid = sem("a_sigmoid")
        taps_hi_made = sem("taps_hi_made")
        taps_lo_made = sem("taps_lo_made")
        diags_made = sem("diags_made")
        a_made = sem("a_made")
        a_pad_hi_made = sem("a_pad_hi_made")
        a_pad_lo_made = sem("a_pad_lo_made")
        taps_summed = sem("taps_summed")
        taps_copied = sem("taps_copied")
        late_added = sem("late_added")
        v_scaled = sem("v_scaled")
        v_centred = sem("v_centred")
        v_squared = sem("v_squared")
        v_stat_made = sem("v_stat_made")
        v_std_made = sem("v_std_made")
        v_rstd_made = sem("v_rstd_made")
        v_normed = sem("v_normed")
        v_n_hi_made = sem("v_n_hi_made")
        v_n_lo_made = sem("v_n_lo_made")
        sp_ready = sem("sp_ready")
        u_scaled = sem("u_scaled")
        mixed = sem("mixed")
        b_made = sem("b_made")
        b_hi_made = sem("b_hi_made")
        b_lo_made = sem("b_lo_made")
        conv_made = sem("conv_made")
        ysum_made = sem("ysum_made")
        y_mean_sum = sem("y_mean_sum")
        y_centred = sem("y_centred")
        y_squared = sem("y_squared")
        ysq_sum_made = sem("ysq_sum_made")
        y_var_sum = sem("y_var_sum")
        y_std_made = sem("y_std_made")
        y_normed = sem("y_normed")
        a_silu = sem("a_silu")
        a_hi_made = sem("a_hi_made")
        a_lo_made = sem("a_lo_made")
        mix_summed = sem("mix_summed")
        v_hi_made = sem("v_hi_made")
        v_lo_made = sem("v_lo_made")
        proj_summed = sem("proj_summed")
        proj_scaled = sem("proj_scaled")
        proj_hi_made = sem("proj_hi_made")
        proj_lo_made = sem("proj_lo_made")
        scores_summed = sem("scores_summed")
        log1p_made = sem("log1p_made")
        keep_made = sem("keep_made")
        keep_masked = sem("keep_masked")
        keep_hi_made = sem("keep_hi_made")
        keep_lo_made = sem("keep_lo_made")
        suffix_summed = sem("suffix_summed")
        prob_made = sem("prob_made")
        prob_masked = sem("prob_masked")
        prob_hi_made = sem("prob_hi_made")
        prob_lo_made = sem("prob_lo_made")
        att_summed = sem("att_summed")
        o_part_summed = sem("o_part_summed")
        o_half_summed = sem("o_half_summed")
        o_copied = sem("o_copied")
        o_hi_made = sem("o_hi_made")
        o_lo_made = sem("o_lo_made")
        y_fin_made = sem("y_fin_made")
        fin_turned = sem("fin_turned")
        last_squared = sem("last_squared")
        fin_even = sem("fin_even")
        fin_odd = sem("fin_odd")
        out_stored = sem("out_stored")

        ffn_weights = [(w_ffn1_gate[0], w_ffn1_up[0], w_ffn1_down[0]),
                       (w_ffn2_gate[0], w_ffn2_up[0], w_ffn2_down[0]),
                       (w_ffn1_gate[1], w_ffn1_up[1], w_ffn1_down[1]),
                       (w_ffn2_gate[1], w_ffn2_up[1], w_ffn2_down[1])]
        param_vectors = [g_ffn1, g_mix, g_ffn2, g_final.rearrange("(a d) -> a d", a=1), ln_a_g, ln_a_b, conv_b]
        x_dram = x.rearrange("b (t p) d -> p (b t) d", p=P)
        out_dram = out.rearrange("b (t p) d -> p (b t) d", p=P)

        def rows_of(w, k0, k1, cols):
            return w.rearrange("(k p) f -> p k f", p=P)[:, k0:k1, cols]

        def three(pe, to, a_hi, a_lo, b_hi, b_lo, start, stop=False):
            pe.matmul(to, a_hi, b_hi, start=start, stop=False, skip_group_check=True)
            pe.matmul(to, a_hi, b_lo, start=False, stop=False, skip_group_check=True)
            return pe.matmul(to, a_lo, b_hi, start=False, stop=stop, skip_group_check=True)

        def load_params(engine, vectors, row, done):
            for vec in vectors:
                rows = vec.shape[0] * vec.shape[1] // P
                engine.dma_start(param_rows[row:row + rows, :],
                                 vec.rearrange("a (j p) -> (a j) p", p=P)).then_inc(done, 16)
                row += rows

        block = ctx.enter_context(nc.Block())

        @block.sync
        def _(sp):
            def free_slot(c):
                sp.wait_ge(w_hi_made, c - 1)
                sp.wait_ge(w_lo_made, c - 1)

            def load(slot, first, second):
                for n, src in enumerate((first, second)):
                    k, cols = src.shape[1], src.shape[2]
                    at = n * first.shape[1] * cols
                    sp.dma_start(stage[:, slot, at:at + k * cols].rearrange("p (k f) -> p k f", k=k),
                                 src).then_inc(w_loaded[slot], 16)

            def load_ffn(n):
                w_gate, w_up, w_down = ffn_weights[n]
                c0 = C_FFN[n]

                def pair(f, slot):
                    load(slot, rows_of(w_gate, 0, DT, bass.ds(f * P, P)), rows_of(w_up, 0, DT, bass.ds(f * P, P)))

                for f in range(2):
                    if c0 + f >= 2:
                        free_slot(c0 + f)
                    pair(f, f)
                with sp.Fori(1, FT // 2) as i:
                    for s in range(2):
                        free_slot(2 * i + (c0 + s))
                        pair(2 * i + s, s)
                with sp.Fori(0, DT) as j:
                    for s in range(2):
                        free_slot(2 * j + (c0 + FT + s))
                        k = s * HK
                        load(s, rows_of(w_down, k, k + 6, bass.ds(j * P, P)),
                             rows_of(w_down, k + 6, k + HK, bass.ds(j * P, P)))

            def load_cols(c, w, k0, k1, col0, cols):
                free_slot(c)
                mid = (k0 + k1) // 2
                load(c % 2, rows_of(w, k0, mid, slice(col0, col0 + cols)),
                     rows_of(w, mid, k1, slice(col0, col0 + cols)))

            def load_pair(c, w, col_a, col_b):
                free_slot(c)
                load(c % 2, rows_of(w, 0, DT, slice(col_a, col_a + P)), rows_of(w, 0, DT, slice(col_b, col_b + P)))

            for t in range(TT):
                sp.dma_start(x_tok[:, t, :], x_dram[:, t, :]).then_inc(x_loaded[t], 16)
            load_ffn(0)

            w_in, w_out = w_in_ab[0], w_out_ab[0]
            for i in range(CT):
                load_pair(C_CONV + i, w_in, i * P, CA + i * P)
            sp.wait_ge(w_used, C_CONV)
            sp.dma_start(sp_rows[:, :, :], sp_w[0].rearrange("g t s -> t g s")).then_inc(mixer_params, 16)
            sp.dma_start(sp_bias[:, :, :], sp_b[0].partition_broadcast(P)).then_inc(mixer_params, 16)
            sp.dma_start(lnv_g[:, :], ln_v_g[0].rearrange("g d -> (g d)").partition_broadcast(P)).then_inc(mixer_params, 16)
            sp.dma_start(lnv_b[:, :], ln_v_b[0].rearrange("g d -> (g d)").partition_broadcast(P)).then_inc(mixer_params, 16)
            for kh in range(2):
                load_cols(C_CONV + 4 + kh, w_in, 4 * kh, 4 * kh + 4, 3 * CA, CA)
            for i in range(2):
                load_pair(C_CONV + 6 + i, w_in, 2 * CA + 2 * i * P, 2 * CA + (2 * i + 1) * P)
            for n in range(4):
                k0 = CT if n < 2 else 0
                load_cols(C_CONV + 8 + n, w_out, k0, k0 + 4, (n % 2) * S, S)
            load_ffn(1)
            load_ffn(2)
            load_pair(C_ATT, w_qkv[0], 0, D)
            for n in range(4):
                load_cols(C_ATT + 1 + n, w_qkv[0], 4 * (n % 2), 4 * (n % 2) + 4, 2 * D + (n // 2) * 512, 512)
            for j in range(1, DT):
                load_pair(C_ATT + 4 + j, w_qkv[0], j * P, D + j * P)
            for n in range(4):
                k0 = 4 * (n // 2)
                load_cols(C_ATT + 12 + n, w_o[0], k0, k0 + 4, (n % 2) * 512, 512)
            load_ffn(3)

            for n, (half, t, bank) in enumerate(FIN):
                sp.wait_ge(fin_even if n % 2 == 0 else fin_odd, n // 2 + 1)
                cols = slice(half * 512, (half + 1) * 512)
                sp.dma_start(out_dram[:, t, cols], out_tok[:, t, cols]).then_inc(out_stored, 16)
            sp.wait_ge(out_stored, 16 * len(FIN))

        @block.tensor
        def _(pe):
            def sum_squares():
                return pe.matmul(ps[:, 6, :], ones[:, :], ssq[:, :], start=True, stop=True)

            def sum_squares_tok():
                for t in range(TT):
                    mm = pe.matmul(ps[:, 7, t:t + 1], ssq[:, t * P:(t + 1) * P], ones[:, 0:1], start=True, stop=True)
                return mm

            def tile(slot, n):
                return w_hi[:, slot, n * P:(n + 1) * P], w_lo[:, slot, n * P:(n + 1) * P]

            def pair_chunk(slot, banks, norm=None, tok=False, wait_x=None, stats_at=5):
                for k in range(DT):
                    if wait_x is not None:
                        pe.wait_ge(xg_lo_made, wait_x * DT + k + 1)
                    for n in range(2):
                        mm = three(pe, ps[:, banks[n], :], *tile(slot, n * DT + k),
                                   xg_hi[:, k, :], xg_lo[:, k, :], start=(k == 0), stop=(k == DT - 1))
                    if norm is not None and k == stats_at:
                        pe.wait_ge(ssq_added, (norm + 1) * DT)
                        sum_squares().then_inc(ssq_summed, 1)
                        if tok:
                            sum_squares_tok().then_inc(tok_summed, 1)
                mm.then_inc(w_used, 1)

            def ffn(n):
                c0, f0, norm = C_FFN[n], n * FT, NORM_FFN[n]
                for s in range(2):
                    pe.wait_ge(w_lo_made, c0 + s + 1)
                    late = n in (0, 3)
                    stats = s == (1 if late else 0)
                    pair_chunk(s, (2 * s, 2 * s + 1), norm if stats else None, False, norm if s == 0 else None,
                               0 if late else 5)
                with pe.Fori(1, FT // 2) as i:
                    for s in range(2):
                        pe.wait_ge(w_lo_made, 2 * i + (c0 + s + 1))
                        pe.wait_ge(up_scaled, 2 * i + (f0 + s - 1))
                        pair_chunk(s, (2 * s, 2 * s + 1))

                def down(i, q):
                    pe.wait_ge(x_ready, 2 * i + ((norm + 1) * DT + q - 1))
                    for s in range(2):
                        pe.wait_ge(w_lo_made, 4 * i + (c0 + FT + 2 * q + s + 1))
                        for k in range(HK):
                            if s == 1 and k == HK - 1:
                                pe.wait_ge(hid_lo_made, f0 + FT)
                            elif s == 0 and k == 0:
                                pe.wait_ge(hid_lo_made, f0 + FT - 1)
                            h = s * HK + k
                            mm = three(pe, ps[:, 4 + q, :], *tile(s, k), hid_hi[:, h, :], hid_lo[:, h, :],
                                       start=(h == 0), stop=(h == FT - 1))
                        mm.then_inc(w_used, 1)

                if n < 3:
                    with pe.Fori(0, DT // 2) as i:
                        for q in range(2):
                            down(i, q)
                else:
                    with pe.Fori(0, DT // 2 - 1) as i:
                        for q in range(2):
                            down(i, q)
                    for j in range(4):
                        turn_result(j, range(TT))
                    down(DT // 2 - 1, 0)
                    for j in range(4, 6):
                        turn_result(j, range(1))
                    down(DT // 2 - 1, 1)

            def turn_result(j, tiles):
                pe.wait_ge(y_fin_made, j + 1)
                for half, t, bank in FIN:
                    if half == j // 4 and t in tiles:
                        mm = pe.transpose(ps[:, bank, (j % 4) * P:(j % 4 + 1) * P],
                                          x_res[:, j, t * P:(t + 1) * P], ident[:, :])
                        if j % 4 == 3:
                            mm.then_inc(fin_turned, 1)

            def v_chunk(slot, k0, bank0, stop, wait_x=None):
                for k in range(4):
                    if wait_x is not None:
                        pe.wait_ge(xg_lo_made, wait_x * DT + k0 + k + 1)
                    w_h, w_l = w_hi[:, slot, k * 512:(k + 1) * 512], w_lo[:, slot, k * 512:(k + 1) * 512]
                    for t in range(TT):
                        mm = three(pe, ps[:, bank0 + t, :], xg_hi[:, k0 + k, t * P:(t + 1) * P],
                                   xg_lo[:, k0 + k, t * P:(t + 1) * P], w_h, w_l,
                                   start=(k0 + k == 0), stop=(k0 + k == DT - 1))
                return mm

            pe.wait_ge(consts_made, 1)
            for t in range(TT):
                pe.wait_ge(x_loaded[t], 16)
                for j in range(DT):
                    mm = pe.transpose(ps[:, j, t * P:(t + 1) * P], x_tok[:, t, j * P:(j + 1) * P], ident[:, :])
                    if t == TT - 1:
                        mm.then_inc(turned, 1)
            pe.wait_ge(gains_loaded, 16 * 4)
            pe.wait_ge(biases_loaded, 16 * 4)
            pe.wait_ge(x_ready, 1)
            pe.transpose(ps[:, 0, 0:PARAM_ROWS], param_rows[:, :], ident[0:PARAM_ROWS, 0:PARAM_ROWS])
            pe.transpose(ps[:, 0, P:P + TAPS * CT], conv_rows[:, :], ident[0:TAPS * CT, 0:TAPS * CT]).then_inc(turned, 1)
            pe.wait_ge(turned_out, 1)
            pe.wait_ge(x_ready, DT)
            ffn(0)

            c0 = C_CONV
            for i in range(CT):
                pe.wait_ge(w_lo_made, c0 + i + 1)
                if i >= 2:
                    pe.wait_ge(a_val_scaled, i - 1)
                s = i % 2
                first = i == 0
                pair_chunk(s, (2 * s, 2 * s + 1), NORM_CONV if first else None, first, NORM_CONV if first else None)
            pe.wait_ge(mixer_params, 16 * 4)
            pe.wait_ge(a_val_scaled, 3)
            for g in range(GB):
                mm = pe.transpose(ps[:, 0, g * P:(g + 1) * P], sp_rows[:, g, :], ident[:, :])
            mm.then_inc(turned, 1)
            pe.wait_ge(rms_made, NORM_CONV + 1)
            pe.wait_ge(tok_rms_made, 1)
            pe.wait_ge(w_lo_made, c0 + 5)
            v_chunk(0, 0, 4, False).then_inc(w_used, 1)

            def convolve_diagonal(bank, diags, first):
                taps = diags[0].shape[1]
                for n in range(taps):
                    k = first + n
                    mm = three(pe, ps[:, bank, :], diags[0][:, n, :], diags[1][:, n, :], a_pad_hi[:, k:k + S],
                               a_pad_lo[:, k:k + S], start=(n == 0), stop=(n == taps - 1))
                mm.then_inc(taps_summed, 1)

            pe.wait_ge(diags_made, 2)
            pe.wait_ge(a_pad_lo_made, 1)
            convolve_diagonal(1, diags_early, 0)
            pe.wait_ge(w_lo_made, c0 + 6)
            v_chunk(1, 4, 4, True).then_inc(w_used, 1)
            pe.wait_ge(a_val_scaled, CT)
            pe.wait_ge(taps_copied, 1)
            pe.wait_ge(turned_out, 2)
            for i in range(2):
                pe.wait_ge(w_lo_made, c0 + 7 + i)
                pair_chunk(i, (2 * i, 2 * i + 1))
            pe.wait_ge(v_centred, TT)
            pe.wait_ge(diags_made, 4)
            convolve_diagonal(7, diags_late, EARLY)
            pe.wait_ge(sp_ready, 1)
            for g in range(GB):
                if g == 3:
                    pe.wait_ge(late_added, 1)
                for t in range(TT):
                    pe.wait_ge(v_n_lo_made, t + 1)
                    mm = three(pe, ps[:, 4 + g, t * P:(t + 1) * P], v_n_hi[:, t, g * P:(g + 1) * P],
                               v_n_lo[:, t, g * P:(g + 1) * P], sp_hi[:, g, :], sp_lo[:, g, :], start=True, stop=True)
                mm.then_inc(mixed, 1)
            for n in range(4):
                pe.wait_ge(w_lo_made, c0 + 9 + n)
                for m in range(4):
                    j = 4 * (n % 2) + m
                    if n == 0:
                        pe.wait_ge(u_scaled, m + 1)
                    elif n == 1 and m == 2:
                        pe.wait_ge(y_centred, CT)
                    elif n == 1 and m == 3:
                        pe.wait_ge(y_std_made, 1)
                    for k in range(4):
                        src = k + (CT if n < 2 else 0)
                        if n < 2:
                            pe.wait_ge(b_lo_made, k + 1)
                        else:
                            pe.wait_ge(a_lo_made, k + 1)
                        mm = three(pe, ps[:, j, :], *tile(n % 2, 4 * k + m), ab_hi[:, src, :], ab_lo[:, src, :],
                                   start=(n < 2 and k == 0), stop=(n >= 2 and k == 3))
                    if n >= 2 and m < 3:
                        mm.then_inc(mix_summed, 1)
                    if n == 1 and m == 0:
                        pe.wait_ge(ysum_made, 1)
                        pe.matmul(ps[:, 6, :], ones[:, :], sq[:, :], start=True, stop=True).then_inc(y_mean_sum, 1)
                    if n == 1 and m == 2:
                        pe.wait_ge(ysq_sum_made, 1)
                        pe.matmul(ps[:, 7, :], ones[:, :], sq[:, :], start=True, stop=True).then_inc(y_var_sum, 1)
                mm.then_inc(w_used, 1)
            ffn(1)
            ffn(2)

            c0 = C_ATT
            pe.wait_ge(w_lo_made, c0 + 1)
            pair_chunk(0, (2, 3), NORM_ATT, True, NORM_ATT)
            for n in range(4):
                half, kh = n // 2, n % 2
                pe.wait_ge(w_lo_made, c0 + 2 + n)
                if n == 0:
                    pe.wait_ge(rms_made, NORM_ATT + 1)
                    pe.wait_ge(tok_rms_made, 2)
                elif n == 2:
                    pe.wait_ge(proj_scaled, 2)
                v_chunk((n + 1) % 2, 4 * kh, 4 - 4 * half, kh == 1).then_inc(w_used, 1)

            def project(n):
                slot = (n // 2) % 2
                pe.wait_ge(w_lo_made, c0 + 5 + n // 2)
                if n == 2:
                    pe.wait_ge(v_lo_made, TT)
                else:
                    pe.wait_ge(proj_scaled, n)
                for k in range(DT):
                    mm = three(pe, ps[:, 6, :], *tile(slot, (n % 2) * DT + k), xg_hi[:, k, :], xg_lo[:, k, :],
                               start=(k == 0), stop=(k == DT - 1))
                mm.then_inc(w_used if n % 2 else proj_summed, 1)

            def zcols(h, b, skip=0, cols=None):
                at = 3 * (h % 2) * 512 + KEY_OFF[b] + skip * P
                return ps[:, :, :].rearrange("p a c -> p (a c)")[:, at:at + (cols or KEY_COLS[b] - skip * P)]

            def scores(h):
                j, r0 = h // 2, DH * (h % 2)
                pe.wait_ge(proj_lo_made, 2 * j + 2)
                if h >= 2:
                    pe.wait_ge(prob_made, h - 1)
                elif h == 0:
                    pe.wait_ge(v_lo_made, 2 * TT)
                for b in range(TT):
                    r = slice(r0, r0 + DH)
                    mm = three(pe, zcols(h, b), qk_hi[r, j % 2, 1, b * P:(b + 1) * P],
                               qk_lo[r, j % 2, 1, b * P:(b + 1) * P], qk_hi[r, j % 2, 0, b * P:S],
                               qk_lo[r, j % 2, 0, b * P:S], start=(b < 3))
                mm.then_inc(scores_summed, 1)

            def suffix(h):
                pe.wait_ge(keep_lo_made, h + 1)
                for part in (keep_hi, keep_lo):
                    for b, cols in ((0, KEY_COLS[0]), (1, KEY_COLS[1] + KEY_COLS[3]), (2, KEY_COLS[2])):
                        pe.matmul(zcols(h, b, cols=cols), neg_tri[:, :], part[:, KEY_OFF[b]:KEY_OFF[b] + cols],
                                  start=False, stop=False, skip_group_check=True)
                    for b in range(TT):
                        for later in range(b + 1, TT):
                            off = KEY_OFF[later]
                            mm = pe.matmul(zcols(h, b, later - b), neg_ones[:, :],
                                           part[:, off:off + KEY_COLS[later]],
                                           start=False, stop=False, skip_group_check=True)
                mm.then_inc(suffix_summed, 1)

            def attend(h):
                j = h // 2
                pe.wait_ge(prob_lo_made, h + 1)
                if h >= 1:
                    pe.wait_ge(o_copied, h)
                for b in range(TT):
                    off = KEY_OFF[b]
                    cols = slice(off, off + KEY_COLS[b])
                    mm = three(pe, ps[:, 7, b * P:S], v_hi[:, b, j * P:(j + 1) * P], v_lo[:, b, j * P:(j + 1) * P],
                               prob_hi[:, cols], prob_lo[:, cols], start=(b == 0), stop=(b == TT - 1))
                mm.then_inc(att_summed, 1)

            def out_tile(q, bank, k_from=0, k_to=4):
                n, k0 = q // 4, 4 * (q // 8)
                pe.wait_ge(w_lo_made, c0 + 13 + n)
                for k in range(k_from, k_to):
                    pe.wait_ge(o_lo_made, k0 + k + 1)
                    cols = slice((k0 + k) * P, (k0 + k + 1) * P)
                    mm = three(pe, ps[:, bank, :].rearrange("p (t c) -> p t c", t=TT), *tile(n % 2, 4 * k + q % 4),
                               v_hi[:, :, cols], v_lo[:, :, cols], start=(k == 0), stop=(k == 3))
                if k_to < 4:
                    return
                if q % 4 == 3:
                    mm.then_inc(w_used, 1)
                else:
                    mm.then_inc(o_part_summed if q < DT else o_half_summed, 1)

            def out_part(q):
                if q:
                    pe.wait_ge(x_added, q)
                else:
                    pe.wait_ge(proj_scaled, HEADS)
                out_tile(q, 6)

            for h in range(HEADS + 2):
                if h == 0:
                    project(2)
                if h < HEADS:
                    scores(h)
                if 13 <= h < 17:
                    out_part(2 * (h - 13))
                if 1 <= h <= HEADS:
                    suffix(h - 1)
                if 13 <= h < 17:
                    out_part(2 * (h - 13) + 1)
                if h == HEADS + 1:
                    for q in range(DT, DT + 3):
                        out_tile(q, q - DT, 0, 3)
                if h >= 2:
                    attend(h - 2)
                if h + 3 < HEADS:
                    project(h + 3)
            out_tile(DT + 3, 3, 0, 3)
            for q in range(DT, DT + 4):
                out_tile(q, q - DT, 3, 4)
            for q in range(DT + 4, 2 * DT):
                if q == DT + 6:
                    pe.wait_ge(x_added, DT)
                elif q == DT + 7:
                    pe.wait_ge(o_copied, HEADS)
                out_tile(q, q - DT)
            ffn(3)

            pe.wait_ge(ssq_added, (NORM_FINAL + 1) * DT - 1)
            pe.wait_ge(x_ready, (NORM_FINAL + 1) * DT - 1)
            for t in range(TT):
                pe.matmul(ps[:, 7, t:t + 1], ssq[:, t * P:(t + 1) * P], ones[:, 0:1], start=(t == 0), stop=False,
                          skip_group_check=True)
            turn_result(6, range(2))
            for j in range(4, 6):
                turn_result(j, range(1, 2))
            pe.wait_ge(last_squared, 1)
            for t in range(TT):
                mm = pe.matmul(ps[:, 7, t:t + 1], sq[:, t * P:(t + 1) * P], ones[:, 0:1], start=False, stop=True,
                               skip_group_check=True)
            mm.then_inc(tok_summed, 1)
            turn_result(7, range(2))
            for j in range(4, DT):
                turn_result(j, range(2, 3))
            pe.wait_ge(fin_even, 1)
            for j in range(4, DT):
                turn_result(j, range(3, 4))

        @block.scalar
        def _(act):
            steps = [0]

            def step(ins):
                steps[0] += 1
                ins.then_inc(act_step, 1)
                act.wait_ge(act_step, steps[0])

            def split_hi(c, slot, loads, cols=SLOT):
                act.wait_ge(w_loaded[slot], loads)
                act.wait_ge(w_used, c - 1)
                act.activation(w_hi[:, slot, 0:cols], stage[:, slot, 0:cols], ACT.Copy).then_inc(w_hi_made, 1)

            def split_static(c, cols=SLOT):
                if c < CHUNKS:
                    act.wait_ge(w_loaded[c % 2], 32 * (c // 2 + 1))
                    if c >= 2:
                        act.wait_ge(w_used, c - 1)
                    act.activation(w_hi[:, c % 2, 0:cols], stage[:, c % 2, 0:cols], ACT.Copy).then_inc(w_hi_made, 1)

            def x_tile(n, j, ready):
                act.wait_ge(x_ready, ready)
                act.activation(xg_hi[:, bass.ds(j, 1), :].rearrange("p a s -> p (a s)"),
                               x_res[:, bass.ds(j, 1), :].rearrange("p a s -> p (a s)"), ACT.Copy,
                               scale=params[:, bass.ds(j + GAIN_ROW[n], 1)]).then_inc(xg_hi_made, 1)

            def token_rms(n):
                act.wait_ge(ssq_summed, n + 1)
                act.activation(rms[:, :], ps[:, 6, :], ACT.Sqrt, bias=eps_col[:, 0:1], scale=1.0 / D).then_inc(rms_made, 1)

            def token_rms_tok(n):
                act.wait_ge(tok_summed, n)
                act.activation(tok_rms[:, :], ps[:, 7, 0:TT], ACT.Sqrt, bias=eps_col[:, 0:1],
                               scale=1.0 / D).then_inc(tok_rms_made, 1)

            def hidden(f, count, s):
                act.wait_ge(gate_scaled, count)
                act.activation(gate[:, s, :], gate[:, s, :], ACT.Silu).then_inc(silu_made, 1)
                act.wait_ge(gated, count)
                act.activation(hid_hi[:, bass.ds(f, 1), :].rearrange("p a s -> p (a s)"), up[:, s, :],
                               ACT.Copy).then_inc(hid_hi_made, 1)

            def ffn(n):
                c0, f0, norm = C_FFN[n], n * FT, NORM_FFN[n]
                half0 = c0 // 2
                split_static(c0 + 1)
                token_rms(norm)
                hidden(0, f0 + 1, 0)
                split_static(c0 + 2)
                hidden(1, f0 + 2, 1)
                with act.Fori(1, FT // 2 - 1) as i:
                    for s in range(2):
                        o = 1 - s
                        split_hi(2 * i + (c0 + s + 1), o, 32 * i + 32 * (half0 + s + 1))
                        hidden(2 * i + s, 2 * i + (f0 + s + 1), s)
                split_static(c0 + FT - 1)
                hidden(FT - 2, f0 + FT - 1, 0)
                split_static(c0 + FT, HK * P)
                hidden(FT - 1, f0 + FT, 1)
                act.activation(eps_root[:, :], eps_col[:, :], ACT.Sqrt)
                last = n == 3
                with act.Fori(0, DT - 1) as j:
                    split_hi(2 * j + (c0 + FT + 1), 1, 32 * j + 32 * (half0 + HK + 1), HK * P)
                    split_hi(2 * j + (c0 + FT + 2), 0, 32 * j + 32 * (half0 + HK + 2), HK * P)
                    if last:
                        final_tile(j, j + (NORM_FINAL * DT + 1))
                    else:
                        x_tile(norm + 1, j, j + ((norm + 1) * DT + 1))
                split_static(c0 + FT + 2 * DT - 1, HK * P)
                split_static(c0 + FT + 2 * DT)
                if last:
                    act.wait_ge(ssq_added, (NORM_FINAL + 1) * DT - 1)
                    act.wait_ge(x_ready, (NORM_FINAL + 1) * DT)
                    act.activation(sq[:, :], x_res[:, DT - 1, :], ACT.Square).then_inc(last_squared, 1)
                    act.wait_ge(last_squared, 1)
                    final_tile(DT - 1, (NORM_FINAL + 1) * DT - 1)
                else:
                    x_tile(norm + 1, DT - 1, (norm + 2) * DT)

            def final_tile(j, ready):
                act.wait_ge(ssq_added, ready)
                act.activation(x_res[:, bass.ds(j, 1), :].rearrange("p a s -> p (a s)"),
                               x_res[:, bass.ds(j, 1), :].rearrange("p a s -> p (a s)"), ACT.Copy,
                               scale=params[:, bass.ds(j + GAIN_ROW[NORM_FINAL], 1)]).then_inc(y_fin_made, 1)

            load_params(act, param_vectors[:4], 0, gains_loaded)
            act.wait_ge(consts_made, 2)
            act.activation(eps_root[:, :], eps_col[:, :], ACT.Sqrt)
            act.wait_ge(turned_out, 1)
            for j in range(2):
                x_tile(0, j, j + 1)
            split_static(0)
            for j in range(2, DT):
                x_tile(0, j, j + 1)
            ffn(0)

            c0 = C_CONV
            for i in range(CT):
                split_static(c0 + i + 1)
                if i == 0:
                    token_rms(NORM_CONV)
                    token_rms_tok(1)
                act.wait_ge(a_gate_scaled, i + 1)
                act.activation(g_buf[:, 0, :], g_buf[:, 0, :], ACT.Sigmoid).then_inc(a_sigmoid, 1)
                if i == 1:
                    act.activation(taps_hi[:, :], taps[:, PE_TILE:TAPS * CT:CT], ACT.Copy).then_inc(taps_hi_made, 1)
            act.wait_ge(a_made, 1)
            act.activation(a_pad_hi[:, :], a_pad[:, PE_TILE, :], ACT.Copy).then_inc(a_pad_hi_made, 1)
            split_static(c0 + 5)
            act.wait_ge(turned, DT + 2)
            act.activation(sp_rows[:, :, :], ps[:, 0, :].rearrange("p (g t) -> p g t", g=GB), ACT.Copy).then_inc(turned_out, 1)
            split_static(c0 + 6)
            act.wait_ge(taps_summed, 1)
            act.activation(y[:, PE_TILE, :], ps[:, 1, :], ACT.Identity,
                           bias=params[:, ROW_CONV_B + PE_TILE:ROW_CONV_B + PE_TILE + 1]).then_inc(taps_copied, 1)
            split_static(c0 + 7)
            for t in range(TT):
                act.wait_ge(v_centred, t + 1)
                for g in range(GB):
                    ins = act.activation(u[:, t, g * P:(g + 1) * P], v_cen[:, t, g, :], ACT.Square,
                                         accum_out=v_stat[:, t, g:g + 1])
                ins.then_inc(v_squared, 1)
            act.wait_ge(v_stat_made, 1)
            act.activation(v_stat[:, :, :], v_stat[:, :, :], ACT.Sqrt, bias=eps_col[:, 0:1], scale=1.0 / P).then_inc(v_std_made, 1)
            act.wait_ge(v_rstd_made, 1)
            for t in range(TT):
                for g in range(GB):
                    ins = act.activation(v_cen[:, t, g, :], v_cen[:, t, g, :], ACT.Copy, scale=v_rstd[:, t, g:g + 1])
                ins.then_inc(v_scaled, 1)
            split_static(c0 + 8)
            for t in range(TT):
                act.wait_ge(v_normed, t + 1)
                act.activation(v_n_hi[:, t, :], v_cen[:, t].rearrange("p g c -> p (g c)"), ACT.Copy).then_inc(v_n_hi_made, 1)
            split_static(c0 + 9)
            for g in range(GB):
                act.wait_ge(b_made, g + 1)
                act.activation(ab_hi[:, CT + g, :], u[:, g, :], ACT.Copy).then_inc(b_hi_made, 1)
            split_static(c0 + 10)
            for i in range(CT):
                act.wait_ge(y_centred, i + 1)
                act.activation(v_cen[:, i].rearrange("p g c -> p (g c)"), y[:, i, :], ACT.Square).then_inc(y_squared, 1)
            act.wait_ge(y_var_sum, 1)
            act.activation(rms[:, :], ps[:, 7, :], ACT.Sqrt, bias=eps_col[:, 0:1], scale=1.0 / CA).then_inc(y_std_made, 1)
            for i in range(CT):
                act.wait_ge(y_normed, i + 1)
                act.activation(y[:, i, :], y[:, i, :], ACT.Silu, scale=params[:, ROW_LN_G + i:ROW_LN_G + i + 1],
                               bias=params[:, ROW_LN_B + i:ROW_LN_B + i + 1]).then_inc(a_silu, 1)
                act.wait_ge(a_silu, i + 1)
                act.activation(ab_hi[:, i, :], y[:, i, :], ACT.Copy).then_inc(a_hi_made, 1)
            split_static(c0 + 11)
            for j in range(4):
                x_tile(2, j, 2 * DT + j + 1)
            split_static(c0 + 12)
            for j in range(4, DT):
                x_tile(2, j, 2 * DT + j + 1)
            ffn(1)
            ffn(2)

            c0 = C_ATT
            split_static(c0 + 1)
            token_rms(NORM_ATT)
            token_rms_tok(2)

            def split_v(half):
                act.wait_ge(tok_rinv_made, 2)
                act.wait_ge(w_used, c0 + 3 + 2 * half)
                for t in range(TT):
                    act.activation(v_hi[:, t, half * 512:(half + 1) * 512], ps[:, 4 - 4 * half + t, :], ACT.Copy,
                                   scale=tok_rinv[:, t:t + 1]).then_inc(v_hi_made, 1)

            def split_proj(n):
                act.wait_ge(proj_scaled, n + 1)
                act.activation(qk_hi[:, (n // 2) % 2, n % 2, :], qk_f[:, :], ACT.Copy).then_inc(proj_hi_made, 1)

            def zall(h):
                at = 3 * (h % 2) * 512
                return ps[:, :, :].rearrange("p a c -> p (a c)")[:, at:at + SCORES]

            def split_out(j):
                act.wait_ge(o_copied, 2 * j + 2)
                act.activation(v_hi[:, :, j * P:(j + 1) * P], o_att[:, j, :].rearrange("p (t c) -> p t c", t=TT),
                               ACT.Copy).then_inc(o_hi_made, 1)

            split_proj(0)
            split_proj(1)
            for n in range(2, 5):
                split_static(c0 + n)
            split_v(0)
            split_static(c0 + 5)
            act.add_instruction(mybir.InstLoadActFuncSet(
                name=nc.get_next_instruction_name(), engine=mybir.EngineType.Activation, act_func_set_id=EXP_LN_SET))
            split_v(1)
            split_static(c0 + 6)
            for h in range(HEADS + 2):
                if h < HEADS:
                    act.wait_ge(scores_summed, h + 1)
                    if h >= 1:
                        act.wait_ge(keep_lo_made, h)
                    step(act.activation(keep[:, :], zall(h), ACT.Abs))
                    step(act.activation(keep[:, :], keep[:, :], ACT.Exp, scale=-1.0))
                    act.activation(keep[:, :], keep[:, :], ACT.Ln, bias=1.0).then_inc(log1p_made, 1)
                if 1 <= h <= HEADS:
                    act.wait_ge(suffix_summed, h)
                    if h >= 2:
                        act.wait_ge(prob_lo_made, h - 1)
                    act.activation(prob[:, :], zall(h - 1), ACT.Exp).then_inc(prob_made, 1)
                if h + 2 < HEADS:
                    split_proj(h + 2)
                if h >= 2:
                    act.wait_ge(att_summed, h - 1)
                    r = slice(DH * (h % 2), DH * (h % 2) + DH)
                    act.activation(o_att[r, (h - 2) // 2, :], ps[r, 7, :], ACT.Copy).then_inc(o_copied, 1)
                if h >= 3 and h % 2:
                    split_out((h - 3) // 2)
                if h % 2 and h <= 13:
                    split_static(c0 + 6 + (h + 1) // 2)
                elif h == 15:
                    split_static(c0 + 14)
            for j in range(DT):
                if j % 4 == 0:
                    split_static(c0 + 15 + j // 4)
                x_tile(5, j, 5 * DT + j + 1)
            ffn(3)
            token_rms_tok(3)
            act.wait_ge(tok_rinv_made, 3)
            for n in range(1, len(FIN), 2):
                half, t, bank = FIN[n]
                act.wait_ge(fin_turned, n + 1)
                act.activation(out_tok[:, t, half * 512:(half + 1) * 512], ps[:, bank, :], ACT.Copy,
                               scale=tok_rinv[:, t:t + 1]).then_inc(fin_odd, 1)

        @block.vector
        def _(dve):
            steps = [0]

            def step(ins):
                steps[0] += 1
                ins.then_inc(dve_step, 1)
                dve.wait_ge(dve_step, steps[0])
                return ins

            def split_lo(c, slot, cols=SLOT):
                dve.wait_ge(w_hi_made, c + 1)
                dve.tensor_tensor(w_lo[:, slot, 0:cols], stage[:, slot, 0:cols],
                                  w_hi[:, slot, 0:cols].bitcast(F32), ALU.subtract).then_inc(w_lo_made, 1)

            def split_static(c, cols=SLOT):
                if c < CHUNKS:
                    split_lo(c, c % 2, cols)

            def x_low(n, j, made):
                dve.wait_ge(xg_hi_made, made)
                dve.scalar_tensor_tensor(xg_lo[:, bass.ds(j, 1), :].rearrange("p a s -> p (a s)"),
                                         x_res[:, bass.ds(j, 1), :].rearrange("p a s -> p (a s)"),
                                         params[:, bass.ds(j + GAIN_ROW[n], 1)],
                                         xg_hi[:, bass.ds(j, 1), :].rearrange("p a s -> p (a s)").bitcast(F32),
                                         ALU.mult, ALU.subtract).then_inc(xg_lo_made, 1)

            def add_to_x(j, bank, factor, done):
                xj = x_res[:, bass.ds(j, 1), :].rearrange("p a s -> p (a s)")
                dve.scalar_tensor_tensor(xj, ps[:, bank, :], factor, xj, ALU.mult, ALU.add).then_inc(done, 1)

            def invert_rms(n):
                dve.wait_ge(rms_made, n + 1)
                dve.reciprocal(rinv[:, :], rms[:, :]).then_inc(rinv_made, 1)
                dve.wait_ge(rinv_made, n + 1)

            def invert_rms_tok(n):
                dve.wait_ge(tok_rms_made, n)
                dve.reciprocal(tok_rinv[:, :], tok_rms[:, :]).then_inc(tok_rinv_made, 1)
                dve.wait_ge(tok_rinv_made, n)

            def hidden(c_used, count, prev, s):
                dve.wait_ge(w_used, c_used)
                if prev is not None:
                    dve.wait_ge(hid_lo_made, prev)
                dve.tensor_tensor(gate[:, s, :], ps[:, 2 * s, :], rinv[:, :], ALU.mult).then_inc(gate_scaled, 1)
                dve.tensor_tensor(up[:, s, :], ps[:, 2 * s + 1, :], rinv[:, :], ALU.mult).then_inc(up_scaled, 1)
                dve.wait_ge(silu_made, count)
                dve.wait_ge(up_scaled, count)
                dve.tensor_tensor(up[:, s, :], gate[:, s, :], up[:, s, :], ALU.mult).then_inc(gated, 1)

            def ffn(n):
                c0, f0, norm = C_FFN[n], n * FT, NORM_FFN[n]
                split_static(c0 + 1)
                invert_rms(norm)
                hidden(c0 + 1, f0 + 1, None, 0)
                split_static(c0 + 2)
                hidden(c0 + 2, f0 + 2, None, 1)
                with dve.Fori(1, FT // 2 - 1) as i:
                    for s in range(2):
                        split_lo(2 * i + (c0 + s + 1), 1 - s)
                        hidden(2 * i + (c0 + s + 1), 2 * i + (f0 + s + 1), 2 * i + (f0 + s - 1), s)
                split_static(c0 + FT - 1)
                hidden(c0 + FT - 1, f0 + FT - 1, f0 + FT - 3, 0)
                split_static(c0 + FT, HK * P)
                hidden(c0 + FT, f0 + FT, f0 + FT - 2, 1)
                last = n == 3
                a = (norm + 1) * DT

                def down(j, q, next_cols):
                    split_lo(2 * j + (c0 + FT + 1), 1, HK * P)
                    if next_cols is not None:
                        split_lo(2 * j + (c0 + FT + 2), 0, next_cols)
                    dve.wait_ge(w_used, 2 * j + (c0 + FT + 2))
                    add_to_x(j, 4 + q, 0.5, x_ready)
                    if not last:
                        x_low(norm + 1, j, j + (a + 1))

                with dve.Fori(0, DT // 2 - 1) as i:
                    for q in range(2):
                        down(2 * i + q, q, HK * P)
                down(DT - 2, 0, HK * P)
                down(DT - 1, 1, SLOT if not last else None)

            for j in range(DT):
                dve.wait_ge(turned, j + 1)
                dve.tensor_copy(x_res[:, j, :], ps[:, j, :]).then_inc(x_ready, 1)
                if j == 2:
                    dve.wait_ge(turned, DT + 1)
                    dve.tensor_copy(params[:, :], ps[:, 0, 0:PARAM_ROWS])
                    dve.tensor_copy(taps[:, :], ps[:, 0, P:P + TAPS * CT]).then_inc(turned_out, 1)
            dve.wait_ge(turned_out, 1)
            for j in range(2):
                x_low(0, j, j + 1)
            split_static(0)
            for j in range(2, DT):
                x_low(0, j, j + 1)
            ffn(0)

            c0 = C_CONV
            taken = [0] * (CT - 1)
            last = [0] * CT

            def convolve(n, *tiles):
                for _ in range(n):
                    i = min((i for i in tiles if taken[i] < TAPS), key=lambda i: taken[i])
                    k = taken[i]
                    seen, yi = a_pad[:, i, k:k + S], y[:, i, :]
                    w = taps[:, k * CT + i:k * CT + i + 1]
                    if k:
                        dve.wait_ge(dve_step, last[i])
                        ins = dve.scalar_tensor_tensor(yi, seen, w, yi, ALU.mult, ALU.add)
                    else:
                        ins = dve.tensor_scalar(yi, seen, w, params[:, ROW_CONV_B + i:ROW_CONV_B + i + 1],
                                                ALU.mult, ALU.add)
                    taken[i] += 1
                    if taken[i] == TAPS:
                        ins.then_inc(conv_made, 1)
                    else:
                        steps[0] += 1
                        last[i] = steps[0]
                        ins.then_inc(dve_step, 1)

            def gate_pair(i):
                dve.wait_ge(w_used, c0 + i + 1)
                dve.tensor_tensor(g_buf[:, 0, :], ps[:, 2 * (i % 2) + 1, :], rinv[:, :], ALU.mult).then_inc(a_gate_scaled, 1)
                dve.tensor_tensor(g_buf[:, 1, :], ps[:, 2 * (i % 2), :], rinv[:, :], ALU.mult).then_inc(a_val_scaled, 1)
                dve.wait_ge(a_val_scaled, i + 1)
                dve.wait_ge(a_sigmoid, i + 1)
                ins = dve.tensor_tensor(a_pad[:, i, PAD:PAD + S], g_buf[:, 0, :], g_buf[:, 1, :], ALU.mult)
                if i == PE_TILE:
                    ins.then_inc(a_made, 1)
                else:
                    step(ins)

            def scale_u(g):
                dve.tensor_tensor(u[:, g, :], ps[:, g, :], rinv[:, :], ALU.mult).then_inc(u_scaled, 1)

            split_static(c0 + 1)
            step(dve.memset(a_pad[:, :, 0:PAD], 0.0))
            invert_rms(NORM_CONV)
            invert_rms_tok(1)
            step(dve.tensor_tensor(rinv2[:, :], tok_rinv[:, :], tok_rinv[:, :], ALU.mult))
            gate_pair(0)
            split_static(c0 + 2)
            convolve(TAPS_AT[0], 0)
            gate_pair(1)
            split_static(c0 + 3)
            dve.wait_ge(taps_hi_made, 1)
            dve.tensor_tensor(taps_lo[:, :], taps[:, PE_TILE:TAPS * CT:CT], taps_hi[:, :].bitcast(F32),
                              ALU.subtract).then_inc(taps_lo_made, 1)
            convolve(TAPS_AT[1], 0, 1)
            gate_pair(2)
            split_static(c0 + 4)
            convolve(TAPS_AT[2], 0, 1, 2)
            gate_pair(3)
            dve.wait_ge(a_pad_hi_made, 1)
            dve.tensor_tensor(a_pad_lo[:, :], a_pad[:, PE_TILE, :], a_pad_hi[:, :].bitcast(F32),
                              ALU.subtract).then_inc(a_pad_lo_made, 1)
            split_static(c0 + 5)
            convolve(TAPS_AT[3], 0, 1, 2)
            split_static(c0 + 6)
            convolve(TAPS_AT[4], 0, 1, 2)
            dve.wait_ge(w_used, c0 + 6)
            for t in range(TT):
                raw = ps[:, 4 + t, :].rearrange("p (g c) -> p g c", g=GB)
                step(dve.tensor_reduce(v_mean[:, t, :], raw, AX.X, ALU.add))
                dve.scalar_tensor_tensor(v_cen[:, t], v_mean[:, t, :].unsqueeze(2).to_broadcast([P, GB, P]), -1.0 / P,
                                         raw, ALU.mult, ALU.add).then_inc(v_centred, 1)
            split_static(c0 + 7)
            dve.wait_ge(v_squared, TT)
            dve.tensor_tensor(v_stat[:, :, :], v_stat[:, :, :], rinv2[:, :].unsqueeze(2).to_broadcast([P, TT, GB]),
                              ALU.mult).then_inc(v_stat_made, 1)
            convolve(TAPS_AT[5], 0, 1, 2)
            dve.wait_ge(v_std_made, 1)
            step(dve.reciprocal(v_rstd[:, :, :], v_stat[:, :, :]))
            dve.tensor_tensor(v_rstd[:, :, :], v_rstd[:, :, :], tok_rinv[:, :].unsqueeze(2).to_broadcast([P, TT, GB]),
                              ALU.mult).then_inc(v_rstd_made, 1)
            dve.wait_ge(w_used, c0 + 7)
            scale_u(0)
            scale_u(1)
            convolve(TAPS_AT[6], 0, 1, 2)
            split_static(c0 + 8)
            for t in range(TT):
                convolve(TAPS_AT[7], 0, 1, 2)
                dve.wait_ge(v_n_hi_made, t + 1)
                dve.tensor_tensor(v_n_lo[:, t, :], v_cen[:, t].rearrange("p g c -> p (g c)"),
                                  v_n_hi[:, t, :].bitcast(F32), ALU.subtract).then_inc(v_n_lo_made, 1)
            dve.wait_ge(w_used, c0 + 8)
            scale_u(2)
            scale_u(3)
            split_static(c0 + 9)
            convolve(TAPS_AT[8], 0, 1, 2)
            dve.wait_ge(taps_summed, 2)
            dve.wait_ge(taps_copied, 1)
            dve.tensor_tensor(y[:, PE_TILE, :], ps[:, 7, :], y[:, PE_TILE, :], ALU.add).then_inc(late_added, 1)
            convolve(TAPS_AT[9], 0, 1, 2)
            dve.wait_ge(u_scaled, GB)
            for g in range(GB):
                dve.wait_ge(mixed, g + 1)
                step(dve.tensor_tensor(v_cen[:, g].rearrange("p g c -> p (g c)").rearrange("p (t c) -> p t c", t=TT),
                                       ps[:, 4 + g, :].rearrange("p (t c) -> p t c", t=TT),
                                       sp_bias[:, g, :].unsqueeze(1).to_broadcast([P, TT, P]), ALU.add))
                dve.tensor_tensor(u[:, g, :], u[:, g, :], v_cen[:, g].rearrange("p g c -> p (g c)"),
                                  ALU.mult).then_inc(b_made, 1)
            convolve(TAPS * PE_TILE - sum(taken), 0, 1, 2)
            dve.wait_ge(y_mean_sum, 1)
            for i in range(CT):
                dve.scalar_tensor_tensor(y[:, i, :], ps[:, 6, :], -1.0 / CA, y[:, i, :], ALU.mult,
                                         ALU.add).then_inc(y_centred, 1)
            split_static(c0 + 10)
            dve.wait_ge(y_std_made, 1)
            step(dve.reciprocal(g_buf[:, 1, :], rms[:, :]))
            for i in range(CT):
                dve.wait_ge(y_squared, CT)
                dve.tensor_tensor(y[:, i, :], y[:, i, :], g_buf[:, 1, :], ALU.mult).then_inc(y_normed, 1)
            for i in range(CT):
                dve.wait_ge(a_hi_made, i + 1)
                dve.tensor_tensor(ab_lo[:, i, :], y[:, i, :], ab_hi[:, i, :].bitcast(F32), ALU.subtract).then_inc(a_lo_made, 1)
            split_static(c0 + 11)
            for j in range(DT):
                if j == 4:
                    split_static(c0 + 12)
                if j % 4 == 3:
                    dve.wait_ge(w_used, c0 + 11 + j // 4)
                else:
                    dve.wait_ge(mix_summed, j + 1 - j // 4)
                add_to_x(j, j, 1.0, x_ready)
                if j:
                    x_low(2, j - 1, 2 * DT + j)
            x_low(2, DT - 1, 3 * DT)
            ffn(1)
            ffn(2)

            c0 = C_ATT
            split_static(c0 + 1)
            invert_rms(NORM_ATT)
            invert_rms_tok(2)

            def v_low(half):
                for t in range(TT):
                    dve.wait_ge(v_hi_made, 4 * half + t + 1)
                    cols = slice(half * 512, (half + 1) * 512)
                    dve.scalar_tensor_tensor(v_lo[:, t, cols], ps[:, 4 - 4 * half + t, :], tok_rinv[:, t:t + 1],
                                             v_hi[:, t, cols].bitcast(F32), ALU.mult,
                                             ALU.subtract).then_inc(v_lo_made, 1)

            def scale_proj(n):
                if n < 2:
                    dve.wait_ge(w_used, c0 + 1)
                elif n % 2:
                    dve.wait_ge(w_used, c0 + 5 + n // 2)
                else:
                    dve.wait_ge(proj_summed, n // 2)
                dve.scalar_tensor_tensor(qk_f[:, :], ps[:, 2 + n if n < 2 else 6, :], 1.0 if n % 2 else DH ** -0.5, rinv[:, :],
                                         ALU.mult, ALU.mult).then_inc(proj_scaled, 1)

            def proj_low(n):
                dve.wait_ge(proj_scaled, n + 1)
                dve.wait_ge(proj_hi_made, n + 1)
                dve.tensor_tensor(qk_lo[:, (n // 2) % 2, n % 2, :], qk_f[:, :],
                                  qk_hi[:, (n // 2) % 2, n % 2, :].bitcast(F32), ALU.subtract).then_inc(proj_lo_made, 1)
                dve.wait_ge(proj_lo_made, n + 1)

            def zall(h):
                at = 3 * (h % 2) * 512
                return ps[:, :, :].rearrange("p a c -> p (a c)")[:, at:at + SCORES]

            def split_out(j):
                dve.wait_ge(o_hi_made, j + 1)
                cols = slice(j * P, (j + 1) * P)
                dve.tensor_tensor(v_lo[:, :, cols], o_att[:, j, :].rearrange("p (t c) -> p t c", t=TT),
                                  v_hi[:, :, cols].bitcast(F32), ALU.subtract).then_inc(o_lo_made, 1)

            def add_part(q):
                if q % 4 == 3:
                    dve.wait_ge(w_used, c0 + 13 + q // 4)
                else:
                    dve.wait_ge(o_part_summed, q + 1 - q // 4)
                add_to_x(q, 6, 1.0, x_added)

            for n in range(2):
                scale_proj(n)
                proj_low(n)
            for n in range(2, 5):
                split_static(c0 + n)
            v_low(0)
            split_static(c0 + 5)
            v_low(1)
            for h in range(HEADS + 2):
                if h + 2 < HEADS:
                    scale_proj(h + 2)
                if h % 2 == 0 and h <= 14:
                    split_static(c0 + 6 + h // 2)
                elif h == 16:
                    split_static(c0 + 14)
                if 13 <= h < 17:
                    add_part(2 * (h - 13))
                if h < HEADS:
                    dve.wait_ge(log1p_made, h + 1)
                    dve.scalar_tensor_tensor(keep[:, :], zall(h), 0.0, keep[:, :], ALU.max, ALU.add).then_inc(keep_made, 1)
                    if h + 2 < HEADS:
                        proj_low(h + 2)
                if h < HEADS:
                    dve.wait_ge(keep_masked, h + 1)
                    if h >= 1:
                        dve.wait_ge(suffix_summed, h)
                    dve.tensor_copy(keep_hi[:, :], keep[:, :]).then_inc(keep_hi_made, 1)
                    dve.wait_ge(keep_hi_made, h + 1)
                    dve.tensor_tensor(keep_lo[:, :], keep[:, :], keep_hi[:, :].bitcast(F32),
                                      ALU.subtract).then_inc(keep_lo_made, 1)
                if 13 <= h < HEADS:
                    add_part(2 * (h - 13) + 1)
                if 1 <= h <= HEADS:
                    dve.wait_ge(prob_masked, h)
                    if h >= 2:
                        dve.wait_ge(att_summed, h - 1)
                    dve.tensor_copy(prob_hi[:, :], prob[:, :]).then_inc(prob_hi_made, 1)
                    dve.wait_ge(prob_hi_made, h)
                    dve.tensor_tensor(prob_lo[:, :], prob[:, :], prob_hi[:, :].bitcast(F32),
                                      ALU.subtract).then_inc(prob_lo_made, 1)
                if h == HEADS:
                    add_part(7)
                if h >= 3 and h % 2:
                    split_out((h - 3) // 2)
            for j in range(DT):
                if j % 4 == 0:
                    split_static(c0 + 15 + j // 4)
                if j == 0:
                    dve.wait_ge(x_added, DT)
                if j % 4 == 3:
                    dve.wait_ge(w_used, c0 + 15 + j // 4)
                else:
                    dve.wait_ge(o_half_summed, j + 1 - j // 4)
                add_to_x(j, j, 1.0, x_ready)
                if j:
                    x_low(5, j - 1, 5 * DT + j)
            x_low(5, DT - 1, 6 * DT)
            ffn(3)
            invert_rms_tok(3)
            for n in range(0, len(FIN), 2):
                half, t, bank = FIN[n]
                dve.wait_ge(fin_turned, n + 1)
                dve.tensor_scalar(out_tok[:, t, half * 512:(half + 1) * 512], ps[:, bank, :],
                                  tok_rinv[:, t:t + 1], None, ALU.mult).then_inc(fin_even, 1)

        @block.gpsimd
        def _(pool):
            steps = [0]

            def step(ins):
                steps[0] += 1
                ins.then_inc(pool_step, 1)
                pool.wait_ge(pool_step, steps[0])

            def clear_ssq(n):
                if n:
                    if n - 1 in (NORM_CONV, NORM_ATT):
                        pool.wait_ge(tok_summed, 1 if n - 1 == NORM_CONV else 2)
                    pool.wait_ge(ssq_summed, n)
                pool.memset(ssq[:, :], 0.0).then_inc(ssq_cleared, 1)
                pool.wait_ge(ssq_cleared, n + 1)

            def square_tile(j, count):
                pool.wait_ge(x_ready, count)
                xj = x_res[:, bass.ds(j, 1), :].rearrange("p a s -> p (a s)")
                pool.tensor_tensor(sq[:, :], xj, xj, ALU.mult).then_inc(sq_made, 1)
                pool.wait_ge(sq_made, count)
                pool.tensor_tensor(ssq[:, :], ssq[:, :], sq[:, :], ALU.add).then_inc(ssq_added, 1)
                pool.wait_ge(ssq_added, count)

            def ffn(n):
                f0, norm = n * FT, NORM_FFN[n]
                with pool.Fori(0, FT // 2) as i:
                    for s in range(2):
                        pool.wait_ge(hid_hi_made, 2 * i + (f0 + s + 1))
                        pool.tensor_tensor(hid_lo[:, bass.ds(2 * i + s, 1), :].rearrange("p a s -> p (a s)"),
                                           up[:, s, :], hid_hi[:, bass.ds(2 * i + s, 1), :].rearrange(
                                               "p a s -> p (a s)").bitcast(F32), ALU.subtract).then_inc(hid_lo_made, 1)
                clear_ssq(norm + 1)
                with pool.Fori(0, DT if n < 3 else DT - 1) as j:
                    square_tile(j, j + ((norm + 1) * DT + 1))

            def mask_diagonals(of, compare, count_sem):
                for b in range(TT):
                    at = KEY_OFF[b]
                    ins = pool.affine_select(out=of[:, at:at + P], in_=of[:, at:at + P], compare_op=compare, fill=0.0,
                                             base=0, pattern=[[1, P]], channel_multiplier=-1)
                ins.then_inc(count_sem, 1)

            step(pool.memset(ident[:, :], 0.0))
            pool.affine_select(out=ident[:, :], in_=ident[:, :], compare_op=ALU.not_equal, fill=1.0, base=0,
                               pattern=[[-1, P]], channel_multiplier=1).then_inc(consts_made, 1)
            load_params(pool, param_vectors[4:], 7 * DT, biases_loaded)
            pool.dma_start(conv_rows[:, :], conv_w[0].rearrange("k (c p) -> (k c) p", p=P)).then_inc(biases_loaded, 16)
            pool.memset(ones[:, :], 1.0)
            pool.memset(eps_col[:, :], EPS)
            step(pool.memset(neg_ones[:, :].bitcast(F32), -1.0))
            pool.affine_select(out=neg_tri[:, :], in_=neg_ones[:, :].bitcast(F32), compare_op=ALU.is_ge, fill=0.0, base=0,
                               pattern=[[-1, P]], channel_multiplier=1).then_inc(consts_made, 1)
            clear_ssq(0)
            for j in range(DT):
                square_tile(j, j + 1)
            ffn(0)

            pool.wait_ge(taps_lo_made, 1)
            for diags, k0 in ((diags_early, 0), (diags_late, EARLY)):
                for diag, part in zip(diags, (taps_hi, taps_lo)):
                    n = diag.shape[1]
                    pool.affine_select(out=diag[:, :, :], in_=part[:, k0:k0 + n].unsqueeze(2).to_broadcast([P, n, P]),
                                       compare_op=ALU.is_equal, fill=0.0, base=0, pattern=[[0, n], [-1, P]],
                                       channel_multiplier=1).then_inc(diags_made, 1)
            pool.wait_ge(turned_out, 2)
            for g in range(GB):
                ins = pool.affine_select(out=sp_rows[:, g, :], in_=sp_rows[:, g, :], compare_op=ALU.is_ge, fill=0.0, base=0,
                                         pattern=[[1, P]], channel_multiplier=-1)
            step(ins)
            step(pool.tensor_copy(sp_hi[:, :, :], sp_rows[:, :, :]))
            pool.tensor_tensor(sp_lo[:, :, :], sp_rows[:, :, :], sp_hi[:, :, :].bitcast(F32), ALU.subtract).then_inc(sp_ready, 1)
            for t in range(TT):
                pool.wait_ge(v_scaled, t + 1)
                if t == 0:
                    pool.wait_ge(mixer_params, 16 * 4)
                vt = v_cen[:, t].rearrange("p g c -> p (g c)")
                step(pool.tensor_tensor(vt, vt, lnv_g[:, :], ALU.mult))
                pool.tensor_tensor(vt, vt, lnv_b[:, :], ALU.add).then_inc(v_normed, 1)
            for g in range(GB):
                pool.wait_ge(b_hi_made, g + 1)
                pool.tensor_tensor(ab_lo[:, CT + g, :], u[:, g, :], ab_hi[:, CT + g, :].bitcast(F32),
                                   ALU.subtract).then_inc(b_lo_made, 1)
            pool.wait_ge(late_added, 1)
            pool.wait_ge(conv_made, 1)
            step(pool.tensor_tensor(sq[:, :], y[:, PE_TILE, :], y[:, 0, :], ALU.add))
            pool.wait_ge(conv_made, 2)
            step(pool.tensor_tensor(sq[:, :], sq[:, :], y[:, 1, :], ALU.add))
            pool.wait_ge(conv_made, 3)
            pool.tensor_tensor(sq[:, :], sq[:, :], y[:, 2, :], ALU.add).then_inc(ysum_made, 1)
            ysq = [v_cen[:, i].rearrange("p g c -> p (g c)") for i in range(CT)]
            pool.wait_ge(y_squared, 2)
            step(pool.tensor_tensor(sq[:, :], ysq[0], ysq[1], ALU.add))
            pool.wait_ge(y_squared, 3)
            step(pool.tensor_tensor(sq[:, :], sq[:, :], ysq[2], ALU.add))
            pool.wait_ge(y_squared, 4)
            pool.tensor_tensor(sq[:, :], sq[:, :], ysq[3], ALU.add).then_inc(ysq_sum_made, 1)
            clear_ssq(2)
            for j in range(DT):
                square_tile(j, 2 * DT + j + 1)
            ffn(1)
            ffn(2)

            for h in range(HEADS + 1):
                if h < HEADS:
                    pool.wait_ge(keep_made, h + 1)
                    mask_diagonals(keep, ALU.is_gt, keep_masked)
                if h >= 1:
                    pool.wait_ge(prob_made, h)
                    mask_diagonals(prob, ALU.is_gt, prob_masked)
            clear_ssq(5)
            for j in range(DT):
                square_tile(j, 5 * DT + j + 1)
            ffn(3)


_INS = ["x", "g_ffn1", "w_ffn1_gate", "w_ffn1_up", "w_ffn1_down", "g_mix", "w_in_ab", "conv_w", "conv_b", "ln_a_g",
        "ln_a_b", "ln_v_g", "ln_v_b", "sp_w", "sp_b", "w_out_ab", "w_qkv", "w_o", "g_ffn2", "w_ffn2_gate",
        "w_ffn2_up", "w_ffn2_down", "g_final"]
_OUT = ((1, S, D), "float32")


def kernel(**inputs):
    import numpy as _np
    import concourse.bacc as _bacc
    from concourse import mybir as _mybir
    from concourse.bass_utils import run_bass_kernel_spmd as _run

    nc = _bacc.Bacc("TRN2", target_bir_lowering=False, num_devices=1)
    arrays, args = {}, []
    for name in _INS:
        a = _np.ascontiguousarray(inputs[name])
        arrays[f"in_{name}_dram"] = a
        args.append(nc.dram_tensor(f"in_{name}_dram", a.shape, _mybir.dt.from_np(a.dtype), kind="ExternalInput").ap())
    shape, dtype = _OUT
    args.append(nc.dram_tensor("out_0_dram", shape, _mybir.dt.from_np(_np.dtype(dtype)), kind="ExternalOutput").ap())
    trunk_kernel(nc, *args)
    r = _run(nc, [arrays], core_ids=[0])
    return r.results[0]["out_0_dram"]
```
